# Optimizing a Trainium2 kernel written in Bass

```python
import jax, jax.numpy as jnp
from jax import lax
import numpy as np

D_MODEL = 1024
BATCH = 1
SEQ = 256
DEPTH = 1

A_HEADS = 8
A_HEAD_DIM = 64
A_WIDTH = A_HEADS * A_HEAD_DIM
MOBA_BLOCK = 256
MOBA_TOPK = 3
MOBA_QCHUNK = 128
M_HEADS = 4
M_HEAD_DIM = 128
M_WIDTH = M_HEADS * M_HEAD_DIM
M_CONV = 4
M_CHUNK = 64
N_EXPERTS = 32
TOP_K = 4
D_FF = 1024
SWIGLU_LIMIT = 7.0
SWIGLU_ALPHA = 1.702
MOE_BLOCK = 256
ROPE_THETA = 10000.0
EPS = 1e-6
NEG = -1e30
IN_SIZES = (A_WIDTH, A_WIDTH, A_WIDTH, M_WIDTH, M_WIDTH, M_WIDTH, M_WIDTH, M_HEADS, M_HEADS, D_MODEL, D_MODEL)
IN_SPLITS = tuple(sum(IN_SIZES[:i + 1]) for i in range(len(IN_SIZES) - 1))
IN_COLS = sum(IN_SIZES)

kernel_name = 'hybrid_moba_mlstm_moe_block'

def rmsnorm(x, w):
    xf = x.astype(jnp.float32)
    y = xf * lax.rsqrt(jnp.mean(xf * xf, axis=-1, keepdims=True) + EPS)
    return (y * w.astype(jnp.float32)).astype(x.dtype)

def rope(t):
    s, dh = t.shape[-2], t.shape[-1]
    inv = ROPE_THETA ** (-jnp.arange(0, dh, 2, dtype=jnp.float32) / dh)
    ang = jnp.arange(s, dtype=jnp.float32)[:, None] * inv[None, :]
    cos = jnp.concatenate([jnp.cos(ang), jnp.cos(ang)], axis=-1)
    sin = jnp.concatenate([jnp.sin(ang), jnp.sin(ang)], axis=-1)
    tf = t.astype(jnp.float32)
    rot = jnp.concatenate([-tf[..., dh // 2:], tf[..., :dh // 2]], axis=-1)
    return (tf * cos + rot * sin).astype(t.dtype)

def causal_dwconv(u, w, b):
    width, ch = w.shape
    y = lax.conv_general_dilated(u, w[:, None, :].astype(u.dtype), window_strides=(1,),
                                 padding=[(width - 1, 0)],
                                 dimension_numbers=('NWC', 'WIO', 'NWC'),
                                 feature_group_count=ch)
    return y + b.astype(u.dtype)

def moba_attention(q, k, v):
    bsz, nh, s, dh = q.shape
    nb = -(-s // MOBA_BLOCK)
    pad = nb * MOBA_BLOCK - s
    kb = jnp.pad(k, ((0, 0), (0, 0), (0, pad), (0, 0))).reshape(bsz, nh, nb, MOBA_BLOCK, dh)
    vb = jnp.pad(v, ((0, 0), (0, 0), (0, pad), (0, 0))).reshape(bsz, nh, nb, MOBA_BLOCK, dh)
    k_mean = jnp.mean(kb.astype(jnp.float32), axis=3)
    q_blk = jnp.arange(s) // MOBA_BLOCK
    past = jnp.arange(nb)[None, :] < q_blk[:, None]
    gate = jnp.einsum('bhsd,bhnd->bhsn', q.astype(jnp.float32), k_mean)
    gate = jnp.where(past, gate, -jnp.inf)
    ksel = min(MOBA_TOPK, nb)
    _, sel = lax.top_k(gate, ksel)
    valid = jnp.arange(ksel)[None, :] < q_blk[:, None]
    nq = s // MOBA_QCHUNK
    qc = q.reshape(bsz, nh, nq, MOBA_QCHUNK, dh).transpose(0, 2, 1, 3, 4)
    selc = sel.reshape(bsz, nh, nq, MOBA_QCHUNK, ksel).transpose(0, 2, 1, 3, 4)
    validc = valid.reshape(nq, MOBA_QCHUNK, ksel)
    scale = dh ** -0.5
    gather_blocks = jax.vmap(lambda blocks, idx: blocks[idx])

    def per_batch(args):
        q_b, sel_b, kb_b, vb_b = args

        def per_chunk(cargs):
            c, q_c, sel_c, valid_c = cargs
            j = (c * MOBA_QCHUNK) // MOBA_BLOCK
            k_sel = gather_blocks(kb_b, sel_c)
            v_sel = gather_blocks(vb_b, sel_c)
            k_own = lax.dynamic_index_in_dim(kb_b, j, axis=1, keepdims=False)
            v_own = lax.dynamic_index_in_dim(vb_b, j, axis=1, keepdims=False)
            q_pos = c * MOBA_QCHUNK + jnp.arange(MOBA_QCHUNK)
            k_pos = j * MOBA_BLOCK + jnp.arange(MOBA_BLOCK)
            s_own = jnp.einsum('hqd,hkd->hqk', q_c, k_own).astype(jnp.float32) * scale
            s_own = jnp.where(k_pos[None, :] <= q_pos[:, None], s_own, NEG)
            s_sel = jnp.einsum('hqd,hqnkd->hqnk', q_c, k_sel).astype(jnp.float32) * scale
            s_sel = jnp.where(valid_c[None, :, :, None], s_sel, NEG)
            scores = jnp.concatenate([s_own, s_sel.reshape(nh, MOBA_QCHUNK, ksel * MOBA_BLOCK)], axis=-1)
            p = jax.nn.softmax(scores, axis=-1).astype(q_c.dtype)
            p_own = p[..., :MOBA_BLOCK]
            p_sel = p[..., MOBA_BLOCK:].reshape(nh, MOBA_QCHUNK, ksel, MOBA_BLOCK)
            return (jnp.einsum('hqk,hkd->hqd', p_own, v_own)
                    + jnp.einsum('hqnk,hqnkd->hqd', p_sel, v_sel))

        return lax.map(per_chunk, (jnp.arange(nq), q_b, sel_b, validc))

    out = lax.map(per_batch, (qc, selc, kb, vb))
    return out.transpose(0, 2, 1, 3, 4).reshape(bsz, nh, s, dh)

def mlstm_chunkwise(q, k, v, i_pre, f_pre):
    bsz, nh, s, dh = q.shape
    nc = s // M_CHUNK
    k = k * (dh ** -0.5)
    log_f = jax.nn.log_sigmoid(f_pre)

    def chunks(t):
        return jnp.moveaxis(t.reshape((bsz, nh, nc, M_CHUNK) + t.shape[3:]), 2, 0)

    causal = jnp.tril(jnp.ones((M_CHUNK, M_CHUNK), dtype=bool))

    def step(carry, xs):
        c_st, n_st, m_st = carry
        q_c, k_c, v_c, i_c, f_c = xs
        b = jnp.cumsum(f_c, axis=-1)
        d = b[..., :, None] - b[..., None, :] + i_c[..., None, :]
        d = jnp.where(causal, d, -jnp.inf)
        g = b + m_st[..., None]
        m_t = jnp.maximum(g, jnp.max(d, axis=-1))
        w_intra = jnp.exp(d - m_t[..., None])
        w_inter = jnp.exp(g - m_t)
        qk = jnp.einsum('bhtd,bhsd->bhts', q_c, k_c) * w_intra
        num = (w_inter[..., None] * jnp.einsum('bhvd,bhtd->bhtv', c_st, q_c)
               + jnp.einsum('bhts,bhsv->bhtv', qk, v_c))
        den = w_inter * jnp.einsum('bhd,bhtd->bht', n_st, q_c) + jnp.sum(qk, axis=-1)
        h = num / jnp.maximum(jnp.abs(den), jnp.exp(-m_t))[..., None]
        b_last = b[..., -1]
        log_w = b_last[..., None] - b + i_c
        m_new = jnp.maximum(b_last + m_st, jnp.max(log_w, axis=-1))
        w_k = jnp.exp(log_w - m_new[..., None])
        decay = jnp.exp(b_last + m_st - m_new)
        c_new = decay[..., None, None] * c_st + jnp.einsum('bhs,bhsv,bhsd->bhvd', w_k, v_c, k_c)
        n_new = decay[..., None] * n_st + jnp.einsum('bhs,bhsd->bhd', w_k, k_c)
        return (c_new, n_new, m_new), h

    init = (jnp.zeros((bsz, nh, dh, dh), jnp.float32),
            jnp.zeros((bsz, nh, dh), jnp.float32),
            jnp.zeros((bsz, nh), jnp.float32))
    _, hs = lax.scan(step, init, (chunks(q), chunks(k), chunks(v), chunks(i_pre), chunks(log_f)))
    return jnp.moveaxis(hs, 0, 2).reshape(bsz, nh, s, dh)

def token_mixer(xn, w_in, m_conv_w, m_conv_b, m_gate_bias, m_head_norm_w, w_branch, w_out):
    bsz, s, _ = xn.shape
    proj = xn @ w_in
    a_q, a_k, a_v, m_q, m_k, m_v, m_o, m_i, m_f, g_a, g_m = jnp.split(proj, IN_SPLITS, axis=-1)

    def heads(t, nh, dh):
        return t.reshape(bsz, s, nh, dh).transpose(0, 2, 1, 3)

    y_a = moba_attention(rope(heads(a_q, A_HEADS, A_HEAD_DIM)),
                         rope(heads(a_k, A_HEADS, A_HEAD_DIM)),
                         heads(a_v, A_HEADS, A_HEAD_DIM))
    y_a = y_a.transpose(0, 2, 1, 3).reshape(bsz, s, A_WIDTH)

    qk = jax.nn.silu(causal_dwconv(jnp.concatenate([m_q, m_k], axis=-1), m_conv_w, m_conv_b))
    m_q, m_k = qk[..., :M_WIDTH], qk[..., M_WIDTH:]
    gates = (jnp.concatenate([m_i, m_f], axis=-1) + m_gate_bias).astype(jnp.float32).transpose(0, 2, 1)
    h_m = mlstm_chunkwise(heads(m_q, M_HEADS, M_HEAD_DIM).astype(jnp.float32),
                          heads(m_k, M_HEADS, M_HEAD_DIM).astype(jnp.float32),
                          heads(m_v, M_HEADS, M_HEAD_DIM).astype(jnp.float32),
                          gates[:, :M_HEADS], gates[:, M_HEADS:])
    h_m = h_m * lax.rsqrt(jnp.mean(h_m * h_m, axis=-1, keepdims=True) + EPS)
    h_m = h_m.transpose(0, 2, 1, 3).reshape(bsz, s, M_WIDTH)
    y_m = (h_m * m_head_norm_w.astype(jnp.float32)).astype(xn.dtype) * jax.nn.sigmoid(m_o)

    p_a = y_a @ w_branch[:A_WIDTH]
    p_m = y_m @ w_branch[A_WIDTH:]
    merged = jax.nn.sigmoid(g_a) * p_a + jax.nn.sigmoid(g_m) * p_m
    return merged @ w_out

def moe_ffn(xn, w_router, b_router, w_mlp1, b_mlp1, w_mlp2, b_mlp2):
    bsz, s, d = xn.shape
    n_tok = bsz * s
    xt = xn.reshape(n_tok, d)
    logits = (xt @ w_router + b_router).astype(jnp.float32)
    top_val, top_idx = lax.top_k(logits, TOP_K)
    gate = jax.nn.softmax(top_val, axis=-1)
    n_asg = n_tok * TOP_K
    e_flat = top_idx.reshape(n_asg).astype(jnp.int32)
    tok_flat = jnp.arange(n_asg, dtype=jnp.int32) // TOP_K
    counts = jnp.bincount(e_flat, length=N_EXPERTS).astype(jnp.int32)
    padded = (counts + MOE_BLOCK - 1) // MOE_BLOCK * MOE_BLOCK
    pad_end = jnp.cumsum(padded)
    pad_start = pad_end - padded
    start = jnp.cumsum(counts) - counts
    order = jnp.argsort(e_flat)
    e_sorted = e_flat[order]
    dest_sorted = (pad_start[e_sorted] + jnp.arange(n_asg, dtype=jnp.int32) - start[e_sorted]).astype(jnp.int32)
    dest = jnp.zeros((n_asg,), jnp.int32).at[order].set(dest_sorted)
    n_blk = -(-n_asg // MOE_BLOCK) + N_EXPERTS
    n_rows = n_blk * MOE_BLOCK
    row_tok = jnp.full((n_rows,), n_tok, jnp.int32).at[dest].set(tok_flat)
    x_rows = jnp.concatenate([xt, jnp.zeros((1, d), xt.dtype)], axis=0)[row_tok].reshape(n_blk, MOE_BLOCK, d)
    blk_expert = jnp.minimum(jnp.searchsorted(pad_end, jnp.arange(n_blk, dtype=jnp.int32) * MOE_BLOCK,
                                              side='right'), N_EXPERTS - 1)

    def expert_block(args):
        xb, e = args
        hdn = xb @ w_mlp1[e] + b_mlp1[e]
        glu = jnp.minimum(hdn[:, :D_FF], SWIGLU_LIMIT)
        lin = jnp.clip(hdn[:, D_FF:], -SWIGLU_LIMIT, SWIGLU_LIMIT)
        act = glu * jax.nn.sigmoid(SWIGLU_ALPHA * glu) * (lin + 1.0)
        return act @ w_mlp2[e] + b_mlp2[e]

    y_rows = lax.map(expert_block, (x_rows, blk_expert)).reshape(n_rows, d)
    y = y_rows[dest].reshape(n_tok, TOP_K, d)
    return jnp.einsum('tk,tkd->td', gate.astype(y.dtype), y).reshape(bsz, s, d)

def setup_inputs(seed: int = 0) -> dict:
    key = jax.random.key(seed)
    ks = jax.random.split(key, 18)
    f32 = jnp.float32
    L = DEPTH

    def nrm(k, shape, scale):
        return jax.random.normal(k, shape, f32) * scale

    return {
        'x': nrm(ks[0], (BATCH, SEQ, D_MODEL), 1.0),
        'norm_mix_w': 1.0 + nrm(ks[1], (L, D_MODEL), 0.02),
        'w_in': nrm(ks[2], (L, D_MODEL, IN_COLS), D_MODEL ** -0.5),
        'm_conv_w': nrm(ks[3], (L, M_CONV, 2 * M_WIDTH), M_CONV ** -0.5),
        'm_conv_b': nrm(ks[4], (L, 2 * M_WIDTH), 0.01),
        'm_gate_bias': jnp.concatenate([nrm(ks[5], (L, M_HEADS), 0.1),
                                        3.0 + 3.0 * jax.random.uniform(ks[6], (L, M_HEADS), f32)], axis=-1),
        'm_head_norm_w': 1.0 + nrm(ks[7], (L, M_WIDTH), 0.02),
        'w_branch': nrm(ks[8], (L, A_WIDTH + M_WIDTH, D_MODEL), A_WIDTH ** -0.5),
        'w_out': nrm(ks[9], (L, D_MODEL, D_MODEL), D_MODEL ** -0.5),
        'norm_ffn_w': 1.0 + nrm(ks[10], (L, D_MODEL), 0.02),
        'w_router': nrm(ks[11], (L, D_MODEL, N_EXPERTS), D_MODEL ** -0.5),
        'b_router': nrm(ks[12], (L, N_EXPERTS), 0.01),
        'w_mlp1': nrm(ks[13], (L, N_EXPERTS, D_MODEL, 2 * D_FF), D_MODEL ** -0.5),
        'b_mlp1': nrm(ks[14], (L, N_EXPERTS, 2 * D_FF), 0.01),
        'w_mlp2': nrm(ks[15], (L, N_EXPERTS, D_FF, D_MODEL), D_FF ** -0.5),
        'b_mlp2': nrm(ks[16], (L, N_EXPERTS, D_MODEL), 0.01),
        'norm_final_w': 1.0 + nrm(ks[17], (D_MODEL,), 0.02),
    }

def reference(x, norm_mix_w, w_in, m_conv_w, m_conv_b, m_gate_bias, m_head_norm_w, w_branch, w_out,
              norm_ffn_w, w_router, b_router, w_mlp1, b_mlp1, w_mlp2, b_mlp2, norm_final_w):
    h = x
    for l in range(DEPTH):
        h = h + token_mixer(rmsnorm(h, norm_mix_w[l]), w_in[l], m_conv_w[l], m_conv_b[l],
                            m_gate_bias[l], m_head_norm_w[l], w_branch[l], w_out[l])
        h = h + moe_ffn(rmsnorm(h, norm_ffn_w[l]), w_router[l], b_router[l],
                        w_mlp1[l], b_mlp1[l], w_mlp2[l], b_mlp2[l])
    return rmsnorm(h, norm_final_w)


_drawn_inputs = setup_inputs


def setup_inputs(seed=0):
    import zlib

    import numpy as np

    out = dict(_drawn_inputs(seed))
    spreads = {}
    factors = {'m_conv_b': 3.531,
     'm_head_norm_w': 2.82,
     'b_mlp1': 8.0,
     'b_mlp2': 8.0,
     'norm_final_w': 2.869}
    for name, (base, spread) in spreads.items():
        noise = np.random.default_rng([zlib.crc32(name.encode()), seed]).standard_normal(out[name].shape)
        drawn = base * np.exp(spread * noise) if base else spread * noise
        out[name] = __import__('jax').numpy.asarray(drawn.astype(out[name].dtype))
    for name, factor in factors.items():
        out[name] = (out[name] * factor).astype(out[name].dtype)
    return out
```

```python
from contextlib import ExitStack

import numpy as np

import concourse.bass as bass
from concourse import mybir

F32 = mybir.dt.float32
I32 = mybir.dt.int32
ALU = mybir.AluOpType
ACT = mybir.ActivationFunctionType
AX = mybir.AxisListType.X

P = 128
S = 256
TT = S // P
D = 1024
KB = D // P
AH, ADH = 8, 64
MH, MDH = 4, 128
AW = AH * ADH
MW = MH * MDH
CONV = 4
E = 32
TOPK = 4
FF = 1024
C = 64
NR = S // C
LIMIT = 7.0
ALPHA = 1.702
EPS = 1e-6
NEG = -1e30
N = 512

O_MI = 3 * AW + 4 * MW
O_G = O_MI + 2 * MH
SLICES = ["mq", "mk", "mv", "aq", "ak", "av", "mo", "ga0", "ga1", "gm0", "gm1"]
COL = {"aq": 0, "ak": AW, "av": 2 * AW, "mq": 3 * AW, "mk": 3 * AW + MW, "mv": 3 * AW + 2 * MW,
       "mo": 3 * AW + 3 * MW, "ga0": O_G, "ga1": O_G + N, "gm0": O_G + 2 * N, "gm1": O_G + 3 * N}

SLOT = 2 * FF
RING = 12
Q_BRANCH = 2 * len(SLICES)
Q_OUT = Q_BRANCH + 4
Q_MOE = Q_OUT + 4
PER_EXPERT = 12
assert RING == PER_EXPERT

K_ID, K_COS, K_SIN = 0, 128, 256
K_MASK, K_MASKT, K_LOWER, K_ONES = 320, 448, 576, 704
K_IOTA, K_SEL, K_END = 832, 1088, 1600


def constants():
    c = np.zeros((P, K_END), np.float32)
    p = np.arange(P)
    c[:, K_ID:K_ID + P] = np.eye(P)
    inv = np.float32(10000.0) ** (-np.arange(0, ADH, 2, dtype=np.float32) / np.float32(ADH))
    for t in range(TT):
        ang = (p + P * t).astype(np.float32)[:, None] * inv[None, :].astype(np.float32)
        c[:, K_COS + ADH * t:K_COS + ADH * (t + 1)] = np.tile(np.cos(ang), 2)
        c[:, K_SIN + 32 * t:K_SIN + 32 * (t + 1)] = np.sin(ang)
    c[:, K_MASK:K_MASK + P] = np.where(p[None, :] <= p[:, None], 0.0, NEG)
    c[:, K_MASKT:K_MASKT + P] = np.where(p[:, None] <= p[None, :], 0.0, NEG)
    c[:, K_LOWER:K_LOWER + P] = p[:, None] < p[None, :]
    c[:, K_ONES:K_ONES + P] = 1.0
    c[:, K_IOTA:K_IOTA + S] = np.arange(S)
    for h in range(MH):
        c[h, K_SEL + P * h:K_SEL + P * (h + 1)] = 1.0
    return c


def slot_of(q):
    return q % RING


def build(nc, x, norm_mix_w, w_in, m_conv_w, m_conv_b, m_gate_bias, m_head_norm_w, w_branch, w_out,
          norm_ffn_w, w_router, b_router, w_mlp1, b_mlp1, w_mlp2, b_mlp2, norm_final_w, table, out):
    with ExitStack() as ctx:
        def sb(name, shape, dt=F32):
            return ctx.enter_context(nc.sbuf_tensor(name, shape, dt))

        def sem(name):
            return ctx.enter_context(nc.semaphore(name))

        ring = sb("ring", [P, RING, SLOT])
        cst = sb("cst", [P, K_END])
        xs = sb("xs", [P, TT, D])
        xn = sb("xn", [P, TT, D])
        xnT = sb("xnT", [P, KB, S])
        rows = sb("rows", [60, P])
        cols = sb("cols", [P, 60])
        gbias = sb("gbias", [MH, 2])
        wgate = sb("wgate", [P, KB, 2 * MH])
        wr = sb("wr", [P, KB, E])
        brt = sb("brt", [P, E])
        st = sb("st", [P, 16])
        pre = sb("pre", [P, 2 * MH, S + 3])
        mqk = sb("mqk", [P, 2 * MH, S])
        gr = sb("gr", [MH, 8, S])
        gcol = sb("gcol", [P, 2, TT, MH])
        wm = sb("wm", [P, MH, 3, P])
        vaug = sb("vaug", [P, TT, MH, MDH + 1])
        av = sb("av", [P, TT, AW])
        smo = sb("smo", [P, TT, MW])
        sga = sb("sga", [P, TT, D])
        sgm = sb("sgm", [P, TT, D])
        hm = sb("hm", [P, TT, MH, MDH])
        dn = sb("dn", [P, MH, 3, TT])
        hs = sb("hs", [P, 4, TT, MH])
        qk = sb("qk", [P, 2, TT, AW])
        rt = sb("rt", [P, 2, AW])
        am = sb("am", [P, AH, 4, TT])
        qkT = xn[:, :, :].rearrange("p a (b s) -> p (a b) s", s=S)
        sg = sga[:, :, :].rearrange("p t (a s) -> p (t a) s", s=S)
        dg = smo[:, :, :].rearrange("p t (a s) -> p (t a) s", s=P)
        ps = wm[:, :, :, :].rearrange("p h b s -> p h (b s)")
        pt = mqk[:, :, :].rearrange("p a s -> p (a s)")[:, 0:4 * 3 * P].rearrange("p (a s) -> p a s", a=4)
        wfin = av[:, :, :].rearrange("p t n -> p (t n)")
        b2 = rt[0:E, :, :].rearrange("p a n -> p (a n)")
        b1row = pre[0:1, :, :].rearrange("p a s -> p (a s)")[:, 0:2 * FF]
        yaT = pre[:, 0:4, 0:S]
        ymT = pre[:, 4:8, 0:S]
        mg = qk[:, :, :, :].rearrange("p a t n -> p (a t n)").rearrange("p (t n) -> p t n", t=TT)
        mgT = xnT
        lg = sb("lg", [P, TT, 6, E])
        mx8 = sb("mx8", [P, TT, 16])
        pos = sb("pos", [P, TT, E])
        gate = sb("gate", [P, TT, E])
        gateT = sb("gateT", [E, S])
        cnt = sb("cnt", [1, 5, E])
        first_item = sb("first_item", [1, E + 1], I32)
        moe = sga[:, :, :].rearrange("p t n -> p (t n)")
        moe2 = sgm[:, :, :].rearrange("p t n -> p (t n)")
        xgT = moe[:, 0:N].rearrange("p (k s) -> p k s", k=KB)
        glu = moe[:, N:2 * N]
        lin = moe[:, 2 * N:3 * N]
        actv = moe[:, 3 * N:4 * N]
        sig = moe2[:, 0:N]
        actT = moe2[:, N:2 * N].rearrange("p (j c) -> p j c", j=4)
        yw = moe2[:, 2 * N:3 * N]
        oneh = hm[:, :, 0, 0:C]
        gated = hm[:, :, 1, :]
        gatedT = smo[:, 0, 0:S]

        B = [ctx.enter_context(nc.psum_tensor(f"bank{i}", [P, N], F32)) for i in range(8)]

        s_x, s_cst, s_small, s_small2 = sem("x_in"), sem("constants_in"), sem("small_in"), sem("late_small_in")
        landed = [sem(f"slot{i}_landed") for i in range(RING)]
        slot_free = sem("slot_free")
        sumsq, meansq, root, rstd = sem("sumsq"), sem("meansq"), sem("root"), sem("rstd")
        xn_ready = sem("xn_ready")
        rows_turned, cols_ready = sem("rows_turned"), sem("cols_ready")
        xT_turned, xT_even, xT_odd = sem("xT_turned"), sem("xT_even"), sem("xT_odd")
        gates_done, grow, gexp = sem("gates_done"), sem("gate_rows"), sem("gate_exp")
        pads = sem("pads")
        projected = sem("projected")
        taken = {n: sem(f"taken_{n}") for n in SLICES}
        conv, silu_sig, silu = sem("conv"), sem("silu_sigmoid"), sem("silu")
        mbc, gcols, gcols_act, diag, wexp = sem("m_broadcast"), sem("gate_cols"), sem("gate_cols_exp"), sem("diag"), sem("w_exp")
        mqk_done, wqk, mpv, mden, mh = sem("m_qk"), sem("w_times_qk"), sem("m_pv"), sem("m_den"), sem("m_h")
        hnorm, hroot, ym = sem("head_norm"), sem("head_root"), sem("y_m")
        rope = sem("rope")
        qkT_turned, qkT_ready = sem("qkT_turned"), sem("qkT_ready")
        scored, masked, smax, nsmax = sem("scored"), sem("masked"), sem("score_max"), sem("neg_max")
        probs, psum_r, pnorm = sem("probs"), sem("prob_recip"), sem("prob_normed")
        p_turned, pT_ready, apv, yaT_ready = sem("p_turned"), sem("pT_ready"), sem("a_pv"), sem("yaT_ready")
        ym_turned, ymT_ready = sem("ym_turned"), sem("ymT_ready")
        branched, gated_br, merged = sem("branched"), sem("gated_branch"), sem("merged")
        mg_turned, mgT_ready, mixed, resid = sem("merged_turned"), sem("mergedT_ready"), sem("mixed"), sem("resid")
        logits_done, router = sem("logits_done"), sem("router")
        rexp = sem("router_exp")
        ranked, pos_ready, counted, tabled = sem("ranked"), sem("pos_ready"), sem("counted"), sem("tabled")
        gate_turned, gateT_ready = sem("gate_turned"), sem("gateT_ready")
        b1_in, b1_free = sem("b1_in"), sem("b1_free")
        onehot, gath, xg_ready = sem("onehot"), sem("gathered"), sem("xg_ready")
        gt_turned, gT_ready = sem("gated_turned"), sem("gatedT_ready")
        up, gl_ready, sig_ready, act_ready = sem("up"), sem("glu_lin"), sem("sigmoid_ready"), sem("act_ready")
        act_turned, actT_ready, down, yw_ready, scat = (sem("act_turned"), sem("actT_ready"), sem("down"),
                                                       sem("y_ready"), sem("scattered"))
        rope_step, diag_half, router_step = sem("rope_step"), sem("diag_half"), sem("router_step")
        count_step, pos_step, glin = sem("count_step"), sem("pos_step"), sem("glu_times_lin")
        out_sem = sem("out_stored")

        ident = cst[:, K_ID:K_ID + P]
        ones = cst[:, K_ONES:K_ONES + P]

        def wcol(i):
            return cols[:, i:i + 1]

        NORM_MIX, NORM_FFN, CONV_W, CONV_B, HEAD_W = 0, 8, 16, 48, 56

        def slab(q, n):
            return ring[:, slot_of(q):slot_of(q) + n, :]

        def loads_before(q):
            return sum(1 for p in range(slot_of(q), q, RING) if p >= Q_BRANCH or p % 2 == 0)

        def wslice(n):
            return slab(2 * n, 2).rearrange("p a (k n) -> p (a k) n", n=N)

        def wblock(q0, b):
            return ring[:, slot_of(q0 + b // 2), (b % 2) * D:(b % 2 + 1) * D]

        w_in2, w_branch2, w_out2 = w_in[0], w_branch[0], w_out[0]
        block = ctx.enter_context(nc.Block())

        @block.sync
        def _(sp):
            sp.dma_start(xs[:, :, :], x[0].rearrange("(t p) d -> p t d", p=P)).then_inc(s_x, 16)
            for n, name in enumerate(SLICES):
                if 2 * n >= RING:
                    sp.wait_ge(slot_free, 2 * n + 2 - RING)
                src = w_in2[:, COL[name]:COL[name] + N].rearrange("(k p) n -> p k n", p=P)
                sp.dma_start(wslice(n), src).then_inc(landed[slot_of(2 * n)], 16)
            for q0, w in ((Q_BRANCH, w_branch2), (Q_OUT, w_out2)):
                for j in range(4):
                    sp.wait_ge(slot_free, q0 + j + 1 - RING)
                    dst = ring[:, slot_of(q0 + j), :].rearrange("p (b n) -> p b n", b=2)
                    src = w[2 * P * j:2 * P * (j + 1), :].rearrange("(b p) n -> p b n", p=P)
                    sp.dma_start(dst, src).then_inc(landed[slot_of(q0 + j)], 16)

            def expert(e, freed):
                for k in range(KB):
                    sp.wait_ge(slot_free, freed(k))
                    sp.dma_start(ring[:, slot_of(Q_MOE + k), :], w_mlp1[0, e, k * P:(k + 1) * P, :])\
                      .then_inc(landed[slot_of(Q_MOE + k)], 16)
                for j in range(4):
                    k = KB + j
                    sp.wait_ge(slot_free, freed(k))
                    dst = ring[:, slot_of(Q_MOE + k), :].rearrange("p (h n) -> p h n", h=2)
                    src = w_mlp2[0, e].rearrange("(h j p) n -> j p h n", h=2, j=4)[j]
                    sp.dma_start(dst, src).then_inc(landed[slot_of(Q_MOE + k)], 16)

            expert(0, lambda k: Q_MOE + k + 1 - RING)
            sp.wait_ge(tabled, 1)
            with sp.Fori(1, E) as e:
                before = sp.value_load(first_item[0:1, bass.ds(e, 1)], min_val=1, max_val=E + 16)
                expert(e, lambda k: before * PER_EXPERT + (Q_MOE - PER_EXPERT + k + 1))
            sp.wait_ge(out_sem, 16 * TT)

        @block.gpsimd
        def _(pool):
            pool.memset(pre[:, :, 0:3], 0.0).then_inc(pads, 1)
            pool.memset(vaug[:, :, :, MDH:MDH + 1], 1.0).then_inc(pads, 1)
            pool.wait_ge(branched, 2 * TT)
            pool.dma_start(b1row, b_mlp1[0, 0:1, :]).then_inc(b1_in, 16)
            pool.wait_ge(tabled, 1)
            with pool.Fori(1, E) as e:
                before = pool.value_load(first_item[0:1, bass.ds(e, 1)], min_val=1, max_val=E + 16)
                pool.wait_ge(b1_free, before)
                pool.dma_start(b1row, b_mlp1[0, bass.ds(e, 1), :]).then_inc(b1_in, 16)

        @block.scalar
        def _(act):
            act.dma_start(rows[0:8, :], norm_mix_w[0].rearrange("(a b) -> a b", b=P)).then_inc(s_small, 16)
            act.dma_start(rows[8:16, :], norm_ffn_w[0].rearrange("(a b) -> a b", b=P)).then_inc(s_small, 16)
            act.dma_start(rows[16:48, :], m_conv_w[0].rearrange("j (a b) -> (j a) b", b=P)).then_inc(s_small, 16)
            act.dma_start(rows[48:56, :], m_conv_b[0].rearrange("(a b) -> a b", b=P)).then_inc(s_small, 16)
            act.dma_start(rows[56:60, :], m_head_norm_w[0].rearrange("(a b) -> a b", b=P)).then_inc(s_small, 16)
            act.dma_start(cst[:, :], table[:, :]).then_inc(s_cst, 16)
            for g in range(2):
                act.dma_start(gbias[:, g:g + 1], m_gate_bias[0, g * MH:(g + 1) * MH].rearrange("(h a) -> h a", a=1))\
                   .then_inc(s_small, 16)
            act.dma_start(wgate[:, :, :], w_in2[:, O_MI:O_MI + 2 * MH].rearrange("(k p) n -> p k n", p=P))\
               .then_inc(s_small, 16)
            act.dma_start(wr[:, :, :], w_router[0].rearrange("(k p) n -> p k n", p=P)).then_inc(s_small2, 16)
            act.dma_start(brt[:, :], b_router[0:1, :].broadcast_to([P, E])).then_inc(s_small2, 16)

            def norm_root(i):
                act.wait_ge(meansq, i + 1)
                nc.scalar.activation(st[:, 4:6], st[:, 2:4], ACT.Sqrt).then_inc(root, 1)

            def take(name, outs, func=ACT.Copy):
                n = SLICES.index(name)
                act.wait_ge(projected, n + 1)
                for j in range(2):
                    src = B[2 * (n % 2) + j][:, :]
                    dst = outs(j)
                    if len(dst.shape) == 3:
                        src = src.rearrange("p (a b) -> p a b", a=dst.shape[1])
                    nc.scalar.activation(dst, src, func).then_inc(taken[name], 1)

            norm_root(0)
            act.wait_ge(cols_ready, 1)
            for k in (2, 3, 6, 7):
                act.wait_ge(xT_turned, k // 2 + 1)
                nc.scalar.activation(xnT[:, k, :], B[4 + k // 2][:, (k % 2) * S:(k % 2 + 1) * S], ACT.Copy,
                                     scale=wcol(NORM_MIX + k)).then_inc(xT_odd, 1)
            act.wait_ge(grow, 3)
            nc.scalar.activation(gr[:, 3, :], gr[:, 2, :], ACT.Exp, scale=-1.0).then_inc(gexp, 1)
            act.wait_ge(grow, 4)
            nc.scalar.activation(gr[:, 3, :], gr[:, 3, :], ACT.Ln).then_inc(gexp, 1)
            act.wait_ge(pads, 2)
            take("mq", lambda j: pre[:, 2 * j:2 * j + 2, 3:3 + S])
            take("mk", lambda j: pre[:, MH + 2 * j:MH + 2 * j + 2, 3:3 + S])
            for g in range(2):
                act.wait_ge(conv, MH * CONV * (g + 1))
                nc.scalar.activation(sg[:, MH * g:MH * (g + 1), :], mqk[:, MH * g:MH * (g + 1), :], ACT.Sigmoid)\
                  .then_inc(silu_sig, 1)
            take("mv", lambda j: vaug[:, j, :, 0:MDH])
            act.wait_ge(gcols, 1)
            nc.scalar.activation(gcol[:, 1, :, :], B[6][:, 8:16].rearrange("p (t h) -> p t h", t=TT), ACT.Exp)\
              .then_inc(gcols_act, 1)
            act.wait_ge(diag, 1)
            for h in range(MH):
                off = B[4 + h // 2][:, (h % 2) * S + P:(h % 2) * S + 2 * P]
                for b, (src, s0) in enumerate(((dg[:, 2 * h, :], 0), (off, 0), (dg[:, 2 * h + 1, :], 1))):
                    nc.scalar.activation(wm[:, h, b, :], src, ACT.Exp, bias=gcol[:, 0, s0, h:h + 1]).then_inc(wexp, 1)
            take("av", lambda j: av[:, j, :])
            take("mo", lambda j: smo[:, j, :], ACT.Sigmoid)
            act.wait_ge(hnorm, 3)
            nc.scalar.activation(hs[:, 2, :, :], hs[:, 1, :, :], ACT.Sqrt).then_inc(hroot, 1)

            def softmax(h):
                act.wait_ge(nsmax, h + 1)
                if h >= 4:
                    act.wait_ge(p_turned, h - 3)
                for t in range(TT):
                    lo, hi = (0, P) if t == 0 else (P, 3 * P)
                    nc.scalar.activation(ps[:, h % 4, lo:hi], B[4 + h % 4][:, lo:hi], ACT.Exp,
                                         bias=am[:, h, 1, t:t + 1], scale=ADH ** -0.5,
                                         accum_out=am[:, h, 2, t:t + 1]).then_inc(probs, 1)

            for h in range(4):
                softmax(h)
            take("ga0", lambda j: sga[:, j, 0:N], ACT.Sigmoid)
            take("ga1", lambda j: sga[:, j, N:D], ACT.Sigmoid)
            act.wait_ge(rope, 2 * TT)
            act.dma_start(b2, b_mlp2[0]).then_inc(s_small2, 16)
            for h in range(4, AH):
                softmax(h)
            take("gm0", lambda j: sgm[:, j, 0:N], ACT.Sigmoid)
            take("gm1", lambda j: sgm[:, j, N:D], ACT.Sigmoid)
            act.wait_ge(apv, 4)
            act.dma_start(wfin, norm_final_w.rearrange("(a d) -> a d", a=1).broadcast_to([P, D]))\
               .then_inc(s_small2, 16)
            for t in range(TT):
                for b in range(2):
                    act.wait_ge(mg_turned, 2 * t + b + 1)
                    src = B[4 + 2 * t + b][:, :].rearrange("p (k s) -> p k s", k=4)
                    nc.scalar.activation(mgT[:, 4 * b:4 * b + 4, t * P:(t + 1) * P], src, ACT.Copy)\
                      .then_inc(mgT_ready, 1)
            norm_root(1)
            for k in (2, 3, 6, 7):
                act.wait_ge(xT_turned, 4 + k // 2 + 1)
                nc.scalar.activation(xnT[:, k, :], B[4 + k // 2][:, (k % 2) * S:(k % 2 + 1) * S], ACT.Copy,
                                     scale=wcol(NORM_FFN + k)).then_inc(xT_odd, 1)
            act.wait_ge(router, 4)
            for t in range(TT):
                nc.scalar.activation(lg[:, t, 2, :], lg[:, t, 0, :], ACT.Exp, bias=mx8[:, t, 8:9]).then_inc(rexp, 1)

            for s in (sig_ready, yw_ready):
                act.sem_inc(s, 1)
            act.wait_ge(tabled, 1)
            with act.Fori(0, E) as e:
                i0 = act.value_load(first_item[0:1, bass.ds(e, 1)], min_val=0, max_val=E + 16)
                i1 = act.value_load(first_item[0:1, bass.ds(e + 1, 1)], min_val=1, max_val=E + 16)
                with act.Fori(i0, i1) as i:
                    act.wait_ge(gt_turned, i + 2)
                    act.wait_ge(scat, i + 1)
                    nc.scalar.activation(gatedT, B[7][:, 0:S], ACT.Copy).then_inc(gT_ready, 1)
                    act.wait_ge(gl_ready, 2 * i + 3)
                    nc.scalar.activation(sig, glu, ACT.Sigmoid, scale=ALPHA).then_inc(sig_ready, 1)
                    act.wait_ge(down, i + 2)
                    nc.scalar.activation(yw, B[7][:, :], ACT.Copy).then_inc(yw_ready, 1)

            norm_root(2)
            for t in range(TT):
                act.wait_ge(resid, 2 * TT + 2 * t + 2 * TT + 2)
                act.dma_start(out[0, t * P:(t + 1) * P, :], xn[:, t, :]).then_inc(out_sem, 16)

        @block.tensor
        def _(pe):
            mm = nc.tensor.matmul

            def turn(i):
                pe.wait_ge(xn_ready, TT * (i + 1))
                for k in range(KB):
                    for t in range(TT):
                        last = nc.tensor.transpose(B[4 + k // 2][:, (k % 2) * S + t * P:(k % 2) * S + (t + 1) * P],
                                                   xn[:, t, k * P:(k + 1) * P], ident)
                    if k % 2:
                        last.then_inc(xT_turned, 1)

            def project(n):
                name = SLICES[n]
                w = wslice(n)
                pe.wait_ge(landed[slot_of(2 * n)], 16 * (loads_before(2 * n) + 1))
                if n < 2:
                    pe.wait_ge(grow, 2)
                else:
                    pe.wait_ge(taken[SLICES[n - 2]], 2)
                for j in range(2):
                    bank = B[2 * (n % 2) + j]
                    if n < 2:
                        for f in range(2):
                            for k in range(KB):
                                last = mm(bank[:, f * S:(f + 1) * S], w[:, k, (2 * j + f) * P:(2 * j + f + 1) * P],
                                          xnT[:, k, :], start=(k == 0), stop=(k == KB - 1))
                    else:
                        for k in range(KB):
                            last = mm(bank[:, :], xnT[:, k, j * P:(j + 1) * P], w[:, k, :],
                                      start=(k == 0), stop=(k == KB - 1))
                last.then_inc(projected, 1)
                pe.wait_ge(projected, n + 1)
                pe.sem_inc(slot_free, 2)

            pe.wait_ge(s_cst, 16)
            pe.wait_ge(s_small, 16 * 8)
            nc.tensor.transpose(B[0][:, 0:60], rows[:, :], ident[0:60, 0:60]).then_inc(rows_turned, 1)
            turn(0)
            pe.wait_ge(cols_ready, 1)
            pe.wait_ge(xT_even, 4)
            pe.wait_ge(xT_odd, 4)
            for g in range(2):
                for k in range(KB):
                    last = mm(B[g][0:MH, 0:S], wgate[:, k, g * MH:(g + 1) * MH], xnT[:, k, :],
                              start=(k == 0), stop=(k == KB - 1))
                last.then_inc(gates_done, 1)
            project(0)
            project(1)
            pe.wait_ge(grow, 10)
            for h in range(MH):
                mm(B[4 + h // 2][:, (h % 2) * S:(h % 2 + 1) * S], cst[0:MH, K_SEL + P * h:K_SEL + P * (h + 1)],
                   gr[:, 6, :], start=True, stop=True).then_inc(mbc, 1)
            for g, row in enumerate((5, 7)):
                for t in range(TT):
                    last = nc.tensor.transpose(B[6][:, 8 * g + MH * t:8 * g + MH * (t + 1)],
                                               gr[:, row, t * P:(t + 1) * P], ident[0:MH, 0:MH])
            last.then_inc(mbc, 1)
            project(2)
            project(3)
            pe.wait_ge(silu, 2 * MH)
            for h in range(MH):
                pe.wait_ge(wexp, 3 * MH)
                pe.wait_ge(gcols, 1)
                pe.wait_ge(gcols_act, 1)
                mm(B[4 + h][:, 0:S], mqk[:, MH + h, 0:P], mqk[:, h, :], start=True, stop=True)
                mm(B[4 + h][:, S:S + P], mqk[:, MH + h, P:S], mqk[:, h, P:S], start=True, stop=True)\
                    .then_inc(mqk_done, 1)
            project(4)
            pe.wait_ge(taken["mv"], 2)
            for h in range(MH):
                pe.wait_ge(wqk, h + 1)
                o = B[4 + h]
                mm(o[:, 0:MDH + 1], wm[:, h, 0, :], vaug[:, 0, h, :], start=True, stop=True)
                mm(o[:, S:S + MDH + 1], wm[:, h, 1, :], vaug[:, 0, h, :], start=True, stop=False)
                mm(o[:, S:S + MDH + 1], wm[:, h, 2, :], vaug[:, 1, h, :], start=False, stop=True).then_inc(mpv, 1)
            project(5)
            project(6)
            pe.wait_ge(rope, 2 * TT)
            pe.wait_ge(mh, 2 * MH)
            for b in range(8):
                for t in range(TT):
                    last = nc.tensor.transpose(B[4 + b // 2][:, (b % 2) * S + t * P:(b % 2) * S + (t + 1) * P],
                                               qk[:, b // 4, t, (b % 4) * P:(b % 4 + 1) * P], ident)
                if b % 2 == 1:
                    last.then_inc(qkT_turned, 1)

            def scores(h):
                o, r = B[4 + h % 4], (h % 2) * ADH
                if h >= 4:
                    pe.wait_ge(yaT_ready, 2)
                    pe.wait_ge(pT_ready, 4)
                q, k = qkT[r:r + ADH, h // 2, :], qkT[r:r + ADH, 4 + h // 2, :]
                mm(o[:, 0:P], q[:, 0:P], k[:, 0:P], start=True, stop=True)
                mm(o[:, P:3 * P], q[:, P:S], k[:, :], start=True, stop=True).then_inc(scored, 1)

            def turn_probs(h):
                pe.wait_ge(pnorm, 2 * h + 2)
                for b in range(3):
                    last = nc.tensor.transpose(B[4 + h % 4][:, b * P:(b + 1) * P], ps[:, h % 4, b * P:(b + 1) * P], ident)
                last.then_inc(p_turned, 1)

            def attend(h):
                pe.wait_ge(pT_ready, h + 1)
                o = B[4 + (h - h % 2) % 4][(h % 2) * ADH:(h % 2 + 1) * ADH, :]
                v = av[:, :, h * ADH:(h + 1) * ADH]
                p = pt[:, h % 4, :]
                mm(o[:, 0:P], v[:, 0, :], p[:, 0:P], start=True, stop=True)
                mm(o[:, P:S], v[:, 0, :], p[:, P:2 * P], start=True, stop=False)
                last = mm(o[:, P:S], v[:, 1, :], p[:, 2 * P:3 * P], start=False, stop=True)
                if h % 2:
                    last.then_inc(apv, 1)

            pe.wait_ge(qkT_ready, 4)
            for h in range(4):
                scores(h)
            project(7)
            for h in range(4):
                turn_probs(h)
            project(8)
            pe.wait_ge(taken["av"], 2)
            for h in range(0, 4, 2):
                pe.wait_ge(pT_ready, h + 2)
                attend(h)
                attend(h + 1)
            for h in range(4, AH):
                scores(h)
            project(9)
            for h in range(4, AH):
                turn_probs(h)
            project(10)
            for h in range(4, AH, 2):
                pe.wait_ge(pT_ready, h + 2)
                attend(h)
                attend(h + 1)
            pe.wait_ge(ym, 3)
            for b in range(MH):
                if b % 2 == 0:
                    pe.wait_ge(yaT_ready, 3 + b // 2)
                    pe.wait_ge(pT_ready, AH)
                for t in range(TT):
                    last = nc.tensor.transpose(B[4 + b // 2 * 2 + 1][:, (b % 2) * S + t * P:(b % 2) * S + (t + 1) * P],
                                               hm[:, t, b, :], ident)
                if b % 2:
                    last.then_inc(ym_turned, 1)
            for j in range(4):
                pe.wait_ge(landed[slot_of(Q_BRANCH + j)], 16 * (loads_before(Q_BRANCH + j) + 1))
            for c in range(2 * TT):
                t, n = c // 2, c % 2
                if c < 2:
                    pe.wait_ge(taken[SLICES[9 + c]], 2)
                    pe.wait_ge(yaT_ready, 4)
                else:
                    pe.wait_ge(gated_br, 2 * (c - 1))
                for br, yT in ((0, yaT), (1, ymT)):
                    if br:
                        pe.wait_ge(ymT_ready, MH)
                    for b in range(4):
                        last = mm(B[2 - 2 * (c % 2) + br][:, :], yT[:, b, t * P:(t + 1) * P],
                                  wblock(Q_BRANCH, 4 * br + b)[:, n * N:(n + 1) * N], start=(b == 0), stop=(b == 3))
                last.then_inc(branched, 1)
            pe.wait_ge(branched, 2 * TT)
            pe.sem_inc(slot_free, 4)
            for t in range(TT):
                for k in range(KB):
                    if k % 4 == 0:
                        pe.wait_ge(merged, 2 * t + k // 4 + 1)
                    last = nc.tensor.transpose(B[4 + 2 * t + k // 4][:, (k % 4) * P:(k % 4 + 1) * P],
                                               mg[:, t, k * P:(k + 1) * P], ident)
                    if k % 4 == 3:
                        last.then_inc(mg_turned, 1)
            pe.wait_ge(gated_br, 4 * TT)
            for j in range(4):
                pe.wait_ge(landed[slot_of(Q_OUT + j)], 16 * (loads_before(Q_OUT + j) + 1))
            for c in range(2 * TT):
                t, n = c // 2, c % 2
                pe.wait_ge(mgT_ready, 2 * (t + 1))
                for k in range(KB):
                    last = mm(B[c][:, :], mgT[:, k, t * P:(t + 1) * P], wblock(Q_OUT, k)[:, n * N:(n + 1) * N],
                              start=(k == 0), stop=(k == KB - 1))
                last.then_inc(mixed, 1)
            pe.wait_ge(mixed, 2 * TT)
            pe.sem_inc(slot_free, 4)
            turn(1)
            pe.wait_ge(s_small2, 16 * 4)
            pe.wait_ge(xT_even, 8)
            pe.wait_ge(xT_odd, 8)
            for t in range(TT):
                for k in range(KB):
                    last = mm(B[4][:, t * E:(t + 1) * E], xnT[:, k, t * P:(t + 1) * P], wr[:, k, :],
                              start=(k == 0), stop=(k == KB - 1))
            last.then_inc(logits_done, 1)
            pe.wait_ge(router, 8)
            sel = [lg[:, t, 1, :] for t in range(TT)]
            lower = cst[:, K_LOWER:K_LOWER + P]
            mm(B[5][0:1, 0:E], ones[:, 0:1], sel[0], start=True, stop=False)
            mm(B[5][0:1, 0:E], ones[:, 0:1], sel[1], start=False, stop=True).then_inc(counted, 1)
            mm(B[6][:, 0:E], lower, sel[0], start=True, stop=True)
            mm(B[6][:, E:2 * E], lower, sel[1], start=True, stop=False)
            mm(B[6][:, E:2 * E], ones, sel[0], start=False, stop=True).then_inc(ranked, 1)
            pe.wait_ge(router, 14)
            for t in range(TT):
                last = nc.tensor.transpose(B[7][0:E, t * P:(t + 1) * P], gate[:, t, :], ident)
            last.then_inc(gate_turned, 1)
            pe.wait_ge(gateT_ready, 1)
            pe.wait_ge(resid, 2 * TT)
            for t in range(TT):
                for g in range(2):
                    mm(B[2 * t + g][:, :], gateT[:, t * P:(t + 1) * P], b2[:, g * N:(g + 1) * N],
                       start=True, stop=False, skip_group_check=True)
            for s in (gath, gt_turned, up, act_turned, down, scat):
                pe.sem_inc(s, 1)
            pe.wait_ge(tabled, 1)
            pe.wait_ge(pos_ready, 2)
            with pe.Fori(0, E) as e:
                i0 = pe.value_load(first_item[0:1, bass.ds(e, 1)], min_val=0, max_val=E + 16)
                i1 = pe.value_load(first_item[0:1, bass.ds(e + 1, 1)], min_val=1, max_val=E + 16)
                with pe.Fori(i0, i1) as i:
                    pe.wait_ge(onehot, 4 * i + 2)
                    pe.wait_ge(actT_ready, i + 1)
                    for k in range(KB):
                        for t in range(TT):
                            last = mm(B[6][:, k * C:(k + 1) * C], xn[:, t, k * P:(k + 1) * P], oneh[:, t, :],
                                      start=(t == 0), stop=(t == TT - 1))
                    last.then_inc(gath, 1)
                    pe.wait_ge(onehot, 4 * i + 4)
                    pe.wait_ge(yw_ready, i + 1)
                    for t in range(TT):
                        last = nc.tensor.transpose(B[7][:, t * P:(t + 1) * P], gated[:, t, :], ident)
                    last.then_inc(gt_turned, 1)
                    pe.wait_ge(b1_in, 16 * e + 16)
                    pe.wait_ge(gl_ready, 2 * i + 2)
                    for g in range(2):
                        for u in range(2):
                            last = mm(B[4 + u][g * C:(g + 1) * C, :], ones[0:1, 0:C],
                                      b1row[0:1, u * FF + g * N:u * FF + (g + 1) * N], start=True, stop=False,
                                      skip_group_check=True)
                    last.then_inc(b1_free, 1)
                    pe.wait_ge(xg_ready, i + 1)
                    for k in range(KB):
                        q = slot_of(Q_MOE + k)
                        pe.wait_ge(landed[q], e * 16 + 16 * (loads_before(Q_MOE + k) + 1))
                        for u in range(2):
                            for g in range(2):
                                last = mm(B[4 + u][g * C:(g + 1) * C, :], xgT[:, k, :],
                                          ring[:, q, u * FF + g * N:u * FF + (g + 1) * N],
                                          start=False, stop=(k == KB - 1), skip_group_check=True)
                        if k < KB - 1:
                            last.then_inc(slot_free, 1)
                        else:
                            last.then_inc(up, 1)
                    pe.wait_ge(up, i + 2)
                    pe.sem_inc(slot_free, 1)
                    pe.wait_ge(act_ready, i + 1)
                    for j in range(4):
                        last = nc.tensor.transpose(B[6][:, j * P:(j + 1) * P], actv[:, j * P:(j + 1) * P], ident)
                    last.then_inc(act_turned, 1)
                    pe.wait_ge(gT_ready, i + 1)
                    pe.wait_ge(actT_ready, i + 2)
                    for j in range(4):
                        q = slot_of(Q_MOE + KB + j)
                        pe.wait_ge(landed[q], e * 16 + 16 * (loads_before(Q_MOE + KB + j) + 1))
                        for h in range(2):
                            for g in range(2):
                                last = mm(B[7][g * C:(g + 1) * C, :], actT[:, j, h * C:(h + 1) * C],
                                          ring[:, q, h * D + g * N:h * D + (g + 1) * N],
                                          start=(j == 0 and h == 0), stop=(j == 3 and h == 1), skip_group_check=True)
                        if j < 3:
                            last.then_inc(slot_free, 1)
                        else:
                            last.then_inc(down, 1)
                    pe.wait_ge(down, i + 2)
                    pe.sem_inc(slot_free, 1)
                    pe.wait_ge(yw_ready, i + 2)
                    for t in range(TT):
                        for g in range(2):
                            last = mm(B[2 * t + g][:, :], gatedT[g * C:(g + 1) * C, t * P:(t + 1) * P],
                                      yw[g * C:(g + 1) * C, :], start=False, stop=False, skip_group_check=True)
                    last.then_inc(scat, 1)

        @block.vector
        def _(dve):
            v = nc.vector

            def norm(i, t_from=0):
                dve.wait_ge(sumsq, TT * (i + 1))
                v.tensor_scalar(st[:, 2:4], st[:, 0:2], 1.0 / D, EPS, ALU.mult, ALU.add).then_inc(meansq, 1)
                dve.wait_ge(root, i + 1)
                v.reciprocal(st[:, 6:8], st[:, 4:6]).then_inc(rstd, 1)
                dve.wait_ge(rstd, i + 1)

            def squares(t):
                v.tensor_tensor_reduce(xn[:, t, :], xs[:, t, :], xs[:, t, :], 1.0, 0.0, ALU.mult, ALU.add,
                                       st[:, t:t + 1]).then_inc(sumsq, 1)

            def xT(i, first):
                for k in (0, 1, 4, 5):
                    dve.wait_ge(xT_turned, 4 * i + k // 2 + 1)
                    v.tensor_scalar(xnT[:, k, :], B[4 + k // 2][:, (k % 2) * S:(k % 2 + 1) * S], wcol(first + k),
                                    None, ALU.mult)\
                     .then_inc(xT_even, 1)

            dve.wait_ge(s_x, 16)
            for t in range(TT):
                squares(t)
            norm(0)
            for t in range(TT):
                v.tensor_scalar(xn[:, t, :], xs[:, t, :], st[:, 6 + t:7 + t], None, ALU.mult).then_inc(xn_ready, 1)
            dve.wait_ge(rows_turned, 1)
            v.tensor_copy(cols[:, :], B[0][:, 0:60]).then_inc(cols_ready, 1)
            dve.wait_ge(cols_ready, 1)
            xT(0, NORM_MIX)
            dve.wait_ge(gates_done, 2)
            for g in range(2):
                v.tensor_scalar(gr[:, g, :], B[g][0:MH, 0:S], gbias[:, g:g + 1], None, ALU.add).then_inc(grow, 1)
            dve.wait_ge(grow, 2)
            v.scalar_tensor_tensor(out=gr[:, 2, :], in0=gr[:, 1, :], scalar=-1.0, in1=gr[:, 1, :],
                                   op0=ALU.mult, op1=ALU.max).then_inc(grow, 1)
            dve.wait_ge(gexp, 1)
            v.tensor_scalar(gr[:, 3, :], gr[:, 3, :], 1.0, None, ALU.add).then_inc(grow, 1)
            dve.wait_ge(gexp, 2)
            v.scalar_tensor_tensor(out=gr[:, 4, :], in0=gr[:, 1, :], scalar=0.0, in1=gr[:, 3, :],
                                   op0=ALU.min, op1=ALU.subtract).then_inc(grow, 1)
            dve.wait_ge(grow, 5)
            v.tensor_tensor_scan(gr[:, 2, :], gr[:, 4, :], gr[:, 4, :], 0.0, ALU.add, ALU.bypass).then_inc(grow, 1)
            dve.wait_ge(grow, 6)
            v.tensor_tensor(gr[:, 5, :], gr[:, 0, :], gr[:, 2, :], ALU.subtract).then_inc(grow, 1)
            dve.wait_ge(grow, 7)
            v.tensor_tensor_scan(gr[:, 4, :], gr[:, 5, :], gr[:, 5, :], 0.0, ALU.max, ALU.bypass).then_inc(grow, 1)
            dve.wait_ge(grow, 8)
            v.tensor_scalar(gr[:, 6, :], gr[:, 4, :], -1.0, None, ALU.mult).then_inc(grow, 1)
            v.scalar_tensor_tensor(out=gr[:, 7, :], in0=gr[:, 2, :], scalar=-1.0, in1=gr[:, 4, :],
                                   op0=ALU.mult, op1=ALU.subtract).then_inc(grow, 1)

            def convolve(g):
                dve.wait_ge(taken["mk" if g else "mq"], 2)
                for j in range(CONV - 1, -1, -1):
                    for b in range(MH * g, MH * (g + 1)):
                        w = wcol(CONV_W + 2 * MH * j + b)
                        if j == CONV - 1:
                            v.tensor_scalar(mqk[:, b, :], pre[:, b, j:j + S], w, wcol(CONV_B + b), ALU.mult, ALU.add)\
                             .then_inc(conv, 1)
                        else:
                            dve.wait_ge(conv, MH * CONV * g + MH * (CONV - 2 - j) + (b - MH * g) + 1)
                            v.scalar_tensor_tensor(out=mqk[:, b, :], in0=pre[:, b, j:j + S], scalar=w,
                                                   in1=mqk[:, b, :], op0=ALU.mult, op1=ALU.add).then_inc(conv, 1)

            def silu_mul(g):
                dve.wait_ge(silu_sig, g + 1)
                for b in range(MH * g, MH * (g + 1)):
                    v.scalar_tensor_tensor(out=mqk[:, b, :], in0=mqk[:, b, :], scalar=MDH ** -0.5 if g else 1.0,
                                           in1=sg[:, b, :], op0=ALU.mult, op1=ALU.mult).then_inc(silu, 1)

            def rotate(g):
                name = "ak" if g else "aq"
                n = SLICES.index(name)
                dve.wait_ge(projected, n + 1)
                for t in range(TT):
                    src = B[2 * (n % 2) + t][:, :].rearrange("p (h d) -> p h d", h=AH)
                    cos = cst[:, K_COS + ADH * t:K_COS + ADH * (t + 1)].unsqueeze(1).broadcast_to([P, AH, ADH])
                    sin = cst[:, K_SIN + 32 * t:K_SIN + 32 * (t + 1)].unsqueeze(1).broadcast_to([P, AH, 32])
                    a = rt[:, 0, :].rearrange("p (h d) -> p h d", h=AH)
                    b = rt[:, 1, :].rearrange("p (h d) -> p h d", h=AH)
                    o = qk[:, g, t, :].rearrange("p (h d) -> p h d", h=AH)
                    v.tensor_tensor(a, src, cos, ALU.mult).then_inc(rope_step, 1)
                    v.tensor_tensor(b[:, :, 32:64], src[:, :, 0:32], sin, ALU.mult).then_inc(rope_step, 1)
                    v.tensor_tensor(b[:, :, 0:32], src[:, :, 32:64], sin, ALU.mult).then_inc(taken[name], 1)
                    dve.wait_ge(rope_step, 4 * (TT * g + t) + 2)
                    dve.wait_ge(taken[name], t + 1)
                    v.tensor_tensor(o[:, :, 0:32], a[:, :, 0:32], b[:, :, 0:32], ALU.subtract).then_inc(rope_step, 1)
                    v.tensor_tensor(o[:, :, 32:64], a[:, :, 32:64], b[:, :, 32:64], ALU.add).then_inc(rope_step, 1)
                    dve.wait_ge(rope_step, 4 * (TT * g + t) + 4)
                    dve.sem_inc(rope, 1)

            convolve(0)
            silu_mul(0)
            convolve(1)
            silu_mul(1)
            dve.wait_ge(mbc, MH + 1)
            v.tensor_copy(gcol[:, 0, :, :], B[6][:, 0:8].rearrange("p (t h) -> p t h", t=TT)).then_inc(gcols, 1)
            dve.wait_ge(gcols, 1)
            maskT = cst[:, K_MASKT:K_MASKT + P]
            for b in range(2):
                dst = dg[:, 4 * b:4 * b + 4, :]
                src = B[4 + b][:, :].rearrange("p (a s) -> p a s", a=4)
                ins = v.tensor_tensor(dst, src, maskT.unsqueeze(1).broadcast_to([P, 4, P]), ALU.add)
                ins.then_inc(diag_half, 1)
            dve.wait_ge(diag_half, 2)
            dve.sem_inc(diag, 1)
            rotate(0)
            for h in range(MH):
                dve.wait_ge(mqk_done, h + 1)
                dve.wait_ge(wexp, 3 * (h + 1))
                w = wm[:, h, :, :].rearrange("p b s -> p (b s)")
                v.tensor_tensor(w, B[4 + h][:, 0:3 * P], w, ALU.mult).then_inc(wqk, 1)
            rotate(1)
            dve.wait_ge(gcols_act, 1)
            for h in range(MH):
                dve.wait_ge(mpv, h + 1)
                o = B[4 + h][:, :].rearrange("p (t n) -> p t n", t=TT)
                den = o[:, :, MDH]
                v.tensor_scalar(dn[:, h, 2, :], den, -1.0, None, ALU.mult).then_inc(mden, 1)
                dve.wait_ge(mden, 4 * h + 1)
                v.tensor_tensor(dn[:, h, 0, :], den, dn[:, h, 2, :], ALU.max).then_inc(mden, 1)
                dve.wait_ge(mden, 4 * h + 2)
                v.tensor_tensor(dn[:, h, 0, :], dn[:, h, 0, :], gcol[:, 1, :, h], ALU.max).then_inc(mden, 1)
                dve.wait_ge(mden, 4 * h + 3)
                v.reciprocal(dn[:, h, 1, :], dn[:, h, 0, :]).then_inc(mden, 1)
                dve.wait_ge(mden, 4 * h + 4)
                for t in range(TT):
                    v.tensor_scalar(hm[:, t, h, :], o[:, t, 0:MDH], dn[:, h, 1, t:t + 1], None, ALU.mult)\
                     .then_inc(mh, 1)
            dve.wait_ge(mh, 2 * MH)
            hsq = sg[:, 0:4, :].rearrange("p a s -> p (a s)")
            hall = hm[:, :, :, :].rearrange("p t h d -> p (t h d)")
            h8 = hm[:, :, :, :].rearrange("p t h d -> p (t h) d")
            v.tensor_tensor(hsq, hall, hall, ALU.mult).then_inc(hnorm, 1)
            dve.wait_ge(hnorm, 1)
            v.tensor_reduce(hs[:, 0, :, :].rearrange("p t h -> p (t h)"), hsq.rearrange("p (a d) -> p a d", a=8),
                            AX, ALU.add).then_inc(hnorm, 1)
            dve.wait_ge(hnorm, 2)
            v.tensor_scalar(hs[:, 1, :, :], hs[:, 0, :, :], 1.0 / MDH, EPS, ALU.mult, ALU.add).then_inc(hnorm, 1)
            for b in range(4):
                dve.wait_ge(qkT_turned, b + 1)
                v.tensor_copy(qkT[:, 2 * b:2 * b + 2, :], B[4 + b][:, :].rearrange("p (a s) -> p a s", a=2))\
                 .then_inc(qkT_ready, 1)
            dve.wait_ge(hroot, 1)
            v.reciprocal(hs[:, 3, :, :], hs[:, 2, :, :]).then_inc(ym, 1)
            dve.wait_ge(ym, 1)
            v.tensor_tensor(h8, h8, hs[:, 3, :, :].rearrange("p t h -> p (t h)").unsqueeze(2).broadcast_to([P, 8, MDH]),
                            ALU.mult).then_inc(ym, 1)
            dve.wait_ge(ym, 2)
            dve.wait_ge(taken["mo"], 2)
            v.tensor_tensor(hall, hall, smo[:, :, :].rearrange("p t n -> p (t n)"), ALU.mult).then_inc(ym, 1)

            mask = cst[:, K_MASK:K_MASK + P]

            def head_max(h):
                dve.wait_ge(scored, h + 1)
                o = B[4 + h % 4]
                for t in range(TT):
                    d = o[:, 2 * P * t:2 * P * t + P]
                    v.tensor_tensor(d, d, mask, ALU.add).then_inc(masked, 1)
                dve.wait_ge(masked, 2 * h + 2)
                for t in range(TT):
                    lo, hi = (0, P) if t == 0 else (P, 3 * P)
                    v.tensor_reduce(am[:, h, 0, t:t + 1], o[:, lo:hi], AX, ALU.max).then_inc(smax, 1)
                dve.wait_ge(smax, 2 * h + 2)
                v.tensor_scalar(am[:, h, 1, :], am[:, h, 0, :], -ADH ** -0.5, None, ALU.mult).then_inc(nsmax, 1)

            def head_norm(h):
                dve.wait_ge(probs, 2 * h + 2)
                v.reciprocal(am[:, h, 3, :], am[:, h, 2, :]).then_inc(psum_r, 1)
                dve.wait_ge(psum_r, h + 1)
                for t in range(TT):
                    lo, hi = (0, P) if t == 0 else (P, 3 * P)
                    v.tensor_scalar(ps[:, h % 4, lo:hi], ps[:, h % 4, lo:hi], am[:, h, 3, t:t + 1], None, ALU.mult)\
                     .then_inc(pnorm, 1)

            def take_pT(h):
                dve.wait_ge(p_turned, h + 1)
                if h >= 4:
                    dve.wait_ge(apv, 2)
                v.tensor_copy(pt[:, h % 4, :], B[4 + h % 4][:, 0:3 * P]).then_inc(pT_ready, 1)

            def take_yaT(j):
                dve.wait_ge(apv, j + 1)
                v.tensor_copy(yaT[:, j, :], B[4 + 2 * (j % 2)][:, 0:S]).then_inc(yaT_ready, 1)

            for g in range(2):
                for h in range(4 * g, 4 * g + 4):
                    head_max(h)
                for h in range(4 * g, 4 * g + 4):
                    head_norm(h)
                for h in range(4 * g, 4 * g + 4):
                    take_pT(h)
                for j in range(2 * g, 2 * g + 2):
                    take_yaT(j)
            for b in range(MH):
                dve.wait_ge(ym_turned, b // 2 + 1)
                v.tensor_scalar(ymT[:, b, :], B[4 + b // 2 * 2 + 1][:, (b % 2) * S:(b % 2 + 1) * S], wcol(HEAD_W + b),
                                None, ALU.mult).then_inc(ymT_ready, 1)
            dve.wait_ge(taken["gm1"], 2)
            for c in range(2 * TT):
                t, n = c // 2, c % 2
                dve.wait_ge(branched, c + 1)
                cut = slice(n * N, (n + 1) * N)
                v.tensor_tensor(sga[:, t, cut], B[2 - 2 * (c % 2)][:, :], sga[:, t, cut], ALU.mult).then_inc(gated_br, 1)
                v.tensor_tensor(sgm[:, t, cut], B[2 - 2 * (c % 2) + 1][:, :], sgm[:, t, cut], ALU.mult).then_inc(gated_br, 1)
                dve.wait_ge(gated_br, 2 * c + 2)
                v.tensor_tensor(mg[:, t, cut], sga[:, t, cut], sgm[:, t, cut], ALU.add).then_inc(merged, 1)
            for c in range(2 * TT):
                t, n = c // 2, c % 2
                cut = slice(n * N, (n + 1) * N)
                dve.wait_ge(mixed, c + 1)
                v.tensor_tensor(xs[:, t, cut], B[c][:, :], xs[:, t, cut], ALU.add).then_inc(resid, 1)
                if n:
                    dve.wait_ge(resid, c + 1)
                    squares(t)
            norm(1)
            for t in range(TT):
                v.tensor_scalar(xn[:, t, :], xs[:, t, :], st[:, 6 + t:7 + t], None, ALU.mult).then_inc(xn_ready, 1)
            xT(1, NORM_FFN)
            dve.wait_ge(s_small2, 16 * 4)
            for t in range(TT):
                dve.wait_ge(logits_done, 1)
                v.tensor_tensor(lg[:, t, 0, :], B[4][:, t * E:(t + 1) * E], brt[:, :], ALU.add).then_inc(router_step, 1)
                dve.wait_ge(router_step, 3 * t + 1)
                v.max(out=mx8[:, t, 0:8], in_=lg[:, t, 0, :]).then_inc(router_step, 1)
                dve.wait_ge(router_step, 3 * t + 2)
                v.tensor_scalar(mx8[:, t, 8:9], mx8[:, t, 0:1], -1.0, None, ALU.mult).then_inc(router, 1)
                v.tensor_scalar(mx8[:, t, TOPK:8], mx8[:, t, TOPK:8], 0.0, 3.0e38, ALU.mult, ALU.add)\
                 .then_inc(router_step, 1)
                dve.wait_ge(router_step, 3 * t + 3)
                v.match_replace(out=lg[:, t, 3, :], in_to_replace=mx8[:, t, 0:8], in_values=lg[:, t, 0, :],
                                imm_value=-3.0e38).then_inc(router, 1)
            dve.wait_ge(router, 4)
            for t in range(TT):
                v.tensor_tensor(lg[:, t, 1, :], lg[:, t, 0, :], lg[:, t, 3, :], ALU.not_equal).then_inc(router, 1)
            dve.wait_ge(router, 6)
            dve.wait_ge(rexp, 2)
            for t in range(TT):
                v.tensor_tensor_reduce(lg[:, t, 4, :], lg[:, t, 2, :], lg[:, t, 1, :], 1.0, 0.0, ALU.mult, ALU.add,
                                       mx8[:, t, 9:10]).then_inc(router, 1)
            dve.wait_ge(router, 8)
            for t in range(TT):
                v.reciprocal(mx8[:, t, 10:11], mx8[:, t, 9:10]).then_inc(router, 1)
            dve.wait_ge(router, 10)
            for t in range(TT):
                v.tensor_scalar(gate[:, t, :], lg[:, t, 4, :], mx8[:, t, 10:11], None, ALU.mult).then_inc(router, 1)
            dve.wait_ge(counted, 1)
            v.tensor_scalar(cnt[:, 0, :], B[5][0:1, 0:E], C + 0.5, 1.0, ALU.is_gt, ALU.add).then_inc(router, 1)
            v.tensor_scalar(cnt[:, 1, :], B[5][0:1, 0:E], 2 * C + 0.5, None, ALU.is_gt).then_inc(router, 1)
            dve.wait_ge(router, 14)
            v.tensor_scalar(cnt[:, 2, :], B[5][0:1, 0:E], 3 * C + 0.5, None, ALU.is_gt).then_inc(count_step, 1)
            v.tensor_tensor(cnt[:, 0, :], cnt[:, 0, :], cnt[:, 1, :], ALU.add).then_inc(count_step, 1)
            dve.wait_ge(count_step, 2)
            v.tensor_tensor(cnt[:, 0, :], cnt[:, 0, :], cnt[:, 2, :], ALU.add).then_inc(count_step, 1)
            dve.wait_ge(count_step, 3)
            v.tensor_tensor_scan(cnt[:, 3, :], cnt[:, 0, :], cnt[:, 0, :], 0.0, ALU.add, ALU.bypass).then_inc(count_step, 1)
            v.memset(first_item[:, 0:1], 0).then_inc(count_step, 1)
            dve.wait_ge(count_step, 5)
            v.tensor_copy(first_item[:, 1:E + 1], cnt[:, 3, :]).then_inc(tabled, 1)
            dve.wait_ge(ranked, 1)
            for t in range(TT):
                v.scalar_tensor_tensor(out=pos[:, t, :], in0=B[6][:, t * E:(t + 1) * E], scalar=1.0,
                                       in1=lg[:, t, 1, :], op0=ALU.add, op1=ALU.mult).then_inc(pos_step, 1)
            dve.wait_ge(pos_step, 2)
            v.tensor_scalar(pos[:, :, :], pos[:, :, :], -1.0, None, ALU.add).then_inc(pos_ready, 1)
            dve.wait_ge(gate_turned, 1)
            v.tensor_copy(gateT[:, :], B[7][0:E, 0:S]).then_inc(gateT_ready, 1)
            dve.wait_ge(pos_ready, 1)
            dve.wait_ge(gateT_ready, 1)
            dve.sem_inc(pos_ready, 1)
            for s, n in ((gl_ready, 2), (actT_ready, 1)):
                dve.sem_inc(s, n)
            dve.wait_ge(tabled, 1)
            with dve.Fori(0, E) as e:
                i0 = dve.value_load(first_item[0:1, bass.ds(e, 1)], min_val=0, max_val=E + 16)
                i1 = dve.value_load(first_item[0:1, bass.ds(e + 1, 1)], min_val=1, max_val=E + 16)
                with dve.Fori(i0, i1) as i:
                    r = nc.s_assert_within(i1 - 1 - i, 0, NR - 1, skip_runtime_bounds_check_because=
                                           "an expert has 1 to NR tiles, by the sum that made the table")
                    places = cst[:, bass.ds(r * C + K_IOTA, C)]
                    dve.wait_ge(gath, i + 1)
                    for t in range(TT):
                        v.tensor_scalar(oneh[:, t, :], places, pos[:, t, bass.ds(e, 1)],
                                        None, ALU.is_equal).then_inc(onehot, 1)
                    dve.wait_ge(gt_turned, i + 1)
                    for t in range(TT):
                        v.tensor_scalar(gated[:, t, :].rearrange("p (g s) -> p g s", g=2),
                                        places.unsqueeze(1).broadcast_to([P, 2, C]), pos[:, t, bass.ds(e, 1)],
                                        gate[:, t, bass.ds(e, 1)], ALU.is_equal, ALU.mult).then_inc(onehot, 1)
                    dve.wait_ge(gath, i + 2)
                    dve.wait_ge(up, i + 1)
                    wf = cols[:, NORM_FFN:NORM_FFN + KB].unsqueeze(2).broadcast_to([P, KB, C])
                    v.tensor_tensor(xgT, B[6][:, :].rearrange("p (k s) -> p k s", k=KB), wf, ALU.mult)\
                     .then_inc(xg_ready, 1)
                    dve.wait_ge(up, i + 2)
                    dve.wait_ge(sig_ready, i + 1)
                    v.tensor_scalar(glu, B[4][:, :], LIMIT, None, ALU.min).then_inc(gl_ready, 1)
                    v.tensor_scalar(lin, B[5][:, :], LIMIT, -LIMIT, ALU.min, ALU.max).then_inc(gl_ready, 1)
                    dve.wait_ge(gl_ready, 2 * i + 4)
                    v.scalar_tensor_tensor(out=lin, in0=lin, scalar=1.0, in1=glu, op0=ALU.add, op1=ALU.mult)\
                     .then_inc(glin, 1)
                    dve.wait_ge(glin, i + 1)
                    dve.wait_ge(sig_ready, i + 2)
                    dve.wait_ge(act_turned, i + 1)
                    v.tensor_tensor(actv, lin, sig, ALU.mult).then_inc(act_ready, 1)
                    dve.wait_ge(act_turned, i + 2)
                    dve.wait_ge(down, i + 1)
                    v.tensor_copy(actT, B[6][:, :].rearrange("p (j c) -> p j c", j=4)).then_inc(actT_ready, 1)
            items = dve.value_load(first_item[0:1, E:E + 1], min_val=1, max_val=E + 16)
            dve.wait_ge(scat, items + 1)
            for c in range(2 * TT):
                t, n = c // 2, c % 2
                cut = slice(n * N, (n + 1) * N)
                v.tensor_tensor(xs[:, t, cut], B[c][:, :], xs[:, t, cut], ALU.add).then_inc(resid, 1)
                if n:
                    dve.wait_ge(resid, 2 * TT + c + 1)
                    squares(t)
            norm(2)
            for t in range(TT):
                v.tensor_scalar(xn[:, t, :], xs[:, t, :], st[:, 6 + t:7 + t], None, ALU.mult).then_inc(resid, 1)
                dve.wait_ge(resid, 4 * TT + 2 * t + 1)
                v.tensor_tensor(xn[:, t, :], xn[:, t, :], wfin[:, :], ALU.mult).then_inc(resid, 1)


_INS = ["x", "norm_mix_w", "w_in", "m_conv_w", "m_conv_b", "m_gate_bias", "m_head_norm_w", "w_branch", "w_out",
        "norm_ffn_w", "w_router", "b_router", "w_mlp1", "b_mlp1", "w_mlp2", "b_mlp2", "norm_final_w"]


def kernel(**inputs):
    import concourse.bacc as _bacc
    from concourse.bass_utils import run_bass_kernel_spmd as _run

    nc = _bacc.Bacc("TRN2", target_bir_lowering=False, num_devices=1)
    arrays, args = {}, []
    for name in _INS:
        a = np.ascontiguousarray(inputs[name])
        arrays[f"in_{name}_dram"] = a
        args.append(nc.dram_tensor(f"in_{name}_dram", a.shape, mybir.dt.from_np(a.dtype), kind="ExternalInput").ap())
    table = constants()
    arrays["table_dram"] = table
    args.append(nc.dram_tensor("table_dram", table.shape, F32, kind="ExternalInput").ap())
    args.append(nc.dram_tensor("out_dram", (1, S, D), F32, kind="ExternalOutput").ap())
    build(nc, *args)
    r = _run(nc, [arrays], core_ids=[0])
    return r.results[0]["out_dram"]
```

```python
from contextlib import ExitStack

import numpy as np

import concourse.bass as bass
from concourse import mybir

F32 = mybir.dt.float32
I32 = mybir.dt.int32
ALU = mybir.AluOpType
ACT = mybir.ActivationFunctionType
AX = mybir.AxisListType.X

P = 128
S = 256
TT = S // P
D = 1024
KB = D // P
AH, ADH = 8, 64
MH, MDH = 4, 128
AW = AH * ADH
MW = MH * MDH
CONV = 4
E = 32
TOPK = 4
FF = 1024
C = 64
NR = S // C
LIMIT = 7.0
ALPHA = 1.702
EPS = 1e-6
NEG = -1e30
N = 512

O_MI = 3 * AW + 4 * MW
O_G = O_MI + 2 * MH
SLICES = ["mq", "mk", "mv", "aq", "ak", "av", "mo", "ga0", "ga1", "gm0", "gm1"]
COL = {"aq": 0, "ak": AW, "av": 2 * AW, "mq": 3 * AW, "mk": 3 * AW + MW, "mv": 3 * AW + 2 * MW,
       "mo": 3 * AW + 3 * MW, "ga0": O_G, "ga1": O_G + N, "gm0": O_G + 2 * N, "gm1": O_G + 3 * N}

SLOT = 2 * FF
RING = 12
Q_BRANCH = 2 * len(SLICES)
Q_OUT = Q_BRANCH + 4
Q_MOE = Q_OUT + 4
ITEMS = E + S * TOPK // C
PER_EXPERT = 12
assert RING == PER_EXPERT

K_ID, K_COS, K_SIN = 0, 128, 256
K_MASK, K_MASKT, K_LOWER, K_ONES = 320, 448, 576, 704
K_IOTA, K_SEL, K_END = 832, 1088, 1600


def constants():
    c = np.zeros((P, K_END), np.float32)
    p = np.arange(P)
    c[:, K_ID:K_ID + P] = np.eye(P)
    inv = np.float32(10000.0) ** (-np.arange(0, ADH, 2, dtype=np.float32) / np.float32(ADH))
    for t in range(TT):
        ang = (p + P * t).astype(np.float32)[:, None] * inv[None, :].astype(np.float32)
        c[:, K_COS + ADH * t:K_COS + ADH * (t + 1)] = np.tile(np.cos(ang), 2)
        c[:, K_SIN + 32 * t:K_SIN + 32 * (t + 1)] = np.sin(ang)
    c[:, K_MASK:K_MASK + P] = np.where(p[None, :] <= p[:, None], 0.0, NEG)
    c[:, K_MASKT:K_MASKT + P] = np.where(p[:, None] <= p[None, :], 0.0, NEG)
    c[:, K_LOWER:K_LOWER + P] = p[:, None] < p[None, :]
    c[:, K_ONES:K_ONES + P] = 1.0
    c[:, K_IOTA:K_IOTA + S] = np.arange(S)
    for h in range(MH):
        c[h, K_SEL + P * h:K_SEL + P * (h + 1)] = 1.0
    return c


def slot_of(q):
    return q % RING


def build(nc, x, norm_mix_w, w_in, m_conv_w, m_conv_b, m_gate_bias, m_head_norm_w, w_branch, w_out,
          norm_ffn_w, w_router, b_router, w_mlp1, b_mlp1, w_mlp2, b_mlp2, norm_final_w, table, out):
    with ExitStack() as ctx:
        def sb(name, shape, dt=F32):
            return ctx.enter_context(nc.sbuf_tensor(name, shape, dt))

        def sem(name):
            return ctx.enter_context(nc.semaphore(name))

        ring = sb("ring", [P, RING, SLOT])
        cst = sb("cst", [P, K_END])
        xs = sb("xs", [P, TT, D])
        xn = sb("xn", [P, TT, D])
        xnT = sb("xnT", [P, KB, S])
        rows = sb("rows", [60, P])
        cols = sb("cols", [P, 60])
        gbias = sb("gbias", [MH, 2])
        wgate = sb("wgate", [P, KB, 2 * MH])
        wr = sb("wr", [P, KB, E])
        brt = sb("brt", [P, E])
        st = sb("st", [P, 16])
        pre = sb("pre", [P, 2 * MH, S + 3])
        mqk = sb("mqk", [P, 2 * MH, S])
        warm = sb("warm", [1, 1])
        gr = sb("gr", [MH, 8, S])
        gcol = sb("gcol", [P, 2, TT, MH])
        wm = sb("wm", [P, MH, 3, P])
        vaug = sb("vaug", [P, TT, MH, MDH + 1])
        av = sb("av", [P, TT, AW])
        smo = sb("smo", [P, TT, MW])
        sga = sb("sga", [P, TT, D])
        sgm = sb("sgm", [P, TT, D])
        hm = sb("hm", [P, TT, MH, MDH])
        dn = sb("dn", [P, MH, 3, TT])
        hs = sb("hs", [P, 4, TT, MH])
        qk = sb("qk", [P, 2, TT, AW])
        rt = sb("rt", [P, 2, AW])
        am = sb("am", [P, AH, 4, TT])
        qkT = xn[:, :, :].rearrange("p a (b s) -> p (a b) s", s=S)
        sg = sga[:, :, :].rearrange("p t (a s) -> p (t a) s", s=S)
        dg = smo[:, :, :].rearrange("p t (a s) -> p (t a) s", s=P)
        ps = wm[:, :, :, :].rearrange("p h b s -> p h (b s)")
        pt = mqk[:, :, :].rearrange("p a s -> p (a s)")[:, 0:4 * 3 * P].rearrange("p (a s) -> p a s", a=4)
        wffn = smo[:, :, :].rearrange("p t n -> p (t n)")
        wfin = av[:, :, :].rearrange("p t n -> p (t n)")
        b2 = rt[0:E, :, :].rearrange("p a n -> p (a n)")
        b1row = pre[0:1, :, :].rearrange("p a s -> p (a s)")[:, 0:2 * FF]
        yaT = pre[:, 0:4, 0:S]
        ymT = pre[:, 4:8, 0:S]
        mg = qk[:, :, :, :].rearrange("p a t n -> p (a t n)").rearrange("p (t n) -> p t n", t=TT)
        mgT = xnT
        lg = sb("lg", [P, TT, 6, E])
        mx8 = sb("mx8", [P, TT, 16])
        pos = sb("pos", [P, TT, E + 1])
        gate = sb("gate", [P, TT, E + 1])
        gateT = sb("gateT", [E, S])
        cnt = sb("cnt", [1, 5, E])
        first_item = sb("first_item", [1, E + 2], I32)
        item_expert = sb("item_expert", [1, ITEMS + 1], I32)
        item_sum = sb("item_sum", [1, ITEMS + 1])
        moe = sga[:, :, :].rearrange("p t n -> p (t n)")
        moe2 = sgm[:, :, :].rearrange("p t n -> p (t n)")
        xgT = moe[:, 0:N].rearrange("p (j g s) -> p j g s", j=4, g=2)
        xg = moe2[:, 3 * N:4 * N]
        glu = moe[:, N:2 * N]
        lin = moe[:, 2 * N:3 * N]
        actv = moe[:, 3 * N:4 * N]
        sig = moe2[:, 0:N]
        actT = moe2[:, N:2 * N].rearrange("p (j c) -> p j c", j=4)
        yw = moe2[:, 2 * N:3 * N]
        oneh = hm[:, :, 0, 0:C]
        gated = hm[:, :, 1, :]
        gatedT = smo[:, 0, 0:S]

        B = [ctx.enter_context(nc.psum_tensor(f"bank{i}", [P, N], F32)) for i in range(8)]

        s_wffn = sem("norm_ffn_w_in")
        s_x, s_cst, s_small, s_small2 = sem("x_in"), sem("constants_in"), sem("small_in"), sem("late_small_in")
        landed = [sem(f"slot{i}_landed") for i in range(RING)]
        slots_used = sem("slots_used")
        sumsq, meansq, root, rstd = sem("sumsq"), sem("meansq"), sem("root"), sem("rstd")
        xn_ready = sem("xn_ready")
        rows_turned, cols_ready = sem("rows_turned"), sem("cols_ready")
        xT_turned, xT_even, xT_odd = sem("xT_turned"), sem("xT_even"), sem("xT_odd")
        gates_done, grow, gexp = sem("gates_done"), sem("gate_rows"), sem("gate_exp")
        pads = sem("pads")
        taken = {n: sem(f"taken_{n}") for n in SLICES}
        conv, silu_sig, silu = sem("conv"), sem("silu_sigmoid"), sem("silu")
        mbc, gcols, gcols_act, diag, wexp = sem("m_broadcast"), sem("gate_cols"), sem("gate_cols_exp"), sem("diag"), sem("w_exp")
        mqk_done, wqk, mpv, mden, mh = sem("m_qk"), sem("w_times_qk"), sem("m_pv"), sem("m_den"), sem("m_h")
        hnorm, hroot, ym = sem("head_norm"), sem("head_root"), sem("y_m")
        rope = sem("rope")
        qkT_turned, qkT_ready = sem("qkT_turned"), sem("qkT_ready")
        scored, masked, smax, nsmax = sem("scored"), sem("masked"), sem("score_max"), sem("neg_max")
        probs, psum_r, pnorm = sem("probs"), sem("prob_recip"), sem("prob_normed")
        p_turned, pT_ready, apv, yaT_ready = sem("p_turned"), sem("pT_ready"), sem("a_pv"), sem("yaT_ready")
        ym_turned, ymT_ready = sem("ym_turned"), sem("ymT_ready")
        branched, gated_br, merged = sem("branched"), sem("gated_branch"), sem("merged")
        mg_turned, mgT_ready, mixed, resid = sem("merged_turned"), sem("mergedT_ready"), sem("mixed"), sem("resid")
        logits_done, router = sem("logits_done"), sem("router")
        rexp = sem("router_exp")
        ranked, pos_ready, counted, tabled = sem("ranked"), sem("pos_ready"), sem("counted"), sem("tabled")
        gate_turned, gateT_ready = sem("gate_turned"), sem("gateT_ready")
        b1_in, b1_free = sem("b1_in"), sem("b1_free")
        onehot, gath, xg_out, xg_turned, xg_ready = (sem("onehot"), sem("gathered"), sem("xg_out"), sem("xg_turned"),
                                                      sem("xg_ready"))
        gated_ready, gt_turned, gT_ready = sem("gated_ready"), sem("gates_turned"), sem("gatedT_ready")
        glu_ready, lin_ready, sig_ready, act_ready = sem("glu_ready"), sem("lin_ready"), sem("sigmoid_ready"), sem("act_ready")
        turned_a, turned_b, actT_a, actT_b = sem("act_turned_a"), sem("act_turned_b"), sem("actT_a_ready"), sem("actT_b_ready")
        yw_ready, scat, normed = sem("y_ready"), sem("scattered"), sem("normed")
        rope_step, diag_half, router_step = sem("rope_step"), sem("diag_half"), sem("router_step")
        count_step, pos_step, glin = sem("count_step"), sem("pos_step"), sem("glu_times_lin")
        last_rows = sem("last_rows")
        warmed, neg_top, chosen, gates_ready = sem("warmed"), sem("neg_top"), sem("chosen"), sem("gates_ready")
        out_sem = sem("out_stored")

        ident = cst[:, K_ID:K_ID + P]
        ones = cst[:, K_ONES:K_ONES + P]

        def wcol(i):
            return cols[:, i:i + 1]

        NORM_MIX, NORM_FFN, CONV_W, CONV_B, HEAD_W = 0, 8, 16, 48, 56

        def slab(q, n):
            return ring[:, slot_of(q):slot_of(q) + n, :]

        def loads_before(q):
            return sum(1 for p in range(slot_of(q), q, RING) if p >= Q_BRANCH or p % 2 == 0)

        def wslice(n):
            return slab(2 * n, 2).rearrange("p a (k n) -> p (a k) n", n=N)

        def wblock(q0, b):
            return ring[:, slot_of(q0 + b // 2), (b % 2) * D:(b % 2 + 1) * D]

        w_in2, w_branch2, w_out2 = w_in[0], w_branch[0], w_out[0]
        block = ctx.enter_context(nc.Block())

        @block.sync
        def _(sp):
            sp.dma_start(xs[:, :, :], x[0].rearrange("(t p) d -> p t d", p=P)).then_inc(s_x, 16)
            sp.dma_start(cst[:, :], table[:, :]).then_inc(s_cst, 16)
            sp.wait_ge(s_small, 16 * 8)
            for n, name in enumerate(SLICES):
                if 2 * n >= RING:
                    sp.wait_ge(slots_used, 2 * n + 2 - RING)
                src = w_in2[:, COL[name]:COL[name] + N].rearrange("(k p) n -> p k n", p=P)
                sp.dma_start(wslice(n), src).then_inc(landed[slot_of(2 * n)], 16)
            for q0, w in ((Q_BRANCH, w_branch2), (Q_OUT, w_out2)):
                for j in range(4):
                    sp.wait_ge(slots_used, q0 + j + 1 - RING)
                    dst = ring[:, slot_of(q0 + j), :].rearrange("p (b n) -> p b n", b=2)
                    src = w[2 * P * j:2 * P * (j + 1), :].rearrange("(b p) n -> p b n", p=P)
                    sp.dma_start(dst, src).then_inc(landed[slot_of(q0 + j)], 16)

            def expert(e, freed):
                for k in range(KB):
                    sp.wait_ge(slots_used, freed(k))
                    sp.dma_start(ring[:, slot_of(Q_MOE + k), :], w_mlp1[0, e, k * P:(k + 1) * P, :])\
                      .then_inc(landed[slot_of(Q_MOE + k)], 16)
                for j in range(4):
                    k = KB + j
                    sp.wait_ge(slots_used, freed(k))
                    dst = ring[:, slot_of(Q_MOE + k), :].rearrange("p (h n) -> p h n", h=2)
                    src = w_mlp2[0, e].rearrange("(h j p) n -> j p h n", h=2, j=4)[j]
                    sp.dma_start(dst, src).then_inc(landed[slot_of(Q_MOE + k)], 16)

            expert(0, lambda k: Q_MOE + k + 1 - RING)
            sp.wait_ge(tabled, 1)
            with sp.Fori(1, E) as e:
                before = sp.value_load(first_item[0:1, bass.ds(e, 1)], min_val=1, max_val=ITEMS - 1)
                expert(e, lambda k: before * PER_EXPERT + (Q_MOE - PER_EXPERT + k + 1))
            sp.wait_ge(out_sem, 16 * TT)

        @block.gpsimd
        def _(pool):
            pool.memset(pre[:, :, 0:3], 0.0).then_inc(pads, 1)
            pool.memset(vaug[:, :, :, MDH:MDH + 1], 1.0).then_inc(pads, 1)
            pool.wait_ge(slots_used, Q_OUT)
            pool.dma_start(b1row, b_mlp1[0, 0:1, :]).then_inc(b1_in, 16)
            pool.wait_ge(tabled, 1)
            with pool.Fori(1, E) as e:
                before = pool.value_load(first_item[0:1, bass.ds(e, 1)], min_val=1, max_val=ITEMS - 1)
                pool.wait_ge(b1_free, before)
                pool.dma_start(b1row, b_mlp1[0, bass.ds(e, 1), :]).then_inc(b1_in, 16)

        @block.scalar
        def _(act):
            act.dma_start(rows[0:8, :], norm_mix_w[0].rearrange("(a b) -> a b", b=P)).then_inc(s_small, 16)
            act.dma_start(rows[8:16, :], norm_ffn_w[0].rearrange("(a b) -> a b", b=P)).then_inc(s_small, 16)
            act.dma_start(rows[16:48, :], m_conv_w[0].rearrange("j (a b) -> (j a) b", b=P)).then_inc(s_small, 16)
            act.dma_start(rows[48:56, :], m_conv_b[0].rearrange("(a b) -> a b", b=P)).then_inc(s_small, 16)
            act.dma_start(rows[56:60, :], m_head_norm_w[0].rearrange("(a b) -> a b", b=P)).then_inc(s_small, 16)
            for g in range(2):
                act.dma_start(gbias[:, g:g + 1], m_gate_bias[0, g * MH:(g + 1) * MH].rearrange("(h a) -> h a", a=1))\
                   .then_inc(s_small, 16)
            act.dma_start(wgate[:, :, :], w_in2[:, O_MI:O_MI + 2 * MH].rearrange("(k p) n -> p k n", p=P))\
               .then_inc(s_small, 16)
            act.dma_start(wr[:, :, :], w_router[0].rearrange("(k p) n -> p k n", p=P)).then_inc(s_small2, 16)
            act.dma_start(brt[:, :], b_router[0:1, :].broadcast_to([P, E])).then_inc(s_small2, 16)

            def preload(func):
                nc.scalar.activation(warm[:, :], cst[0:1, K_ONES:K_ONES + 1], func).then_inc(warmed, 1)

            def squares(i):
                for t in range(TT):
                    if i:
                        act.wait_ge(resid, 2 * TT * (i - 1) + 2 * (t + 1))
                    nc.scalar.activation(xn[:, t, :], xs[:, t, :], ACT.Square, accum_out=st[:, t:t + 1])\
                      .then_inc(sumsq, 1)

            def norm_root(i):
                act.wait_ge(meansq, i + 1)
                nc.scalar.activation(st[:, 4:6], st[:, 2:4], ACT.Sqrt).then_inc(root, 1)

            def take(name, outs, func=ACT.Copy):
                n = SLICES.index(name)
                act.wait_ge(slots_used, 2 * n + 2)
                for j in range(2):
                    src = B[2 * (n % 2) + j][:, :]
                    dst = outs(j)
                    if len(dst.shape) == 3:
                        src = src.rearrange("p (a b) -> p a b", a=dst.shape[1])
                    nc.scalar.activation(dst, src, func).then_inc(taken[name], 1)

            act.wait_ge(s_x, 16)
            squares(0)
            norm_root(0)
            act.wait_ge(cols_ready, 1)
            for k in (2, 3, 6, 7):
                act.wait_ge(xT_turned, k // 2 + 1)
                nc.scalar.activation(xnT[:, k, :], B[4 + k // 2][:, (k % 2) * S:(k % 2 + 1) * S], ACT.Copy,
                                     scale=wcol(NORM_MIX + k)).then_inc(xT_odd, 1)
            act.wait_ge(grow, 3)
            nc.scalar.activation(gr[:, 3, :], gr[:, 2, :], ACT.Exp, scale=-1.0).then_inc(gexp, 1)
            act.wait_ge(grow, 4)
            nc.scalar.activation(gr[:, 3, :], gr[:, 3, :], ACT.Ln).then_inc(gexp, 1)
            act.wait_ge(pads, 2)
            take("mq", lambda j: pre[:, 2 * j:2 * j + 2, 3:3 + S])
            take("mk", lambda j: pre[:, MH + 2 * j:MH + 2 * j + 2, 3:3 + S])
            for g in range(2):
                act.wait_ge(conv, MH * CONV * (g + 1))
                nc.scalar.activation(sg[:, MH * g:MH * (g + 1), :], mqk[:, MH * g:MH * (g + 1), :], ACT.Sigmoid)\
                  .then_inc(silu_sig, 1)
            take("mv", lambda j: vaug[:, j, :, 0:MDH])
            act.wait_ge(gcols, 1)
            nc.scalar.activation(gcol[:, 1, :, :], B[6][:, 8:16].rearrange("p (t h) -> p t h", t=TT), ACT.Exp)\
              .then_inc(gcols_act, 1)
            act.wait_ge(diag, 1)
            for h in range(MH):
                off = B[4 + h // 2][:, (h % 2) * S + P:(h % 2) * S + 2 * P]
                for b, (src, s0) in enumerate(((dg[:, 2 * h, :], 0), (off, 0), (dg[:, 2 * h + 1, :], 1))):
                    nc.scalar.activation(wm[:, h, b, :], src, ACT.Exp, bias=gcol[:, 0, s0, h:h + 1]).then_inc(wexp, 1)
            take("av", lambda j: av[:, j, :])
            take("mo", lambda j: smo[:, j, :], ACT.Sigmoid)
            act.wait_ge(hnorm, 3)
            nc.scalar.activation(hs[:, 2, :, :], hs[:, 1, :, :], ACT.Sqrt).then_inc(hroot, 1)

            def softmax(h):
                act.wait_ge(nsmax, h + 1)
                if h >= 4:
                    act.wait_ge(p_turned, h - 3)
                for t in range(TT):
                    lo, hi = (0, P) if t == 0 else (P, 3 * P)
                    nc.scalar.activation(ps[:, h % 4, lo:hi], B[4 + h % 4][:, lo:hi], ACT.Exp,
                                         bias=am[:, h, 1, t:t + 1], scale=ADH ** -0.5,
                                         accum_out=am[:, h, 2, t:t + 1]).then_inc(probs, 1)

            for h in range(4):
                softmax(h)
            take("ga0", lambda j: sga[:, j, 0:N], ACT.Sigmoid)
            take("ga1", lambda j: sga[:, j, N:D], ACT.Sigmoid)
            act.wait_ge(rope, 2 * TT)
            act.dma_start(b2, b_mlp2[0]).then_inc(s_small2, 16)
            for h in range(4, AH):
                softmax(h)
            take("gm0", lambda j: sgm[:, j, 0:N], ACT.Sigmoid)
            take("gm1", lambda j: sgm[:, j, N:D], ACT.Sigmoid)
            act.wait_ge(ym, 3)
            act.dma_start(wffn, norm_ffn_w[0:1, :].broadcast_to([P, D])).then_inc(s_wffn, 16)
            act.wait_ge(apv, 4)
            act.dma_start(wfin, norm_final_w.rearrange("(a d) -> a d", a=1).broadcast_to([P, D]))\
               .then_inc(s_small2, 16)
            for t in range(TT):
                for b in range(2):
                    act.wait_ge(mg_turned, 2 * t + b + 1)
                    src = B[4 + 2 * t + b][:, :].rearrange("p (k s) -> p k s", k=4)
                    nc.scalar.activation(mgT[:, 4 * b:4 * b + 4, t * P:(t + 1) * P], src, ACT.Copy)\
                      .then_inc(mgT_ready, 1)
            preload(ACT.Sqrt)
            squares(1)
            norm_root(1)
            for b in (1, 3):
                act.wait_ge(xT_turned, 4 + b + 1)
                nc.scalar.activation(xnT[:, 2 * b:2 * b + 2, :], B[4 + b][:, :].rearrange("p (k s) -> p k s", k=2),
                                     ACT.Copy).then_inc(xT_odd, 1)
            preload(ACT.Exp)
            act.wait_ge(neg_top, 1)
            for t in range(TT):
                nc.scalar.activation(lg[:, t, 2, :], lg[:, t, 0, :], ACT.Exp, bias=mx8[:, t, 8:9]).then_inc(rexp, 1)

            def take_xg(ready):
                act.wait_ge(gath, ready)
                nc.scalar.activation(xg, B[6][:, :], ACT.Copy).then_inc(xg_out, 1)

            take_xg(1)
            items = act.value_load(first_item[0:1, E:E + 1], min_val=1, max_val=ITEMS - 1)
            with act.Fori(0, items) as i:
                act.wait_ge(glu_ready, i + 1)
                nc.scalar.activation(sig, glu, ACT.Sigmoid, scale=ALPHA).then_inc(sig_ready, 1)
                take_xg(i + 2)
                act.wait_ge(turned_b, i + 1)
                nc.scalar.activation(actT[:, 2:4, :], B[4][:, 0:2 * P].rearrange("p (j c) -> p j c", j=2), ACT.Copy)\
                  .then_inc(actT_b, 1)
                act.wait_ge(slots_used, i * PER_EXPERT + (Q_MOE + PER_EXPERT))
                nc.scalar.activation(yw, B[7][:, :], ACT.Copy).then_inc(yw_ready, 1)

            preload(ACT.Sqrt)
            squares(2)
            norm_root(2)
            for t in range(TT):
                act.wait_ge(normed, t + 1)
                act.dma_start(out[0, t * P:(t + 1) * P, :], xn[:, t, :]).then_inc(out_sem, 16)

        @block.tensor
        def _(pe):
            mm = nc.tensor.matmul

            def turn(i):
                pe.wait_ge(xn_ready, TT * (i + 1))
                for k in range(KB):
                    for t in range(TT):
                        last = nc.tensor.transpose(B[4 + k // 2][:, (k % 2) * S + t * P:(k % 2) * S + (t + 1) * P],
                                                   xn[:, t, k * P:(k + 1) * P], ident)
                    if k % 2:
                        last.then_inc(xT_turned, 1)

            def project(n):
                name = SLICES[n]
                w = wslice(n)
                pe.wait_ge(landed[slot_of(2 * n)], 16 * (loads_before(2 * n) + 1))
                if n >= 2:
                    pe.wait_ge(taken[SLICES[n - 2]], 2)
                for j in range(2):
                    bank = B[2 * (n % 2) + j]
                    if n < 2:
                        for f in range(2):
                            for k in range(KB):
                                last = mm(bank[:, f * S:(f + 1) * S], w[:, k, (2 * j + f) * P:(2 * j + f + 1) * P],
                                          xnT[:, k, :], start=(k == 0), stop=(k == KB - 1))
                    else:
                        for k in range(KB):
                            last = mm(bank[:, :], xnT[:, k, j * P:(j + 1) * P], w[:, k, :],
                                      start=(k == 0), stop=(k == KB - 1))
                last.then_inc(slots_used, 2)

            pe.wait_ge(s_cst, 16)
            pe.wait_ge(s_small, 16 * 8)
            nc.tensor.transpose(B[0][:, 0:60], rows[:, :], ident[0:60, 0:60]).then_inc(rows_turned, 1)
            turn(0)
            pe.wait_ge(cols_ready, 1)
            pe.wait_ge(xT_even, 4)
            pe.wait_ge(xT_odd, 4)
            project(0)
            for g in range(2):
                for k in range(KB):
                    last = mm(B[4 + g][0:MH, 0:S], wgate[:, k, g * MH:(g + 1) * MH], xnT[:, k, :],
                              start=(k == 0), stop=(k == KB - 1))
                last.then_inc(gates_done, 1)
            project(1)
            pe.wait_ge(grow, 10)
            for h in range(MH):
                mm(B[4 + h // 2][:, (h % 2) * S:(h % 2 + 1) * S], cst[0:MH, K_SEL + P * h:K_SEL + P * (h + 1)],
                   gr[:, 6, :], start=True, stop=True).then_inc(mbc, 1)
            for g, row in enumerate((5, 7)):
                for t in range(TT):
                    last = nc.tensor.transpose(B[6][:, 8 * g + MH * t:8 * g + MH * (t + 1)],
                                               gr[:, row, t * P:(t + 1) * P], ident[0:MH, 0:MH])
            last.then_inc(mbc, 1)
            project(2)
            project(3)
            pe.wait_ge(silu, 2 * MH)
            for h in range(MH):
                pe.wait_ge(wexp, 3 * MH)
                pe.wait_ge(gcols, 1)
                pe.wait_ge(gcols_act, 1)
                mm(B[4 + h][:, 0:S], mqk[:, MH + h, 0:P], mqk[:, h, :], start=True, stop=True)
                mm(B[4 + h][:, S:S + P], mqk[:, MH + h, P:S], mqk[:, h, P:S], start=True, stop=True)\
                    .then_inc(mqk_done, 1)
            project(4)
            pe.wait_ge(taken["mv"], 2)
            for h in range(MH):
                pe.wait_ge(wqk, h + 1)
                o = B[4 + h]
                mm(o[:, 0:MDH + 1], wm[:, h, 0, :], vaug[:, 0, h, :], start=True, stop=True)
                mm(o[:, S:S + MDH + 1], wm[:, h, 1, :], vaug[:, 0, h, :], start=True, stop=False)
                mm(o[:, S:S + MDH + 1], wm[:, h, 2, :], vaug[:, 1, h, :], start=False, stop=True).then_inc(mpv, 1)
            project(5)
            project(6)
            pe.wait_ge(rope, 2 * TT)
            pe.wait_ge(mh, 2 * MH)
            for b in range(8):
                for t in range(TT):
                    last = nc.tensor.transpose(B[4 + b // 2][:, (b % 2) * S + t * P:(b % 2) * S + (t + 1) * P],
                                               qk[:, b // 4, t, (b % 4) * P:(b % 4 + 1) * P], ident)
                if b % 2 == 1:
                    last.then_inc(qkT_turned, 1)

            def scores(h):
                o, r = B[4 + h % 4], (h % 2) * ADH
                if h >= 4:
                    pe.wait_ge(yaT_ready, 2)
                    pe.wait_ge(pT_ready, 4)
                q, k = qkT[r:r + ADH, h // 2, :], qkT[r:r + ADH, 4 + h // 2, :]
                mm(o[:, 0:P], q[:, 0:P], k[:, 0:P], start=True, stop=True)
                mm(o[:, P:3 * P], q[:, P:S], k[:, :], start=True, stop=True).then_inc(scored, 1)

            def turn_probs(h):
                pe.wait_ge(pnorm, 2 * h + 2)
                for b in range(3):
                    last = nc.tensor.transpose(B[4 + h % 4][:, b * P:(b + 1) * P], ps[:, h % 4, b * P:(b + 1) * P], ident)
                last.then_inc(p_turned, 1)

            def attend(h):
                pe.wait_ge(pT_ready, h + 1)
                o = B[4 + (h - h % 2) % 4][(h % 2) * ADH:(h % 2 + 1) * ADH, :]
                v = av[:, :, h * ADH:(h + 1) * ADH]
                p = pt[:, h % 4, :]
                mm(o[:, 0:P], v[:, 0, :], p[:, 0:P], start=True, stop=True)
                mm(o[:, P:S], v[:, 0, :], p[:, P:2 * P], start=True, stop=False)
                last = mm(o[:, P:S], v[:, 1, :], p[:, 2 * P:3 * P], start=False, stop=True)
                if h % 2:
                    last.then_inc(apv, 1)

            pe.wait_ge(qkT_ready, 4)
            for h in range(4):
                scores(h)
            project(7)
            for h in range(4):
                turn_probs(h)
            project(8)
            pe.wait_ge(taken["av"], 2)
            for h in range(0, 4, 2):
                pe.wait_ge(pT_ready, h + 2)
                attend(h)
                attend(h + 1)
            for h in range(4, AH):
                scores(h)
            project(9)
            for h in range(4, AH):
                turn_probs(h)
            project(10)
            for h in range(4, AH, 2):
                pe.wait_ge(pT_ready, h + 2)
                attend(h)
                attend(h + 1)
            pe.wait_ge(ym, 3)
            for b in range(MH):
                if b % 2 == 0:
                    pe.wait_ge(yaT_ready, 3 + b // 2)
                    pe.wait_ge(pT_ready, AH)
                for t in range(TT):
                    last = nc.tensor.transpose(B[4 + b // 2 * 2 + 1][:, (b % 2) * S + t * P:(b % 2) * S + (t + 1) * P],
                                               hm[:, t, b, :], ident)
                if b % 2:
                    last.then_inc(ym_turned, 1)
            for j in range(4):
                pe.wait_ge(landed[slot_of(Q_BRANCH + j)], 16 * (loads_before(Q_BRANCH + j) + 1))
            for c in range(2 * TT):
                t, n = c // 2, c % 2
                if c < 2:
                    pe.wait_ge(taken[SLICES[9 + c]], 2)
                    pe.wait_ge(yaT_ready, 4)
                else:
                    pe.wait_ge(gated_br, 2 * (c - 1))
                for br, yT in ((0, yaT), (1, ymT)):
                    if br:
                        pe.wait_ge(ymT_ready, MH)
                    for b in range(4):
                        last = mm(B[2 - 2 * (c % 2) + br][:, :], yT[:, b, t * P:(t + 1) * P],
                                  wblock(Q_BRANCH, 4 * br + b)[:, n * N:(n + 1) * N], start=(b == 0), stop=(b == 3))
                if c < 2 * TT - 1:
                    last.then_inc(branched, 1)
                else:
                    last.then_inc(slots_used, 4)
            for t in range(TT):
                for k in range(KB):
                    if k % 4 == 0:
                        pe.wait_ge(merged, 2 * t + k // 4 + 1)
                    last = nc.tensor.transpose(B[4 + 2 * t + k // 4][:, (k % 4) * P:(k % 4 + 1) * P],
                                               mg[:, t, k * P:(k + 1) * P], ident)
                    if k % 4 == 3:
                        last.then_inc(mg_turned, 1)
            pe.wait_ge(gated_br, 4 * TT)
            for j in range(4):
                pe.wait_ge(landed[slot_of(Q_OUT + j)], 16 * (loads_before(Q_OUT + j) + 1))
            for c in range(2 * TT):
                t, n = c // 2, c % 2
                pe.wait_ge(mgT_ready, 2 * (t + 1))
                for k in range(KB):
                    last = mm(B[c][:, :], mgT[:, k, t * P:(t + 1) * P], wblock(Q_OUT, k)[:, n * N:(n + 1) * N],
                              start=(k == 0), stop=(k == KB - 1))
                if c < 2 * TT - 1:
                    last.then_inc(mixed, 1)
                else:
                    last.then_inc(slots_used, 4)
            turn(1)
            pe.wait_ge(s_small2, 16 * 4)
            pe.wait_ge(xT_even, 6)
            pe.wait_ge(xT_odd, 6)
            for t in range(TT):
                for k in range(KB):
                    last = mm(B[4][:, t * E:(t + 1) * E], xnT[:, k, t * P:(t + 1) * P], wr[:, k, :],
                              start=(k == 0), stop=(k == KB - 1))
            last.then_inc(logits_done, 1)
            pe.wait_ge(chosen, 1)
            sel = [lg[:, t, 1, :] for t in range(TT)]
            lower = cst[:, K_LOWER:K_LOWER + P]
            mm(B[5][0:1, 0:E], ones[:, 0:1], sel[0], start=True, stop=False)
            mm(B[5][0:1, 0:E], ones[:, 0:1], sel[1], start=False, stop=True).then_inc(counted, 1)
            mm(B[6][:, 0:E], lower, sel[0], start=True, stop=True)
            mm(B[6][:, E:2 * E], lower, sel[1], start=True, stop=False)
            mm(B[6][:, E:2 * E], ones, sel[0], start=False, stop=True).then_inc(ranked, 1)
            pe.wait_ge(gates_ready, 1)
            for t in range(TT):
                last = nc.tensor.transpose(B[7][0:E, t * P:(t + 1) * P], gate[:, t, 0:E], ident)
            last.then_inc(gate_turned, 1)
            pe.wait_ge(tabled, 1)
            pe.wait_ge(pos_ready, 4)

            def gather(ready):
                pe.wait_ge(onehot, ready)
                for t in range(TT):
                    for g in range(2):
                        last = mm(B[6][g * C:(g + 1) * C, :], oneh[:, t, :], xn[:, t, g * N:(g + 1) * N],
                                  start=(t == 0), stop=(t == TT - 1), skip_group_check=True)
                last.then_inc(gath, 1)

            def turn_rows(ready):
                pe.wait_ge(xg_out, ready)
                for j in range(4):
                    last = nc.tensor.transpose(B[6][:, j * P:(j + 1) * P], xg[:, j * P:(j + 1) * P], ident)
                last.then_inc(xg_turned, 1)

            def scatter():
                for t in range(TT):
                    for g in range(2):
                        for c in range(2):
                            o = c * C
                            last = mm(B[2 * t + g][o:o + C, :], gatedT[g * C:(g + 1) * C, t * P + o:t * P + o + C],
                                      yw[g * C:(g + 1) * C, :], start=False, stop=False, skip_group_check=True)
                last.then_inc(scat, 1)

            gather(2)
            pe.wait_ge(s_small2, 16 * 4)
            pe.wait_ge(gateT_ready, 1)
            for t in range(TT):
                for g in range(2):
                    mm(B[2 * t + g][:, :], gateT[:, t * P:(t + 1) * P], b2[:, g * N:(g + 1) * N],
                       start=True, stop=False, skip_group_check=True)
            turn_rows(1)
            pe.sem_inc(gt_turned, 1)
            items = pe.value_load(first_item[0:1, E:E + 1], min_val=1, max_val=ITEMS - 1)
            with pe.Fori(0, items) as i:
                e = pe.value_load(item_expert[0:1, bass.ds(i, 1)], min_val=0, max_val=E - 1)
                pe.wait_ge(gT_ready, i + 1)
                pe.wait_ge(b1_in, 16 * e + 16)
                for u in range(2):
                    for g in range(2):
                        last = mm(B[4 + u][g * C:(g + 1) * C, :], ones[0:1, 0:C],
                                  b1row[0:1, u * FF + g * N:u * FF + (g + 1) * N], start=True, stop=False,
                                  skip_group_check=True)
                last.then_inc(b1_free, 1)
                pe.wait_ge(xg_ready, i + 1)
                for k in range(KB):
                    q = slot_of(Q_MOE + k)
                    if k == 1:
                        pe.wait_ge(yw_ready, i + 1)
                    pe.wait_ge(landed[q], e * 16 + 16 * (loads_before(Q_MOE + k) + 1))
                    for u in range(2):
                        for g in range(2):
                            last = mm(B[4 + u][g * C:(g + 1) * C, :], xgT[:, k % 4, k // 4, :],
                                      ring[:, q, u * FF + g * N:u * FF + (g + 1) * N],
                                      start=False, stop=(k == KB - 1), skip_group_check=True)
                    last.then_inc(slots_used, 1)
                scatter()
                gather(2 * i + 4)
                pe.wait_ge(act_ready, i + 1)
                for j in range(4):
                    last = nc.tensor.transpose(B[7 if j < 2 else 4][:, (j % 2) * P:(j % 2 + 1) * P],
                                               actv[:, j * P:(j + 1) * P], ident)
                    if j == 1:
                        last.then_inc(turned_a, 1)
                last.then_inc(turned_b, 1)
                for j in range(4):
                    if j == 0:
                        pe.wait_ge(actT_a, i + 1)
                    if j == 2:
                        turn_rows(i + 2)
                        pe.wait_ge(gated_ready, 2 * i + 2)
                        for t in range(TT):
                            last = nc.tensor.transpose(B[5][:, t * P:(t + 1) * P], gated[:, t, :], ident)
                        last.then_inc(gt_turned, 1)
                        pe.wait_ge(actT_b, i + 1)
                    q = slot_of(Q_MOE + KB + j)
                    pe.wait_ge(landed[q], e * 16 + 16 * (loads_before(Q_MOE + KB + j) + 1))
                    for h in range(2):
                        for g in range(2):
                            last = mm(B[7][g * C:(g + 1) * C, :], actT[:, j, h * C:(h + 1) * C],
                                      ring[:, q, h * D + g * N:h * D + (g + 1) * N],
                                      start=(j == 0 and h == 0), stop=(j == 3 and h == 1), skip_group_check=True)
                    last.then_inc(slots_used, 1)
            pe.wait_ge(gT_ready, items + 1)
            pe.wait_ge(yw_ready, items + 1)
            pe.sem_inc(last_rows, 1)
            pe.wait_ge(last_rows, 1)
            scatter()

        @block.vector
        def _(dve):
            v = nc.vector

            def norm(i):
                dve.wait_ge(sumsq, TT * (i + 1))
                v.tensor_scalar(st[:, 2:4], st[:, 0:2], 1.0 / D, EPS, ALU.mult, ALU.add).then_inc(meansq, 1)
                dve.wait_ge(root, i + 1)
                v.reciprocal(st[:, 6:8], st[:, 4:6]).then_inc(rstd, 1)
                dve.wait_ge(rstd, i + 1)

            dve.wait_ge(s_x, 16)
            norm(0)
            for t in range(TT):
                v.tensor_scalar(xn[:, t, :], xs[:, t, :], st[:, 6 + t:7 + t], None, ALU.mult).then_inc(xn_ready, 1)
            dve.wait_ge(rows_turned, 1)
            v.tensor_copy(cols[:, :], B[0][:, 0:60]).then_inc(cols_ready, 1)
            dve.wait_ge(cols_ready, 1)
            for k in (0, 1, 4, 5):
                dve.wait_ge(xT_turned, k // 2 + 1)
                v.tensor_scalar(xnT[:, k, :], B[4 + k // 2][:, (k % 2) * S:(k % 2 + 1) * S], wcol(NORM_MIX + k),
                                None, ALU.mult).then_inc(xT_even, 1)
            dve.wait_ge(gates_done, 2)
            for g in range(2):
                v.tensor_scalar(gr[:, g, :], B[4 + g][0:MH, 0:S], gbias[:, g:g + 1], None, ALU.add).then_inc(grow, 1)
            dve.wait_ge(grow, 2)
            v.scalar_tensor_tensor(out=gr[:, 2, :], in0=gr[:, 1, :], scalar=-1.0, in1=gr[:, 1, :],
                                   op0=ALU.mult, op1=ALU.max).then_inc(grow, 1)
            dve.wait_ge(gexp, 1)
            v.tensor_scalar(gr[:, 3, :], gr[:, 3, :], 1.0, None, ALU.add).then_inc(grow, 1)
            dve.wait_ge(gexp, 2)
            v.scalar_tensor_tensor(out=gr[:, 4, :], in0=gr[:, 1, :], scalar=0.0, in1=gr[:, 3, :],
                                   op0=ALU.min, op1=ALU.subtract).then_inc(grow, 1)
            dve.wait_ge(grow, 5)
            v.tensor_tensor_scan(gr[:, 2, :], gr[:, 4, :], gr[:, 4, :], 0.0, ALU.add, ALU.bypass).then_inc(grow, 1)
            dve.wait_ge(grow, 6)
            v.tensor_tensor(gr[:, 5, :], gr[:, 0, :], gr[:, 2, :], ALU.subtract).then_inc(grow, 1)
            dve.wait_ge(grow, 7)
            v.tensor_tensor_scan(gr[:, 4, :], gr[:, 5, :], gr[:, 5, :], 0.0, ALU.max, ALU.bypass).then_inc(grow, 1)
            dve.wait_ge(grow, 8)
            v.tensor_scalar(gr[:, 6, :], gr[:, 4, :], -1.0, None, ALU.mult).then_inc(grow, 1)
            v.scalar_tensor_tensor(out=gr[:, 7, :], in0=gr[:, 2, :], scalar=-1.0, in1=gr[:, 4, :],
                                   op0=ALU.mult, op1=ALU.subtract).then_inc(grow, 1)

            def convolve(g):
                dve.wait_ge(taken["mk" if g else "mq"], 2)
                for j in range(CONV - 1, -1, -1):
                    for b in range(MH * g, MH * (g + 1)):
                        w = wcol(CONV_W + 2 * MH * j + b)
                        if j == CONV - 1:
                            v.tensor_scalar(mqk[:, b, :], pre[:, b, j:j + S], w, wcol(CONV_B + b), ALU.mult, ALU.add)\
                             .then_inc(conv, 1)
                        else:
                            dve.wait_ge(conv, MH * CONV * g + MH * (CONV - 2 - j) + (b - MH * g) + 1)
                            v.scalar_tensor_tensor(out=mqk[:, b, :], in0=pre[:, b, j:j + S], scalar=w,
                                                   in1=mqk[:, b, :], op0=ALU.mult, op1=ALU.add).then_inc(conv, 1)

            def silu_mul(g):
                dve.wait_ge(silu_sig, g + 1)
                for b in range(MH * g, MH * (g + 1)):
                    v.scalar_tensor_tensor(out=mqk[:, b, :], in0=mqk[:, b, :], scalar=MDH ** -0.5 if g else 1.0,
                                           in1=sg[:, b, :], op0=ALU.mult, op1=ALU.mult).then_inc(silu, 1)

            def rotate(g):
                name = "ak" if g else "aq"
                n = SLICES.index(name)
                dve.wait_ge(slots_used, 2 * n + 2)
                for t in range(TT):
                    src = B[2 * (n % 2) + t][:, :].rearrange("p (h d) -> p h d", h=AH)
                    cos = cst[:, K_COS + ADH * t:K_COS + ADH * (t + 1)].unsqueeze(1).broadcast_to([P, AH, ADH])
                    sin = cst[:, K_SIN + 32 * t:K_SIN + 32 * (t + 1)].unsqueeze(1).broadcast_to([P, AH, 32])
                    a = rt[:, 0, :].rearrange("p (h d) -> p h d", h=AH)
                    b = rt[:, 1, :].rearrange("p (h d) -> p h d", h=AH)
                    o = qk[:, g, t, :].rearrange("p (h d) -> p h d", h=AH)
                    v.tensor_tensor(a, src, cos, ALU.mult).then_inc(rope_step, 1)
                    v.tensor_tensor(b[:, :, 32:64], src[:, :, 0:32], sin, ALU.mult).then_inc(rope_step, 1)
                    v.tensor_tensor(b[:, :, 0:32], src[:, :, 32:64], sin, ALU.mult).then_inc(taken[name], 1)
                    dve.wait_ge(rope_step, 4 * (TT * g + t) + 2)
                    dve.wait_ge(taken[name], t + 1)
                    v.tensor_tensor(o[:, :, 0:32], a[:, :, 0:32], b[:, :, 0:32], ALU.subtract).then_inc(rope_step, 1)
                    v.tensor_tensor(o[:, :, 32:64], a[:, :, 32:64], b[:, :, 32:64], ALU.add).then_inc(rope_step, 1)
                    dve.wait_ge(rope_step, 4 * (TT * g + t) + 4)
                    dve.sem_inc(rope, 1)

            convolve(0)
            silu_mul(0)
            convolve(1)
            silu_mul(1)
            dve.wait_ge(mbc, MH + 1)
            v.tensor_copy(gcol[:, 0, :, :], B[6][:, 0:8].rearrange("p (t h) -> p t h", t=TT)).then_inc(gcols, 1)
            dve.wait_ge(gcols, 1)
            maskT = cst[:, K_MASKT:K_MASKT + P]
            for b in range(2):
                dst = dg[:, 4 * b:4 * b + 4, :]
                src = B[4 + b][:, :].rearrange("p (a s) -> p a s", a=4)
                ins = v.tensor_tensor(dst, src, maskT.unsqueeze(1).broadcast_to([P, 4, P]), ALU.add)
                ins.then_inc(diag_half, 1)
            dve.wait_ge(diag_half, 2)
            dve.sem_inc(diag, 1)
            rotate(0)
            for h in range(MH):
                dve.wait_ge(mqk_done, h + 1)
                dve.wait_ge(wexp, 3 * (h + 1))
                w = wm[:, h, :, :].rearrange("p b s -> p (b s)")
                v.tensor_tensor(w, B[4 + h][:, 0:3 * P], w, ALU.mult).then_inc(wqk, 1)
            rotate(1)
            dve.wait_ge(gcols_act, 1)
            for h in range(MH):
                dve.wait_ge(mpv, h + 1)
                o = B[4 + h][:, :].rearrange("p (t n) -> p t n", t=TT)
                den = o[:, :, MDH]
                v.tensor_scalar(dn[:, h, 2, :], den, -1.0, None, ALU.mult).then_inc(mden, 1)
                dve.wait_ge(mden, 4 * h + 1)
                v.tensor_tensor(dn[:, h, 0, :], den, dn[:, h, 2, :], ALU.max).then_inc(mden, 1)
                dve.wait_ge(mden, 4 * h + 2)
                v.tensor_tensor(dn[:, h, 0, :], dn[:, h, 0, :], gcol[:, 1, :, h], ALU.max).then_inc(mden, 1)
                dve.wait_ge(mden, 4 * h + 3)
                v.reciprocal(dn[:, h, 1, :], dn[:, h, 0, :]).then_inc(mden, 1)
                dve.wait_ge(mden, 4 * h + 4)
                for t in range(TT):
                    v.tensor_scalar(hm[:, t, h, :], o[:, t, 0:MDH], dn[:, h, 1, t:t + 1], None, ALU.mult)\
                     .then_inc(mh, 1)
            dve.wait_ge(mh, 2 * MH)
            hsq = sg[:, 0:4, :].rearrange("p a s -> p (a s)")
            hall = hm[:, :, :, :].rearrange("p t h d -> p (t h d)")
            h8 = hm[:, :, :, :].rearrange("p t h d -> p (t h) d")
            v.tensor_tensor(hsq, hall, hall, ALU.mult).then_inc(hnorm, 1)
            dve.wait_ge(hnorm, 1)
            v.tensor_reduce(hs[:, 0, :, :].rearrange("p t h -> p (t h)"), hsq.rearrange("p (a d) -> p a d", a=8),
                            AX, ALU.add).then_inc(hnorm, 1)
            dve.wait_ge(hnorm, 2)
            v.tensor_scalar(hs[:, 1, :, :], hs[:, 0, :, :], 1.0 / MDH, EPS, ALU.mult, ALU.add).then_inc(hnorm, 1)
            for b in range(4):
                dve.wait_ge(qkT_turned, b + 1)
                v.tensor_copy(qkT[:, 2 * b:2 * b + 2, :], B[4 + b][:, :].rearrange("p (a s) -> p a s", a=2))\
                 .then_inc(qkT_ready, 1)
            dve.wait_ge(hroot, 1)
            v.reciprocal(hs[:, 3, :, :], hs[:, 2, :, :]).then_inc(ym, 1)
            dve.wait_ge(ym, 1)
            v.tensor_tensor(h8, h8, hs[:, 3, :, :].rearrange("p t h -> p (t h)").unsqueeze(2).broadcast_to([P, 8, MDH]),
                            ALU.mult).then_inc(ym, 1)
            dve.wait_ge(ym, 2)
            dve.wait_ge(taken["mo"], 2)
            v.tensor_tensor(hall, hall, smo[:, :, :].rearrange("p t n -> p (t n)"), ALU.mult).then_inc(ym, 1)

            mask = cst[:, K_MASK:K_MASK + P]

            def head_max(h):
                dve.wait_ge(scored, h + 1)
                o = B[4 + h % 4]
                for t in range(TT):
                    d = o[:, 2 * P * t:2 * P * t + P]
                    v.tensor_tensor(d, d, mask, ALU.add).then_inc(masked, 1)
                dve.wait_ge(masked, 2 * h + 2)
                for t in range(TT):
                    lo, hi = (0, P) if t == 0 else (P, 3 * P)
                    v.tensor_reduce(am[:, h, 0, t:t + 1], o[:, lo:hi], AX, ALU.max).then_inc(smax, 1)
                dve.wait_ge(smax, 2 * h + 2)
                v.tensor_scalar(am[:, h, 1, :], am[:, h, 0, :], -ADH ** -0.5, None, ALU.mult).then_inc(nsmax, 1)

            def head_norm(h):
                dve.wait_ge(probs, 2 * h + 2)
                v.reciprocal(am[:, h, 3, :], am[:, h, 2, :]).then_inc(psum_r, 1)
                dve.wait_ge(psum_r, h + 1)
                for t in range(TT):
                    lo, hi = (0, P) if t == 0 else (P, 3 * P)
                    v.tensor_scalar(ps[:, h % 4, lo:hi], ps[:, h % 4, lo:hi], am[:, h, 3, t:t + 1], None, ALU.mult)\
                     .then_inc(pnorm, 1)

            def take_pT(h):
                dve.wait_ge(p_turned, h + 1)
                if h >= 4:
                    dve.wait_ge(apv, 2)
                v.tensor_copy(pt[:, h % 4, :], B[4 + h % 4][:, 0:3 * P]).then_inc(pT_ready, 1)

            def take_yaT(j):
                dve.wait_ge(apv, j + 1)
                v.tensor_copy(yaT[:, j, :], B[4 + 2 * (j % 2)][:, 0:S]).then_inc(yaT_ready, 1)

            for g in range(2):
                for h in range(4 * g, 4 * g + 4):
                    head_max(h)
                for h in range(4 * g, 4 * g + 4):
                    head_norm(h)
                for h in range(4 * g, 4 * g + 4):
                    take_pT(h)
                for j in range(2 * g, 2 * g + 2):
                    take_yaT(j)
            for b in range(MH):
                dve.wait_ge(ym_turned, b // 2 + 1)
                v.tensor_scalar(ymT[:, b, :], B[4 + b // 2 * 2 + 1][:, (b % 2) * S:(b % 2 + 1) * S], wcol(HEAD_W + b),
                                None, ALU.mult).then_inc(ymT_ready, 1)
            dve.wait_ge(taken["gm1"], 2)
            for c in range(2 * TT):
                t, n = c // 2, c % 2
                if c < 2 * TT - 1:
                    dve.wait_ge(branched, c + 1)
                else:
                    dve.wait_ge(slots_used, Q_OUT)
                cut = slice(n * N, (n + 1) * N)
                v.tensor_tensor(sga[:, t, cut], B[2 - 2 * (c % 2)][:, :], sga[:, t, cut], ALU.mult).then_inc(gated_br, 1)
                v.tensor_tensor(sgm[:, t, cut], B[2 - 2 * (c % 2) + 1][:, :], sgm[:, t, cut], ALU.mult).then_inc(gated_br, 1)
                dve.wait_ge(gated_br, 2 * c + 2)
                v.tensor_tensor(mg[:, t, cut], sga[:, t, cut], sgm[:, t, cut], ALU.add).then_inc(merged, 1)
            for c in range(2 * TT):
                t, n = c // 2, c % 2
                cut = slice(n * N, (n + 1) * N)
                if c < 2 * TT - 1:
                    dve.wait_ge(mixed, c + 1)
                else:
                    dve.wait_ge(slots_used, Q_MOE)
                v.tensor_tensor(xs[:, t, cut], B[c][:, :], xs[:, t, cut], ALU.add).then_inc(resid, 1)
            norm(1)
            dve.wait_ge(s_wffn, 16)
            for t in range(TT):
                v.scalar_tensor_tensor(out=xn[:, t, :], in0=xs[:, t, :], scalar=st[:, 6 + t:7 + t], in1=wffn,
                                       op0=ALU.mult, op1=ALU.mult).then_inc(xn_ready, 1)
            for b in (0, 2):
                dve.wait_ge(xT_turned, 4 + b + 1)
                v.tensor_copy(xnT[:, 2 * b:2 * b + 2, :], B[4 + b][:, :].rearrange("p (k s) -> p k s", k=2))\
                 .then_inc(xT_even, 1)
            dve.wait_ge(s_small2, 16 * 4)
            dve.wait_ge(logits_done, 1)
            v.tensor_tensor(lg[:, :, 0, :], B[4][:, 0:TT * E].rearrange("p (t e) -> p t e", t=TT),
                            brt[:, :].unsqueeze(1).broadcast_to([P, TT, E]), ALU.add).then_inc(router_step, 1)
            dve.wait_ge(router_step, 1)
            for t in range(TT):
                v.max(out=mx8[:, t, 0:8], in_=lg[:, t, 0, :]).then_inc(router_step, 1)
            dve.wait_ge(router_step, 3)
            v.memset(mx8[:, :, TOPK:8], 3.0e38).then_inc(router_step, 1)
            v.tensor_scalar(mx8[:, :, 8:9], mx8[:, :, 0:1], -1.0, None, ALU.mult).then_inc(neg_top, 1)
            dve.wait_ge(router_step, 4)
            for t in range(TT):
                v.match_replace(out=lg[:, t, 3, :], in_to_replace=mx8[:, t, 0:8], in_values=lg[:, t, 0, :],
                                imm_value=-3.0e38).then_inc(router_step, 1)
            dve.wait_ge(router_step, 6)
            v.tensor_tensor(lg[:, :, 1, :], lg[:, :, 0, :], lg[:, :, 3, :], ALU.not_equal).then_inc(chosen, 1)
            dve.wait_ge(chosen, 1)
            dve.wait_ge(rexp, 2)
            v.tensor_tensor(lg[:, :, 4, :], lg[:, :, 2, :], lg[:, :, 1, :], ALU.mult).then_inc(router, 1)
            dve.wait_ge(router, 1)
            v.tensor_reduce(mx8[:, :, 9:10].rearrange("p t a -> p (t a)"), lg[:, :, 4, :], AX, ALU.add).then_inc(router, 1)
            dve.wait_ge(router, 2)
            v.reciprocal(mx8[:, :, 10:11], mx8[:, :, 9:10]).then_inc(router, 1)
            dve.wait_ge(router, 3)
            v.tensor_tensor(gate[:, :, 0:E], lg[:, :, 4, :], mx8[:, :, 10:11].broadcast_to([P, TT, E]), ALU.mult)\
             .then_inc(gates_ready, 1)
            dve.wait_ge(counted, 1)
            v.tensor_scalar(cnt[:, 0, :], B[5][0:1, 0:E], C + 0.5, 1.0, ALU.is_gt, ALU.add).then_inc(count_step, 1)
            v.tensor_scalar(cnt[:, 1, :], B[5][0:1, 0:E], 2 * C + 0.5, None, ALU.is_gt).then_inc(count_step, 1)
            v.tensor_scalar(cnt[:, 2, :], B[5][0:1, 0:E], 3 * C + 0.5, None, ALU.is_gt).then_inc(count_step, 1)
            dve.wait_ge(count_step, 3)
            v.tensor_tensor(cnt[:, 0, :], cnt[:, 0, :], cnt[:, 1, :], ALU.add).then_inc(count_step, 1)
            dve.wait_ge(count_step, 4)
            v.tensor_tensor(cnt[:, 0, :], cnt[:, 0, :], cnt[:, 2, :], ALU.add).then_inc(count_step, 1)
            dve.wait_ge(count_step, 5)
            v.tensor_tensor_scan(cnt[:, 3, :], cnt[:, 0, :], cnt[:, 0, :], 0.0, ALU.add, ALU.bypass).then_inc(count_step, 1)
            v.memset(first_item[:, 0:1], 0).then_inc(count_step, 1)
            dve.wait_ge(count_step, 7)
            v.tensor_copy(first_item[:, 1:E + 1], cnt[:, 3, :]).then_inc(count_step, 1)
            v.tensor_scalar(first_item[:, E + 1:E + 2], cnt[:, 3, E - 1:E], 1.0, None, ALU.add).then_inc(count_step, 1)
            spread = moe2[0:1, 0:ITEMS * E].rearrange("p (i e) -> p i e", e=E)
            v.tensor_tensor(spread, cnt[:, 3, :].unsqueeze(1).broadcast_to([1, ITEMS, E]),
                            cst[0:1, K_IOTA:K_IOTA + ITEMS].unsqueeze(2).broadcast_to([1, ITEMS, E]), ALU.is_le)\
             .then_inc(count_step, 1)
            dve.wait_ge(count_step, 10)
            v.tensor_reduce(item_sum[:, 0:ITEMS], spread, AX, ALU.add).then_inc(count_step, 1)
            dve.wait_ge(count_step, 11)
            v.tensor_copy(item_expert[:, 0:ITEMS], item_sum[:, 0:ITEMS]).then_inc(tabled, 1)
            dve.wait_ge(ranked, 1)
            for t in range(TT):
                v.scalar_tensor_tensor(out=pos[:, t, 0:E], in0=B[6][:, t * E:(t + 1) * E], scalar=1.0,
                                       in1=lg[:, t, 1, :], op0=ALU.add, op1=ALU.mult).then_inc(pos_step, 1)
            dve.wait_ge(pos_step, 2)
            v.tensor_scalar(pos[:, :, 0:E], pos[:, :, 0:E], -1.0, None, ALU.add).then_inc(pos_ready, 1)
            v.memset(pos[:, :, E:E + 1], -1.0).then_inc(pos_ready, 1)
            v.memset(gate[:, :, E:E + 1], 0.0).then_inc(pos_ready, 1)
            dve.wait_ge(gate_turned, 1)
            v.tensor_copy(gateT[:, :], B[7][0:E, 0:S]).then_inc(gateT_ready, 1)
            dve.wait_ge(pos_ready, 3)
            dve.wait_ge(gateT_ready, 1)
            dve.sem_inc(pos_ready, 1)
            dve.wait_ge(tabled, 1)
            v.memset(gatedT, 0.0).then_inc(gT_ready, 1)
            v.memset(yw, 0.0).then_inc(yw_ready, 1)

            def place(e, i):
                after = dve.value_load(first_item[0:1, bass.ds(e + 1, 1)], min_val=1, max_val=ITEMS)
                r = nc.s_assert_within(after - 1 - i, 0, NR - 1, skip_runtime_bounds_check_because=
                                       "an expert has 1 to NR tiles, by the sum that made the table")
                return cst[:, bass.ds(r * C + K_IOTA, C)], [pos[:, t, bass.ds(e, 1)] for t in range(TT)]

            def one_hots(e, i):
                places, at = place(e, i)
                for t in range(TT):
                    v.tensor_scalar(oneh[:, t, :], places, at[t], None, ALU.is_equal).then_inc(onehot, 1)

            def take_xgT(ready):
                dve.wait_ge(xg_turned, ready)
                v.tensor_copy(xgT, B[6][:, :].rearrange("p (j g s) -> p j g s", j=4, g=2)).then_inc(xg_ready, 1)

            one_hots(dve.value_load(item_expert[0:1, 0:1], min_val=0, max_val=E), 0)
            take_xgT(1)
            items = dve.value_load(first_item[0:1, E:E + 1], min_val=1, max_val=ITEMS - 1)
            with dve.Fori(0, items) as i:
                e = dve.value_load(item_expert[0:1, bass.ds(i, 1)], min_val=0, max_val=E)
                places, at = place(e, i)
                dve.wait_ge(gt_turned, i + 1)
                for t in range(TT):
                    v.tensor_scalar(gated[:, t, :].rearrange("p (g s) -> p g s", g=2),
                                    places.unsqueeze(1).broadcast_to([P, 2, C]), at[t],
                                    gate[:, t, bass.ds(e, 1)], ALU.is_equal, ALU.mult).then_inc(gated_ready, 1)
                dve.wait_ge(gath, i + 1)
                one_hots(dve.value_load(item_expert[0:1, bass.ds(i + 1, 1)], min_val=0, max_val=E), i + 1)
                dve.wait_ge(slots_used, i * PER_EXPERT + (Q_MOE + KB))
                v.tensor_scalar(glu, B[4][:, :], LIMIT, None, ALU.min).then_inc(glu_ready, 1)
                v.tensor_scalar(lin, B[5][:, :], LIMIT, -LIMIT, ALU.min, ALU.max).then_inc(lin_ready, 1)
                dve.wait_ge(glu_ready, i + 1)
                dve.wait_ge(lin_ready, i + 1)
                v.scalar_tensor_tensor(out=lin, in0=lin, scalar=1.0, in1=glu, op0=ALU.add, op1=ALU.mult)\
                 .then_inc(glin, 1)
                dve.wait_ge(glin, i + 1)
                dve.wait_ge(sig_ready, i + 1)
                v.tensor_tensor(actv, lin, sig, ALU.mult).then_inc(act_ready, 1)
                dve.wait_ge(turned_a, i + 1)
                v.tensor_copy(actT[:, 0:2, :], B[7][:, 0:2 * P].rearrange("p (j c) -> p j c", j=2)).then_inc(actT_a, 1)
                take_xgT(i + 2)
                dve.wait_ge(gt_turned, i + 2)
                v.tensor_copy(gatedT, B[5][:, 0:S]).then_inc(gT_ready, 1)
            dve.wait_ge(scat, items + 1)
            for c in range(2 * TT):
                t, n = c // 2, c % 2
                cut = slice(n * N, (n + 1) * N)
                v.tensor_tensor(xs[:, t, cut], B[c][:, :], xs[:, t, cut], ALU.add).then_inc(resid, 1)
            norm(2)
            for t in range(TT):
                v.scalar_tensor_tensor(out=xn[:, t, :], in0=xs[:, t, :], scalar=st[:, 6 + t:7 + t], in1=wfin,
                                       op0=ALU.mult, op1=ALU.mult).then_inc(normed, 1)


_INS = ["x", "norm_mix_w", "w_in", "m_conv_w", "m_conv_b", "m_gate_bias", "m_head_norm_w", "w_branch", "w_out",
        "norm_ffn_w", "w_router", "b_router", "w_mlp1", "b_mlp1", "w_mlp2", "b_mlp2", "norm_final_w"]


def kernel(**inputs):
    import concourse.bacc as _bacc
    from concourse.bass_utils import run_bass_kernel_spmd as _run

    nc = _bacc.Bacc("TRN2", target_bir_lowering=False, num_devices=1)
    arrays, args = {}, []
    for name in _INS:
        a = np.ascontiguousarray(inputs[name])
        arrays[f"in_{name}_dram"] = a
        args.append(nc.dram_tensor(f"in_{name}_dram", a.shape, mybir.dt.from_np(a.dtype), kind="ExternalInput").ap())
    table = constants()
    arrays["table_dram"] = table
    args.append(nc.dram_tensor("table_dram", table.shape, F32, kind="ExternalInput").ap())
    args.append(nc.dram_tensor("out_dram", (1, S, D), F32, kind="ExternalOutput").ap())
    build(nc, *args)
    r = _run(nc, [arrays], core_ids=[0])
    return r.results[0]["out_dram"]
```

```python
from contextlib import ExitStack

import numpy as np

import concourse.bass as bass
from concourse import mybir

F32 = mybir.dt.float32
F32R = mybir.dt.float32r
I32 = mybir.dt.int32
ALU = mybir.AluOpType
ACT = mybir.ActivationFunctionType
AX = mybir.AxisListType.X

P = 128
S = 256
TT = S // P
D = 1024
KB = D // P
AH, ADH = 8, 64
MH, MDH = 4, 128
AW = AH * ADH
MW = MH * MDH
CONV = 4
E = 32
TOPK = 4
FF = 1024
C = 64
NR = S // C
LIMIT = 7.0
ALPHA = 1.702
EPS = 1e-6
NEG = -1e30
N = 512

O_MI = 3 * AW + 4 * MW
O_G = O_MI + 2 * MH
SLICES = ["mq", "mk", "mv", "aq", "ak", "av", "mo", "ga0", "ga1", "gm0", "gm1"]
COL = {"aq": 0, "ak": AW, "av": 2 * AW, "mq": 3 * AW, "mk": 3 * AW + MW, "mv": 3 * AW + 2 * MW,
       "mo": 3 * AW + 3 * MW, "ga0": O_G, "ga1": O_G + N, "gm0": O_G + 2 * N, "gm1": O_G + 3 * N}

SLOT = 2 * FF
RING = 12
HALF = SLOT // N
Q_BRANCH = 2 * len(SLICES)
Q_OUT = Q_BRANCH + 4
Q_MOE = Q_OUT + 4
ITEMS = E + S * TOPK // C
PER_EXPERT = 12
assert RING == PER_EXPERT
MIX_RING = 7
SLOTS = [q % MIX_RING for q in range(Q_MOE - 1)] + [MIX_RING]
SLOTS += list(range(MIX_RING + 1, RING)) + SLOTS[Q_BRANCH:Q_MOE]
assert sorted(SLOTS[Q_MOE:]) == list(range(RING))

K_ID, K_COS, K_SIN = 0, 128, 256
K_MASK, K_MASKT, K_LOWER, K_ONES = 320, 448, 576, 704
K_IOTA, K_SEL, K_END = 832, 1088, 1600


def constants():
    c = np.zeros((P, K_END), np.float32)
    p = np.arange(P)
    c[:, K_ID:K_ID + P] = np.eye(P)
    inv = np.float32(10000.0) ** (-np.arange(0, ADH, 2, dtype=np.float32) / np.float32(ADH))
    for t in range(TT):
        ang = (p + P * t).astype(np.float32)[:, None] * inv[None, :].astype(np.float32)
        c[:, K_COS + ADH * t:K_COS + ADH * (t + 1)] = np.tile(np.cos(ang), 2)
        c[:, K_SIN + 32 * t:K_SIN + 32 * (t + 1)] = np.sin(ang)
    c[:, K_MASK:K_MASK + P] = np.where(p[None, :] <= p[:, None], 0.0, NEG)
    c[:, K_MASKT:K_MASKT + P] = np.where(p[:, None] <= p[None, :], 0.0, NEG)
    c[:, K_LOWER:K_LOWER + P] = p[:, None] < p[None, :]
    c[:, K_ONES:K_ONES + P] = 1.0
    c[:, K_IOTA:K_IOTA + S] = np.arange(S)
    for h in range(MH):
        c[h, K_SEL + P * h:K_SEL + P * (h + 1)] = 1.0
    return c


def slot_of(q):
    return SLOTS[q]


def build(nc, x, norm_mix_w, w_in, m_conv_w, m_conv_b, m_gate_bias, m_head_norm_w, w_branch, w_out,
          norm_ffn_w, w_router, b_router, w_mlp1, b_mlp1, w_mlp2, b_mlp2, norm_final_w, table, out):
    with ExitStack() as ctx:
        def sb(name, shape, dt=F32):
            return ctx.enter_context(nc.sbuf_tensor(name, shape, dt))

        def sem(name):
            return ctx.enter_context(nc.semaphore(name))

        base = -(-nc.sbuf_base // 32) * 32
        ring = sb("ring", [P, RING, SLOT])
        cst = sb("cst", [P, K_END])
        xs = sb("xs", [P, TT, D])
        xn = sb("xn", [P, TT, D])
        xhi_at = -(-nc.sbuf_base // 32) * 32
        xnT = sb("xnT", [P, KB, S])
        xhi = nc.alloc_sbuf_tensor_at("xhi", [P, KB, S], F32R, offset=xhi_at)
        xlo = nc.alloc_sbuf_tensor_at("xlo", [P, KB, S], F32R, offset=base + 4 * SLOT * MIX_RING)
        whi = nc.alloc_sbuf_tensor_at("whi", [P, 2, HALF, N], F32R, offset=base + 4 * SLOT * (MIX_RING + 1))
        wlo = nc.alloc_sbuf_tensor_at("wlo", [P, 2, HALF, N], F32R, offset=base + 4 * SLOT * (MIX_RING + 3))
        rows = sb("rows", [60, P])
        cols = sb("cols", [P, 60])
        gbias = sb("gbias", [MH, 2])
        wgate = sb("wgate", [P, KB, 2 * MH])
        wr = sb("wr", [P, KB, E])
        brt = sb("brt", [P, E])
        st = sb("st", [P, 16])
        pre = sb("pre", [P, 2 * MH, S + 3])
        mqk = sb("mqk", [P, 2 * MH, S])
        warm = sb("warm", [1, 1])
        gr = sb("gr", [MH, 8, S])
        gcol = sb("gcol", [P, 2, TT, MH])
        wm = sb("wm", [P, MH, 3, P])
        vaug = sb("vaug", [P, TT, MH, MDH + 1])
        av = sb("av", [P, TT, AW])
        smo = sb("smo", [P, TT, MW])
        sga = sb("sga", [P, TT, D])
        sgm = sb("sgm", [P, TT, D])
        hm = sb("hm", [P, TT, MH, MDH])
        dn = sb("dn", [P, MH, 3, TT])
        hs = sb("hs", [P, 4, TT, MH])
        qk = sb("qk", [P, 2, TT, AW])
        rt = sb("rt", [P, 2, AW])
        am = sb("am", [P, AH, 4, TT])
        qkT = xn[:, :, :].rearrange("p a (b s) -> p (a b) s", s=S)
        sg = sga[:, :, :].rearrange("p t (a s) -> p (t a) s", s=S)
        dg = smo[:, :, :].rearrange("p t (a s) -> p (t a) s", s=P)
        ps = wm[:, :, :, :].rearrange("p h b s -> p h (b s)")
        pt = mqk[:, :, :].rearrange("p a s -> p (a s)")[:, 0:4 * 3 * P].rearrange("p (a s) -> p a s", a=4)
        wffn = smo[:, :, :].rearrange("p t n -> p (t n)")
        wfin = av[:, :, :].rearrange("p t n -> p (t n)")
        xT32 = sgm[:, :, :].rearrange("p a (b s) -> p (a b) s", s=S)
        lgT = rt[:, 0, 0:S]
        b1row = pre[0:1, :, :].rearrange("p a s -> p (a s)")[:, 0:2 * FF]
        yaT = pre[:, 0:4, 0:S]
        ymT = pre[:, 4:8, 0:S]
        mg = qk[:, :, :, :].rearrange("p a t n -> p (a t n)").rearrange("p (t n) -> p t n", t=TT)
        mgT = xnT
        lg = sb("lg", [P, TT, 6, E])
        mx8 = sb("mx8", [P, TT, 16])
        pos = sb("pos", [P, TT, E + 1])
        gate = sb("gate", [P, TT, E + 1])
        cnt = sb("cnt", [1, 5, E])
        first_item = sb("first_item", [1, E + 2], I32)
        item_expert = sb("item_expert", [1, ITEMS + 1], I32)
        item_sum = sb("item_sum", [1, ITEMS + 1])
        moe = sga[:, :, :].rearrange("p t n -> p (t n)")
        moe2 = sgm[:, :, :].rearrange("p t n -> p (t n)")
        xgT = moe[:, 0:N].rearrange("p (j g s) -> p j g s", j=4, g=2)
        xg = moe2[:, 3 * N:4 * N]
        glu = moe[:, N:2 * N]
        lin = moe[:, 2 * N:3 * N]
        actv = moe[:, 3 * N:4 * N]
        sig = moe2[:, 0:N]
        actT = moe2[:, N:2 * N].rearrange("p (j c) -> p j c", j=4)
        yw = moe2[:, 2 * N:3 * N]
        oneh = hm[:, :, 0, 0:C]
        gated = hm[:, :, 1, :]
        gatedT = smo[:, 0, 0:S]

        B = [ctx.enter_context(nc.psum_tensor(f"bank{i}", [P, N], F32)) for i in range(8)]

        s_wffn = sem("norm_ffn_w_in")
        s_x, s_cst, s_small, s_small2 = sem("x_in"), sem("constants_in"), sem("small_in"), sem("late_small_in")
        landed = [sem(f"slot{i}_landed") for i in range(RING)]
        slots_used = sem("slots_used")
        hi_ready, hi_used, lo_ready = sem("w_hi_ready"), sem("w_hi_used"), sem("w_lo_ready")
        xh_even, xh_odd, xl_even, xl_odd = sem("x_hi_even"), sem("x_hi_odd"), sem("x_lo_even"), sem("x_lo_odd")
        sumsq, meansq, root, rstd = sem("sumsq"), sem("meansq"), sem("root"), sem("rstd")
        xn_ready = sem("xn_ready")
        rows_turned, cols_ready = sem("rows_turned"), sem("cols_ready")
        xT_turned, xT_even, xT_odd = sem("xT_turned"), sem("xT_even"), sem("xT_odd")
        gates_done, grow, gexp = sem("gates_done"), sem("gate_rows"), sem("gate_exp")
        pads = sem("pads")
        taken = {n: sem(f"taken_{n}") for n in SLICES}
        conv, silu_sig, silu = sem("conv"), sem("silu_sigmoid"), sem("silu")
        mbc, gcols, gcols_act, diag, wexp = sem("m_broadcast"), sem("gate_cols"), sem("gate_cols_exp"), sem("diag"), sem("w_exp")
        mqk_done, wqk, mpv, mden, mh = sem("m_qk"), sem("w_times_qk"), sem("m_pv"), sem("m_den"), sem("m_h")
        hnorm, hroot, ym = sem("head_norm"), sem("head_root"), sem("y_m")
        rope = sem("rope")
        qkT_turned, qkT_ready = sem("qkT_turned"), sem("qkT_ready")
        scored, masked, smax, nsmax = sem("scored"), sem("masked"), sem("score_max"), sem("neg_max")
        probs, psum_r, pnorm = sem("probs"), sem("prob_recip"), sem("prob_normed")
        p_turned, pT_ready, apv, yaT_ready = sem("p_turned"), sem("pT_ready"), sem("a_pv"), sem("yaT_ready")
        ym_turned, ymT_ready = sem("ym_turned"), sem("ymT_ready")
        branched, gated_br, merged = sem("branched"), sem("gated_branch"), sem("merged")
        mg_turned, mgT_ready, mixed, resid = sem("merged_turned"), sem("mergedT_ready"), sem("mixed"), sem("resid")
        logits_done, router = sem("logits_done"), sem("router")
        rexp = sem("router_exp")
        opened, gated_zero, yw_zero, b2_in, lgT_ready = (sem("opened"), sem("gated_zero"), sem("y_zero"), sem("b_mlp2_in"),
                                                        sem("logitsT_ready"))
        firsts = sem("first_items")
        ranked, pos_ready, counted, tabled = sem("ranked"), sem("pos_ready"), sem("counted"), sem("tabled")
        b1_in, b1_free = sem("b1_in"), sem("b1_free")
        onehot, gath, xg_out, xg_turned, xg_ready = (sem("onehot"), sem("gathered"), sem("xg_out"), sem("xg_turned"),
                                                      sem("xg_ready"))
        gated_ready, gt_turned, gT_ready = sem("gated_ready"), sem("gates_turned"), sem("gatedT_ready")
        glu_ready, lin_ready, sig_ready, act_ready = sem("glu_ready"), sem("lin_ready"), sem("sigmoid_ready"), sem("act_ready")
        turned_a, turned_b, actT_a, actT_b = sem("act_turned_a"), sem("act_turned_b"), sem("actT_a_ready"), sem("actT_b_ready")
        yw_ready, scat, normed = sem("y_ready"), sem("scattered"), sem("normed")
        rope_step, diag_half, router_step = sem("rope_step"), sem("diag_half"), sem("router_step")
        count_step, pos_step, glin = sem("count_step"), sem("pos_step"), sem("glu_times_lin")
        last_rows = sem("last_rows")
        logit_sum = sem("logit_sum")
        warmed, neg_top, chosen, gates_ready = sem("warmed"), sem("neg_top"), sem("chosen"), sem("gates_ready")
        out_sem = sem("out_stored")

        ident = cst[:, K_ID:K_ID + P]
        ones = cst[:, K_ONES:K_ONES + P]

        def wcol(i):
            return cols[:, i:i + 1]

        NORM_MIX, NORM_FFN, CONV_W, CONV_B, HEAD_W = 0, 8, 16, 48, 56

        def loads_before(q):
            return SLOTS[:q].count(SLOTS[q])

        def raw(u):
            return ring[:, slot_of(u), :].rearrange("p (k n) -> p k n", n=N)

        def wblock(q0, b):
            return ring[:, slot_of(q0 + b // 2), (b % 2) * D:(b % 2 + 1) * D]

        w_in2, w_branch2, w_out2 = w_in[0], w_branch[0], w_out[0]
        block = ctx.enter_context(nc.Block())

        @block.sync
        def _(sp):
            sp.dma_start(xs[:, :, :], x[0].rearrange("(t p) d -> p t d", p=P)).then_inc(s_x, 16)
            sp.dma_start(cst[:, :], table[:, :]).then_inc(s_cst, 16)
            for u in range(Q_BRANCH):
                if u == 2:
                    sp.wait_ge(s_small, 16 * 8)
                if u >= MIX_RING:
                    sp.wait_ge(lo_ready, u - MIX_RING + 1)
                c, k0 = COL[SLICES[u // 2]], (u % 2) * HALF * P
                src = w_in2[k0:k0 + HALF * P, c:c + N].rearrange("(k p) n -> p k n", p=P)
                sp.dma_start(raw(u), src).then_inc(landed[slot_of(u)], 16)
            for q0, w in ((Q_BRANCH, w_branch2), (Q_OUT, w_out2)):
                for j in range(4):
                    if slot_of(q0 + j) == MIX_RING:
                        sp.wait_ge(slots_used, Q_BRANCH)
                    else:
                        sp.wait_ge(lo_ready, q0 + j - MIX_RING + 1)
                    dst = ring[:, slot_of(q0 + j), :].rearrange("p (b n) -> p b n", b=2)
                    src = w[2 * P * j:2 * P * (j + 1), :].rearrange("(b p) n -> p b n", p=P)
                    sp.dma_start(dst, src).then_inc(landed[slot_of(q0 + j)], 16)

            def expert(e, freed):
                for k in range(KB):
                    sp.wait_ge(slots_used, freed(k))
                    sp.dma_start(ring[:, slot_of(Q_MOE + k), :], w_mlp1[0, e, k * P:(k + 1) * P, :])\
                      .then_inc(landed[slot_of(Q_MOE + k)], 16)
                for j in range(4):
                    k = KB + j
                    sp.wait_ge(slots_used, freed(k))
                    dst = ring[:, slot_of(Q_MOE + k), :].rearrange("p (h n) -> p h n", h=2)
                    src = w_mlp2[0, e].rearrange("(h j p) n -> j p h n", h=2, j=4)[j]
                    sp.dma_start(dst, src).then_inc(landed[slot_of(Q_MOE + k)], 16)

            expert(0, lambda k: (Q_BRANCH, Q_OUT, Q_MOE)[k // 4])
            sp.wait_ge(tabled, 1)
            with sp.Fori(1, E) as e:
                before = sp.value_load(first_item[0:1, bass.ds(e, 1)], min_val=1, max_val=ITEMS - 1)
                expert(e, lambda k: before * PER_EXPERT + (Q_MOE - PER_EXPERT + k + 1))
            sp.wait_ge(out_sem, 16 * TT)

        @block.gpsimd
        def _(pool):
            pool.memset(pre[:, :, 0:3], 0.0).then_inc(pads, 1)
            pool.memset(vaug[:, :, :, MDH:MDH + 1], 1.0).then_inc(pads, 1)
            for b in range(2):
                k = slice(4 * b + 2, 4 * b + 4)
                pool.wait_ge(xh_odd, 2 * b + 2)
                pool.wait_ge(xT_odd, 2 * b + 2)
                nc.gpsimd.tensor_tensor(xlo[:, k, :], xT32[:, k, :], xhi[:, k, :].bitcast(F32), ALU.subtract)\
                  .then_inc(xl_odd, 1)
            for u in range(Q_BRANCH):
                pool.wait_ge(hi_ready, u + 1)
                if u >= 2:
                    pool.wait_ge(slots_used, u - 1)
                nc.gpsimd.tensor_tensor(wlo[:, u % 2], raw(u), whi[:, u % 2].bitcast(F32), ALU.subtract)\
                  .then_inc(lo_ready, 1)
            pool.wait_ge(merged, 2 * TT)
            pool.memset(yw, 0.0).then_inc(yw_zero, 1)
            pool.wait_ge(yw_zero, 1)
            for g in range(2):
                pool.dma_start(yw[g * C:g * C + E, :], b_mlp2[0, :, g * N:(g + 1) * N]).then_inc(b2_in, 16)
            pool.wait_ge(slots_used, Q_OUT)
            pool.dma_start(b1row, b_mlp1[0, 0:1, :]).then_inc(b1_in, 16)
            pool.wait_ge(tabled, 1)
            with pool.Fori(1, E) as e:
                before = pool.value_load(first_item[0:1, bass.ds(e, 1)], min_val=1, max_val=ITEMS - 1)
                pool.wait_ge(b1_free, before)
                pool.dma_start(b1row, b_mlp1[0, bass.ds(e, 1), :]).then_inc(b1_in, 16)

        @block.scalar
        def _(act):
            act.dma_start(rows[0:8, :], norm_mix_w[0].rearrange("(a b) -> a b", b=P)).then_inc(s_small, 16)
            act.dma_start(rows[8:16, :], norm_ffn_w[0].rearrange("(a b) -> a b", b=P)).then_inc(s_small, 16)
            act.dma_start(rows[16:48, :], m_conv_w[0].rearrange("j (a b) -> (j a) b", b=P)).then_inc(s_small, 16)
            act.dma_start(rows[48:56, :], m_conv_b[0].rearrange("(a b) -> a b", b=P)).then_inc(s_small, 16)
            act.dma_start(rows[56:60, :], m_head_norm_w[0].rearrange("(a b) -> a b", b=P)).then_inc(s_small, 16)
            for g in range(2):
                act.dma_start(gbias[:, g:g + 1], m_gate_bias[0, g * MH:(g + 1) * MH].rearrange("(h a) -> h a", a=1))\
                   .then_inc(s_small, 16)
            act.dma_start(wgate[:, :, :], w_in2[:, O_MI:O_MI + 2 * MH].rearrange("(k p) n -> p k n", p=P))\
               .then_inc(s_small, 16)
            act.dma_start(wr[:, :, :], w_router[0].rearrange("(k p) n -> p k n", p=P)).then_inc(s_small2, 16)
            act.dma_start(brt[:, :], b_router[0:1, :].broadcast_to([P, E])).then_inc(s_small2, 16)

            def preload(func):
                nc.scalar.activation(warm[:, :], cst[0:1, K_ONES:K_ONES + 1], func).then_inc(warmed, 1)

            def norm_root(i):
                for t in range(TT):
                    if i:
                        act.wait_ge(resid, 2 * TT * (i - 1) + 2 * (t + 1))
                    nc.scalar.activation(xn[:, t, :], xs[:, t, :], ACT.Square, accum_out=st[:, t:t + 1])\
                      .then_inc(sumsq, 1)
                    act.wait_ge(meansq, TT * i + t + 1)
                    nc.scalar.activation(st[:, 4 + t:5 + t], st[:, 2 + t:3 + t], ACT.Sqrt).then_inc(root, 1)

            def take(name, outs, func=ACT.Copy):
                n = SLICES.index(name)
                act.wait_ge(slots_used, 2 * n + 2)
                for j in range(2):
                    src = B[2 * (n % 2) + j][:, :]
                    dst = outs(j)
                    if len(dst.shape) == 3:
                        src = src.rearrange("p (a b) -> p a b", a=dst.shape[1])
                    nc.scalar.activation(dst, src, func).then_inc(taken[name], 1)

            def split(*units):
                for u in units:
                    act.wait_ge(landed[slot_of(u)], 16 * (loads_before(u) + 1))
                    if u >= 2:
                        act.wait_ge(hi_used, u - 1)
                        act.wait_ge(lo_ready, u - 1)
                    nc.scalar.activation(whi[:, u % 2], raw(u), ACT.Copy).then_inc(hi_ready, 1)

            act.wait_ge(s_x, 16)
            norm_root(0)
            split(0)
            act.wait_ge(cols_ready, 1)
            for k in (2, 3, 6, 7):
                act.wait_ge(xT_turned, k // 2 + 1)
                src = B[4 + k // 2][:, (k % 2) * S:(k % 2 + 1) * S]
                nc.scalar.activation(xhi[:, k, :], src, ACT.Copy, scale=wcol(NORM_MIX + k)).then_inc(xh_odd, 1)
                nc.scalar.activation(xT32[:, k, :], src, ACT.Copy, scale=wcol(NORM_MIX + k)).then_inc(xT_odd, 1)
            split(1, 2, 3)
            act.wait_ge(grow, 3)
            nc.scalar.activation(gr[:, 3, :], gr[:, 2, :], ACT.Exp, scale=-1.0).then_inc(gexp, 1)
            act.wait_ge(grow, 4)
            nc.scalar.activation(gr[:, 3, :], gr[:, 3, :], ACT.Ln).then_inc(gexp, 1)
            act.wait_ge(pads, 2)
            take("mq", lambda j: pre[:, 2 * j:2 * j + 2, 3:3 + S])
            split(4, 5)
            take("mk", lambda j: pre[:, MH + 2 * j:MH + 2 * j + 2, 3:3 + S])
            for g in range(2):
                if g:
                    split(6)
                act.wait_ge(conv, MH * CONV * (g + 1))
                nc.scalar.activation(sg[:, MH * g:MH * (g + 1), :], mqk[:, MH * g:MH * (g + 1), :], ACT.Sigmoid)\
                  .then_inc(silu_sig, 1)
            split(7)
            take("mv", lambda j: vaug[:, j, :, 0:MDH])
            act.wait_ge(gcols, 1)
            nc.scalar.activation(gcol[:, 1, :, :], B[6][:, 8:16].rearrange("p (t h) -> p t h", t=TT), ACT.Exp)\
              .then_inc(gcols_act, 1)
            act.wait_ge(diag, 1)
            for h in range(MH):
                off = B[4 + h // 2][:, (h % 2) * S + P:(h % 2) * S + 2 * P]
                for b, (src, s0) in enumerate(((dg[:, 2 * h, :], 0), (off, 0), (dg[:, 2 * h + 1, :], 1))):
                    nc.scalar.activation(wm[:, h, b, :], src, ACT.Exp, bias=gcol[:, 0, s0, h:h + 1]).then_inc(wexp, 1)
            split(8, 9, 10, 11, 12, 13)
            take("av", lambda j: av[:, j, :])
            split(14, 15)
            take("mo", lambda j: smo[:, j, :], ACT.Sigmoid)
            act.wait_ge(hnorm, 3)
            nc.scalar.activation(hs[:, 2, :, :], hs[:, 1, :, :], ACT.Sqrt).then_inc(hroot, 1)

            def softmax(h):
                act.wait_ge(nsmax, h + 1)
                if h >= 4:
                    act.wait_ge(p_turned, h - 3)
                for t in range(TT):
                    lo, hi = (0, P) if t == 0 else (P, 3 * P)
                    nc.scalar.activation(ps[:, h % 4, lo:hi], B[4 + h % 4][:, lo:hi], ACT.Exp,
                                         bias=am[:, h, 1, t:t + 1], scale=ADH ** -0.5,
                                         accum_out=am[:, h, 2, t:t + 1]).then_inc(probs, 1)

            for h in range(4):
                softmax(h)
                if h == 1:
                    split(16)
            split(17)
            take("ga0", lambda j: sga[:, j, 0:N], ACT.Sigmoid)
            split(18, 19)
            take("ga1", lambda j: sga[:, j, N:D], ACT.Sigmoid)
            for h in range(4, AH):
                softmax(h)
                if h == 5:
                    split(20)
            split(21)
            take("gm0", lambda j: sgm[:, j, 0:N], ACT.Sigmoid)
            take("gm1", lambda j: sgm[:, j, N:D], ACT.Sigmoid)
            act.wait_ge(ym, 3)
            act.dma_start(wffn, norm_ffn_w[0:1, :].broadcast_to([P, D])).then_inc(s_wffn, 16)
            act.wait_ge(apv, 4)
            act.dma_start(wfin, norm_final_w.rearrange("(a d) -> a d", a=1).broadcast_to([P, D]))\
               .then_inc(s_small2, 16)
            for t in range(TT):
                for b in range(2):
                    act.wait_ge(mg_turned, 2 * t + b + 1)
                    src = B[4 + 2 * t + b][:, :].rearrange("p (k s) -> p k s", k=4)
                    nc.scalar.activation(mgT[:, 4 * b:4 * b + 4, t * P:(t + 1) * P], src, ACT.Copy)\
                      .then_inc(mgT_ready, 1)
            preload(ACT.Sqrt)
            norm_root(1)
            for t in range(TT):
                act.wait_ge(xT_turned, 4 + 2 * t + 2)
                nc.scalar.activation(xnT[:, 4:8, t * P:(t + 1) * P],
                                     B[5 + 2 * t][:, :].rearrange("p (k s) -> p k s", k=4), ACT.Copy).then_inc(xT_odd, 1)
            preload(ACT.Exp)
            act.wait_ge(neg_top, 1)
            for t in range(TT):
                nc.scalar.activation(lg[:, t, 2, :], lg[:, t, 0, :], ACT.Exp, bias=mx8[:, t, 8:9]).then_inc(rexp, 1)

            def take_xg(ready):
                act.wait_ge(gath, ready)
                nc.scalar.activation(xg, B[6][:, :], ACT.Copy).then_inc(xg_out, 1)

            take_xg(1)
            items = act.value_load(first_item[0:1, E:E + 1], min_val=1, max_val=ITEMS - 1)
            with act.Fori(0, items) as i:
                act.wait_ge(glu_ready, i + 1)
                nc.scalar.activation(sig, glu, ACT.Sigmoid, scale=ALPHA).then_inc(sig_ready, 1)
                take_xg(i + 2)
                act.wait_ge(turned_b, i + 1)
                nc.scalar.activation(actT[:, 2:4, :], B[4][:, 0:2 * P].rearrange("p (j c) -> p j c", j=2), ACT.Copy)\
                  .then_inc(actT_b, 1)
                act.wait_ge(slots_used, i * PER_EXPERT + (Q_MOE + PER_EXPERT))
                nc.scalar.activation(yw, B[7][:, :], ACT.Copy).then_inc(yw_ready, 1)

            preload(ACT.Sqrt)
            norm_root(2)
            for t in range(TT):
                act.wait_ge(normed, t + 1)
                act.dma_start(out[0, t * P:(t + 1) * P, :], xn[:, t, :]).then_inc(out_sem, 16)

        @block.tensor
        def _(pe):
            mm = nc.tensor.matmul

            def turn():
                pe.wait_ge(xn_ready, TT)
                for k in range(KB):
                    for t in range(TT):
                        last = nc.tensor.transpose(B[4 + k // 2][:, (k % 2) * S + t * P:(k % 2) * S + (t + 1) * P],
                                                   xn[:, t, k * P:(k + 1) * P], ident)
                    if k % 2:
                        last.then_inc(xT_turned, 1)

            def turn_tile(t):
                pe.wait_ge(xn_ready, TT + t + 1)
                for k in range(KB):
                    last = nc.tensor.transpose(B[4 + 2 * t + k // 4][:, (k % 4) * P:(k % 4 + 1) * P],
                                               xn[:, t, k * P:(k + 1) * P], ident)
                    if k % 4 == 3:
                        last.then_inc(xT_turned, 1)

            def project(n):
                if n >= 2:
                    pe.wait_ge(taken[SLICES[n - 2]], 2)
                for u in (2 * n, 2 * n + 1):
                    for part, (w, x) in enumerate(((whi, xhi), (whi, xlo), (wlo, xhi))):
                        if part == 0:
                            pe.wait_ge(hi_ready, u + 1)
                        if part == 2:
                            pe.wait_ge(lo_ready, u + 1)
                        if u < 2:
                            pe.wait_ge((xh_even, xl_even, xh_even)[part], (2, 1, 2)[part] * (u + 1))
                            pe.wait_ge((xh_odd, xl_odd, xh_odd)[part], (2, 1, 2)[part] * (u + 1))
                        for j in range(2):
                            bank = B[2 * (n % 2) + j]
                            first, end = part == 0 and u % 2 == 0, part == 2 and u % 2 == 1
                            if n < 2:
                                for f in range(2):
                                    for k in range(HALF):
                                        last = mm(bank[:, f * S:(f + 1) * S],
                                                  w[:, u % 2, k, (2 * j + f) * P:(2 * j + f + 1) * P],
                                                  x[:, (u % 2) * HALF + k, :], start=(first and f == 0 and k == 0),
                                                  stop=(end and k == HALF - 1), skip_group_check=True)
                            else:
                                for k in range(HALF):
                                    last = mm(bank[:, :], x[:, (u % 2) * HALF + k, j * P:(j + 1) * P],
                                              w[:, u % 2, k, :], start=(first and k == 0),
                                              stop=(end and k == HALF - 1))
                        if part == 1:
                            last.then_inc(hi_used, 1)
                    last.then_inc(slots_used, 1)

            pe.wait_ge(s_cst, 16)
            pe.wait_ge(s_small, 16 * 8)
            nc.tensor.transpose(B[0][:, 0:60], rows[:, :], ident[0:60, 0:60]).then_inc(rows_turned, 1)
            turn()
            pe.wait_ge(cols_ready, 1)
            project(0)
            pe.wait_ge(xT_even, 4)
            pe.wait_ge(xT_odd, 4)
            for g in range(2):
                for k in range(KB):
                    last = mm(B[4 + g][0:MH, 0:S], wgate[:, k, g * MH:(g + 1) * MH], xT32[:, k, :],
                              start=(k == 0), stop=(k == KB - 1))
                last.then_inc(gates_done, 1)
            project(1)
            pe.wait_ge(grow, 10)
            for h in range(MH):
                mm(B[4 + h // 2][:, (h % 2) * S:(h % 2 + 1) * S], cst[0:MH, K_SEL + P * h:K_SEL + P * (h + 1)],
                   gr[:, 6, :], start=True, stop=True).then_inc(mbc, 1)
            for g, row in enumerate((5, 7)):
                for t in range(TT):
                    last = nc.tensor.transpose(B[6][:, 8 * g + MH * t:8 * g + MH * (t + 1)],
                                               gr[:, row, t * P:(t + 1) * P], ident[0:MH, 0:MH])
            last.then_inc(mbc, 1)
            project(2)
            project(3)
            pe.wait_ge(silu, 2 * MH)
            for h in range(MH):
                pe.wait_ge(wexp, 3 * MH)
                pe.wait_ge(gcols, 1)
                pe.wait_ge(gcols_act, 1)
                mm(B[4 + h][:, 0:S], mqk[:, MH + h, 0:P], mqk[:, h, :], start=True, stop=True)
                mm(B[4 + h][:, S:S + P], mqk[:, MH + h, P:S], mqk[:, h, P:S], start=True, stop=True)\
                    .then_inc(mqk_done, 1)
            project(4)
            pe.wait_ge(taken["mv"], 2)
            for h in range(MH):
                pe.wait_ge(wqk, h + 1)
                o = B[4 + h]
                mm(o[:, 0:MDH + 1], wm[:, h, 0, :], vaug[:, 0, h, :], start=True, stop=True)
                mm(o[:, S:S + MDH + 1], wm[:, h, 1, :], vaug[:, 0, h, :], start=True, stop=False)
                mm(o[:, S:S + MDH + 1], wm[:, h, 2, :], vaug[:, 1, h, :], start=False, stop=True).then_inc(mpv, 1)
            project(5)
            project(6)
            pe.wait_ge(rope, 2 * TT)
            pe.wait_ge(mh, 2 * MH)
            for b in range(8):
                for t in range(TT):
                    last = nc.tensor.transpose(B[4 + b // 2][:, (b % 2) * S + t * P:(b % 2) * S + (t + 1) * P],
                                               qk[:, b // 4, t, (b % 4) * P:(b % 4 + 1) * P], ident)
                if b % 2 == 1:
                    last.then_inc(qkT_turned, 1)

            def scores(h):
                o, r = B[4 + h % 4], (h % 2) * ADH
                if h >= 4:
                    pe.wait_ge(yaT_ready, 2)
                    pe.wait_ge(pT_ready, 4)
                q, k = qkT[r:r + ADH, h // 2, :], qkT[r:r + ADH, 4 + h // 2, :]
                mm(o[:, 0:P], q[:, 0:P], k[:, 0:P], start=True, stop=True)
                mm(o[:, P:3 * P], q[:, P:S], k[:, :], start=True, stop=True).then_inc(scored, 1)

            def turn_probs(h):
                pe.wait_ge(pnorm, 2 * h + 2)
                for b in range(3):
                    last = nc.tensor.transpose(B[4 + h % 4][:, b * P:(b + 1) * P], ps[:, h % 4, b * P:(b + 1) * P], ident)
                last.then_inc(p_turned, 1)

            def attend(h):
                pe.wait_ge(pT_ready, h + 1)
                o = B[4 + (h - h % 2) % 4][(h % 2) * ADH:(h % 2 + 1) * ADH, :]
                v = av[:, :, h * ADH:(h + 1) * ADH]
                p = pt[:, h % 4, :]
                mm(o[:, 0:P], v[:, 0, :], p[:, 0:P], start=True, stop=True)
                mm(o[:, P:S], v[:, 0, :], p[:, P:2 * P], start=True, stop=False)
                last = mm(o[:, P:S], v[:, 1, :], p[:, 2 * P:3 * P], start=False, stop=True)
                if h % 2:
                    last.then_inc(apv, 1)

            pe.wait_ge(qkT_ready, 4)
            for h in range(4):
                scores(h)
            project(7)
            for h in range(4):
                turn_probs(h)
            project(8)
            pe.wait_ge(taken["av"], 2)
            for h in range(0, 4, 2):
                pe.wait_ge(pT_ready, h + 2)
                attend(h)
                attend(h + 1)
            for h in range(4, AH):
                scores(h)
            project(9)
            for h in range(4, AH):
                turn_probs(h)
            project(10)
            for h in range(4, AH, 2):
                pe.wait_ge(pT_ready, h + 2)
                attend(h)
                attend(h + 1)
            pe.wait_ge(ym, 3)
            for b in range(MH):
                if b % 2 == 0:
                    pe.wait_ge(yaT_ready, 3 + b // 2)
                    pe.wait_ge(pT_ready, AH)
                for t in range(TT):
                    last = nc.tensor.transpose(B[4 + b // 2 * 2 + 1][:, (b % 2) * S + t * P:(b % 2) * S + (t + 1) * P],
                                               hm[:, t, b, :], ident)
                if b % 2:
                    last.then_inc(ym_turned, 1)
            for j in range(4):
                pe.wait_ge(landed[slot_of(Q_BRANCH + j)], 16 * (loads_before(Q_BRANCH + j) + 1))
            for c in range(2 * TT):
                t, n = c // 2, c % 2
                if c < 2:
                    pe.wait_ge(taken[SLICES[9 + c]], 2)
                    pe.wait_ge(yaT_ready, 4)
                else:
                    pe.wait_ge(gated_br, 2 * (c - 1))
                for br, yT in ((0, yaT), (1, ymT)):
                    if br:
                        pe.wait_ge(ymT_ready, MH)
                    for b in range(4):
                        last = mm(B[2 - 2 * (c % 2) + br][:, :], yT[:, b, t * P:(t + 1) * P],
                                  wblock(Q_BRANCH, 4 * br + b)[:, n * N:(n + 1) * N], start=(b == 0), stop=(b == 3))
                if c < 2 * TT - 1:
                    last.then_inc(branched, 1)
                else:
                    last.then_inc(slots_used, 4)
            for t in range(TT):
                for k in range(KB):
                    if k % 4 == 0:
                        pe.wait_ge(merged, 2 * t + k // 4 + 1)
                    last = nc.tensor.transpose(B[4 + 2 * t + k // 4][:, (k % 4) * P:(k % 4 + 1) * P],
                                               mg[:, t, k * P:(k + 1) * P], ident)
                    if k % 4 == 3:
                        last.then_inc(mg_turned, 1)
            pe.wait_ge(gated_br, 4 * TT)
            for j in range(4):
                pe.wait_ge(landed[slot_of(Q_OUT + j)], 16 * (loads_before(Q_OUT + j) + 1))
            for c in range(2 * TT):
                t, n = c // 2, c % 2
                pe.wait_ge(mgT_ready, 2 * (t + 1))
                if c == 2 * TT - 1:
                    pe.wait_ge(mgT_ready, 4)
                    turn_tile(0)
                for k in range(KB):
                    last = mm(B[c][:, :], mgT[:, k, t * P:(t + 1) * P], wblock(Q_OUT, k)[:, n * N:(n + 1) * N],
                              start=(k == 0), stop=(k == KB - 1))
                if c < 2 * TT - 1:
                    last.then_inc(mixed, 1)
                else:
                    last.then_inc(slots_used, 4)
            turn_tile(1)
            pe.wait_ge(s_small2, 16 * 2)
            pe.wait_ge(xT_even, 6)
            pe.wait_ge(xT_odd, 6)
            for a in range(2):
                for j in range(4):
                    last = mm(B[4][j * E:(j + 1) * E, 0:S], wr[:, 2 * j + a, :], xnT[:, 2 * j + a, :],
                              start=(a == 0), stop=(a == 1), skip_group_check=True)
            last.then_inc(logits_done, 1)
            pe.wait_ge(lgT_ready, 1)
            for t in range(TT):
                last = nc.tensor.transpose(B[5][:, t * P:(t + 1) * P], lgT[:, t * P:(t + 1) * P], ident)
            last.then_inc(logits_done, 1)
            pe.wait_ge(chosen, 1)
            sel = [lg[:, t, 1, :] for t in range(TT)]
            lower = cst[:, K_LOWER:K_LOWER + P]
            mm(B[4][0:1, 0:E], ones[:, 0:1], sel[0], start=True, stop=False)
            mm(B[4][0:1, 0:E], ones[:, 0:1], sel[1], start=False, stop=True).then_inc(counted, 1)
            mm(B[6][:, 0:E], lower, sel[0], start=True, stop=True)
            mm(B[6][:, E:2 * E], lower, sel[1], start=True, stop=False)
            mm(B[6][:, E:2 * E], ones, sel[0], start=False, stop=True).then_inc(ranked, 1)
            def gather(ready):
                pe.wait_ge(onehot, ready)
                for t in range(TT):
                    for g in range(2):
                        last = mm(B[6][g * C:(g + 1) * C, :], oneh[:, t, :], xn[:, t, g * N:(g + 1) * N],
                                  start=(t == 0), stop=(t == TT - 1), skip_group_check=True)
                last.then_inc(gath, 1)

            def turn_gates(ready):
                pe.wait_ge(gated_ready, ready)
                for t in range(TT):
                    last = nc.tensor.transpose(B[5][:, t * P:(t + 1) * P], gated[:, t, :], ident)
                last.then_inc(gt_turned, 1)

            def turn_rows(ready):
                pe.wait_ge(xg_out, ready)
                for j in range(4):
                    last = nc.tensor.transpose(B[6][:, j * P:(j + 1) * P], xg[:, j * P:(j + 1) * P], ident)
                last.then_inc(xg_turned, 1)

            def scatter():
                for t in range(TT):
                    for g in range(2):
                        for c in range(2):
                            o = c * C
                            last = mm(B[2 * t + g][o:o + C, :], gatedT[g * C:(g + 1) * C, t * P + o:t * P + o + C],
                                      yw[g * C:(g + 1) * C, :], start=False, stop=False, skip_group_check=True)
                last.then_inc(scat, 1)

            pe.wait_ge(pos_ready, 1)
            gather(2)
            turn_rows(1)
            turn_gates(2)
            pe.wait_ge(b2_in, 32)
            pe.sem_inc(yw_ready, 1)
            pe.wait_ge(opened, 2 * TT)
            pe.wait_ge(tabled, 1)
            items = pe.value_load(first_item[0:1, E:E + 1], min_val=1, max_val=ITEMS - 1)
            with pe.Fori(0, items) as i:
                e = pe.value_load(item_expert[0:1, bass.ds(i, 1)], min_val=0, max_val=E - 1)
                pe.wait_ge(gT_ready, i + 1)
                pe.wait_ge(b1_in, 16 * e + 16)
                for u in range(2):
                    for g in range(2):
                        last = mm(B[4 + u][g * C:(g + 1) * C, :], ones[0:1, 0:C],
                                  b1row[0:1, u * FF + g * N:u * FF + (g + 1) * N], start=True, stop=False,
                                  skip_group_check=True)
                last.then_inc(b1_free, 1)
                pe.wait_ge(xg_ready, i + 1)
                for k in range(KB):
                    q = slot_of(Q_MOE + k)
                    if k == 1:
                        pe.wait_ge(yw_ready, i + 1)
                    pe.wait_ge(landed[q], e * 16 + 16 * (loads_before(Q_MOE + k) + 1))
                    for u in range(2):
                        for g in range(2):
                            last = mm(B[4 + u][g * C:(g + 1) * C, :], xgT[:, k % 4, k // 4, :],
                                      ring[:, q, u * FF + g * N:u * FF + (g + 1) * N],
                                      start=False, stop=(k == KB - 1), skip_group_check=True)
                    last.then_inc(slots_used, 1)
                scatter()
                gather(2 * i + 4)
                pe.wait_ge(act_ready, i + 1)
                for j in range(4):
                    last = nc.tensor.transpose(B[7 if j < 2 else 4][:, (j % 2) * P:(j % 2 + 1) * P],
                                               actv[:, j * P:(j + 1) * P], ident)
                    if j == 1:
                        last.then_inc(turned_a, 1)
                last.then_inc(turned_b, 1)
                for j in range(4):
                    if j == 0:
                        pe.wait_ge(actT_a, i + 1)
                    if j == 2:
                        turn_rows(i + 2)
                        turn_gates(2 * i + 4)
                        pe.wait_ge(actT_b, i + 1)
                    q = slot_of(Q_MOE + KB + j)
                    pe.wait_ge(landed[q], e * 16 + 16 * (loads_before(Q_MOE + KB + j) + 1))
                    for h in range(2):
                        for g in range(2):
                            last = mm(B[7][g * C:(g + 1) * C, :], actT[:, j, h * C:(h + 1) * C],
                                      ring[:, q, h * D + g * N:h * D + (g + 1) * N],
                                      start=(j == 0 and h == 0), stop=(j == 3 and h == 1), skip_group_check=True)
                    last.then_inc(slots_used, 1)
            pe.wait_ge(gT_ready, items + 1)
            pe.wait_ge(yw_ready, items + 1)
            pe.sem_inc(last_rows, 1)
            pe.wait_ge(last_rows, 1)
            scatter()

        @block.vector
        def _(dve):
            v = nc.vector

            def norm(i, t):
                n = TT * i + t + 1
                dve.wait_ge(sumsq, n)
                v.tensor_scalar(st[:, 2 + t:3 + t], st[:, t:t + 1], 1.0 / D, EPS, ALU.mult, ALU.add).then_inc(meansq, 1)
                dve.wait_ge(root, n)
                v.reciprocal(st[:, 6 + t:7 + t], st[:, 4 + t:5 + t]).then_inc(rstd, 1)
                dve.wait_ge(rstd, n)

            dve.wait_ge(s_x, 16)
            for t in range(TT):
                norm(0, t)
                v.tensor_scalar(xn[:, t, :], xs[:, t, :], st[:, 6 + t:7 + t], None, ALU.mult).then_inc(xn_ready, 1)
            dve.wait_ge(rows_turned, 1)
            v.tensor_copy(cols[:, :], B[0][:, 0:60]).then_inc(cols_ready, 1)
            dve.wait_ge(cols_ready, 1)
            for k in (0, 1, 4, 5):
                dve.wait_ge(xT_turned, k // 2 + 1)
                src = B[4 + k // 2][:, (k % 2) * S:(k % 2 + 1) * S]
                v.tensor_scalar(xhi[:, k, :], src, wcol(NORM_MIX + k), None, ALU.mult).then_inc(xh_even, 1)
                v.tensor_scalar(xT32[:, k, :], src, wcol(NORM_MIX + k), None, ALU.mult).then_inc(xT_even, 1)
                if k % 2:
                    pair = slice(k - 1, k + 1)
                    dve.wait_ge(xh_even, k // 4 * 2 + 2)
                    dve.wait_ge(xT_even, k // 4 * 2 + 2)
                    v.tensor_tensor(xlo[:, pair, :], xT32[:, pair, :], xhi[:, pair, :].bitcast(F32), ALU.subtract)\
                     .then_inc(xl_even, 1)
            dve.wait_ge(gates_done, 2)
            for g in range(2):
                v.tensor_scalar(gr[:, g, :], B[4 + g][0:MH, 0:S], gbias[:, g:g + 1], None, ALU.add).then_inc(grow, 1)
            dve.wait_ge(grow, 2)
            v.scalar_tensor_tensor(out=gr[:, 2, :], in0=gr[:, 1, :], scalar=-1.0, in1=gr[:, 1, :],
                                   op0=ALU.mult, op1=ALU.max).then_inc(grow, 1)
            dve.wait_ge(gexp, 1)
            v.tensor_scalar(gr[:, 3, :], gr[:, 3, :], 1.0, None, ALU.add).then_inc(grow, 1)
            dve.wait_ge(gexp, 2)
            v.scalar_tensor_tensor(out=gr[:, 4, :], in0=gr[:, 1, :], scalar=0.0, in1=gr[:, 3, :],
                                   op0=ALU.min, op1=ALU.subtract).then_inc(grow, 1)
            dve.wait_ge(grow, 5)
            v.tensor_tensor_scan(gr[:, 2, :], gr[:, 4, :], gr[:, 4, :], 0.0, ALU.add, ALU.bypass).then_inc(grow, 1)
            dve.wait_ge(grow, 6)
            v.tensor_tensor(gr[:, 5, :], gr[:, 0, :], gr[:, 2, :], ALU.subtract).then_inc(grow, 1)
            dve.wait_ge(grow, 7)
            v.tensor_tensor_scan(gr[:, 4, :], gr[:, 5, :], gr[:, 5, :], 0.0, ALU.max, ALU.bypass).then_inc(grow, 1)
            dve.wait_ge(grow, 8)
            v.tensor_scalar(gr[:, 6, :], gr[:, 4, :], -1.0, None, ALU.mult).then_inc(grow, 1)
            v.scalar_tensor_tensor(out=gr[:, 7, :], in0=gr[:, 2, :], scalar=-1.0, in1=gr[:, 4, :],
                                   op0=ALU.mult, op1=ALU.subtract).then_inc(grow, 1)

            def convolve(g):
                dve.wait_ge(taken["mk" if g else "mq"], 2)
                for j in range(CONV - 1, -1, -1):
                    for b in range(MH * g, MH * (g + 1)):
                        w = wcol(CONV_W + 2 * MH * j + b)
                        if j == CONV - 1:
                            v.tensor_scalar(mqk[:, b, :], pre[:, b, j:j + S], w, wcol(CONV_B + b), ALU.mult, ALU.add)\
                             .then_inc(conv, 1)
                        else:
                            dve.wait_ge(conv, MH * CONV * g + MH * (CONV - 2 - j) + (b - MH * g) + 1)
                            v.scalar_tensor_tensor(out=mqk[:, b, :], in0=pre[:, b, j:j + S], scalar=w,
                                                   in1=mqk[:, b, :], op0=ALU.mult, op1=ALU.add).then_inc(conv, 1)

            def silu_mul(g):
                dve.wait_ge(silu_sig, g + 1)
                for b in range(MH * g, MH * (g + 1)):
                    v.scalar_tensor_tensor(out=mqk[:, b, :], in0=mqk[:, b, :], scalar=MDH ** -0.5 if g else 1.0,
                                           in1=sg[:, b, :], op0=ALU.mult, op1=ALU.mult).then_inc(silu, 1)

            def rotate(g):
                name = "ak" if g else "aq"
                n = SLICES.index(name)
                dve.wait_ge(slots_used, 2 * n + 2)
                for t in range(TT):
                    src = B[2 * (n % 2) + t][:, :].rearrange("p (h d) -> p h d", h=AH)
                    cos = cst[:, K_COS + ADH * t:K_COS + ADH * (t + 1)].unsqueeze(1).broadcast_to([P, AH, ADH])
                    sin = cst[:, K_SIN + 32 * t:K_SIN + 32 * (t + 1)].unsqueeze(1).broadcast_to([P, AH, 32])
                    a = rt[:, 0, :].rearrange("p (h d) -> p h d", h=AH)
                    b = rt[:, 1, :].rearrange("p (h d) -> p h d", h=AH)
                    o = qk[:, g, t, :].rearrange("p (h d) -> p h d", h=AH)
                    v.tensor_tensor(a, src, cos, ALU.mult).then_inc(rope_step, 1)
                    v.tensor_tensor(b[:, :, 32:64], src[:, :, 0:32], sin, ALU.mult).then_inc(rope_step, 1)
                    v.tensor_tensor(b[:, :, 0:32], src[:, :, 32:64], sin, ALU.mult).then_inc(taken[name], 1)
                    dve.wait_ge(rope_step, 4 * (TT * g + t) + 2)
                    dve.wait_ge(taken[name], t + 1)
                    v.tensor_tensor(o[:, :, 0:32], a[:, :, 0:32], b[:, :, 0:32], ALU.subtract).then_inc(rope_step, 1)
                    v.tensor_tensor(o[:, :, 32:64], a[:, :, 32:64], b[:, :, 32:64], ALU.add).then_inc(rope_step, 1)
                    dve.wait_ge(rope_step, 4 * (TT * g + t) + 4)
                    dve.sem_inc(rope, 1)

            convolve(0)
            silu_mul(0)
            convolve(1)
            silu_mul(1)
            dve.wait_ge(mbc, MH + 1)
            v.tensor_copy(gcol[:, 0, :, :], B[6][:, 0:8].rearrange("p (t h) -> p t h", t=TT)).then_inc(gcols, 1)
            dve.wait_ge(gcols, 1)
            maskT = cst[:, K_MASKT:K_MASKT + P]
            for b in range(2):
                dst = dg[:, 4 * b:4 * b + 4, :]
                src = B[4 + b][:, :].rearrange("p (a s) -> p a s", a=4)
                ins = v.tensor_tensor(dst, src, maskT.unsqueeze(1).broadcast_to([P, 4, P]), ALU.add)
                ins.then_inc(diag_half, 1)
            dve.wait_ge(diag_half, 2)
            dve.sem_inc(diag, 1)
            rotate(0)
            for h in range(MH):
                dve.wait_ge(mqk_done, h + 1)
                dve.wait_ge(wexp, 3 * (h + 1))
                w = wm[:, h, :, :].rearrange("p b s -> p (b s)")
                v.tensor_tensor(w, B[4 + h][:, 0:3 * P], w, ALU.mult).then_inc(wqk, 1)
            rotate(1)
            dve.wait_ge(gcols_act, 1)
            for h in range(MH):
                dve.wait_ge(mpv, h + 1)
                o = B[4 + h][:, :].rearrange("p (t n) -> p t n", t=TT)
                den = o[:, :, MDH]
                v.tensor_scalar(dn[:, h, 2, :], den, -1.0, None, ALU.mult).then_inc(mden, 1)
                dve.wait_ge(mden, 4 * h + 1)
                v.tensor_tensor(dn[:, h, 0, :], den, dn[:, h, 2, :], ALU.max).then_inc(mden, 1)
                dve.wait_ge(mden, 4 * h + 2)
                v.tensor_tensor(dn[:, h, 0, :], dn[:, h, 0, :], gcol[:, 1, :, h], ALU.max).then_inc(mden, 1)
                dve.wait_ge(mden, 4 * h + 3)
                v.reciprocal(dn[:, h, 1, :], dn[:, h, 0, :]).then_inc(mden, 1)
                dve.wait_ge(mden, 4 * h + 4)
                for t in range(TT):
                    v.tensor_scalar(hm[:, t, h, :], o[:, t, 0:MDH], dn[:, h, 1, t:t + 1], None, ALU.mult)\
                     .then_inc(mh, 1)
            dve.wait_ge(mh, 2 * MH)
            hsq = sg[:, 0:4, :].rearrange("p a s -> p (a s)")
            hall = hm[:, :, :, :].rearrange("p t h d -> p (t h d)")
            h8 = hm[:, :, :, :].rearrange("p t h d -> p (t h) d")
            v.tensor_tensor(hsq, hall, hall, ALU.mult).then_inc(hnorm, 1)
            dve.wait_ge(hnorm, 1)
            v.tensor_reduce(hs[:, 0, :, :].rearrange("p t h -> p (t h)"), hsq.rearrange("p (a d) -> p a d", a=8),
                            AX, ALU.add).then_inc(hnorm, 1)
            dve.wait_ge(hnorm, 2)
            v.tensor_scalar(hs[:, 1, :, :], hs[:, 0, :, :], 1.0 / MDH, EPS, ALU.mult, ALU.add).then_inc(hnorm, 1)
            for b in range(4):
                dve.wait_ge(qkT_turned, b + 1)
                v.tensor_copy(qkT[:, 2 * b:2 * b + 2, :], B[4 + b][:, :].rearrange("p (a s) -> p a s", a=2))\
                 .then_inc(qkT_ready, 1)
            dve.wait_ge(hroot, 1)
            v.reciprocal(hs[:, 3, :, :], hs[:, 2, :, :]).then_inc(ym, 1)
            dve.wait_ge(ym, 1)
            v.tensor_tensor(h8, h8, hs[:, 3, :, :].rearrange("p t h -> p (t h)").unsqueeze(2).broadcast_to([P, 8, MDH]),
                            ALU.mult).then_inc(ym, 1)
            dve.wait_ge(ym, 2)
            dve.wait_ge(taken["mo"], 2)
            v.tensor_tensor(hall, hall, smo[:, :, :].rearrange("p t n -> p (t n)"), ALU.mult).then_inc(ym, 1)

            mask = cst[:, K_MASK:K_MASK + P]

            def head_max(h):
                dve.wait_ge(scored, h + 1)
                o = B[4 + h % 4]
                for t in range(TT):
                    d = o[:, 2 * P * t:2 * P * t + P]
                    v.tensor_tensor(d, d, mask, ALU.add).then_inc(masked, 1)
                dve.wait_ge(masked, 2 * h + 2)
                for t in range(TT):
                    lo, hi = (0, P) if t == 0 else (P, 3 * P)
                    v.tensor_reduce(am[:, h, 0, t:t + 1], o[:, lo:hi], AX, ALU.max).then_inc(smax, 1)
                dve.wait_ge(smax, 2 * h + 2)
                v.tensor_scalar(am[:, h, 1, :], am[:, h, 0, :], -ADH ** -0.5, None, ALU.mult).then_inc(nsmax, 1)

            def head_norm(h):
                dve.wait_ge(probs, 2 * h + 2)
                v.reciprocal(am[:, h, 3, :], am[:, h, 2, :]).then_inc(psum_r, 1)
                dve.wait_ge(psum_r, h + 1)
                for t in range(TT):
                    lo, hi = (0, P) if t == 0 else (P, 3 * P)
                    v.tensor_scalar(ps[:, h % 4, lo:hi], ps[:, h % 4, lo:hi], am[:, h, 3, t:t + 1], None, ALU.mult)\
                     .then_inc(pnorm, 1)

            def take_pT(h):
                dve.wait_ge(p_turned, h + 1)
                if h >= 4:
                    dve.wait_ge(apv, 2)
                v.tensor_copy(pt[:, h % 4, :], B[4 + h % 4][:, 0:3 * P]).then_inc(pT_ready, 1)

            def take_yaT(j):
                dve.wait_ge(apv, j + 1)
                v.tensor_copy(yaT[:, j, :], B[4 + 2 * (j % 2)][:, 0:S]).then_inc(yaT_ready, 1)

            for g in range(2):
                for h in range(4 * g, 4 * g + 4):
                    head_max(h)
                for h in range(4 * g, 4 * g + 4):
                    head_norm(h)
                for h in range(4 * g, 4 * g + 4):
                    take_pT(h)
                for j in range(2 * g, 2 * g + 2):
                    take_yaT(j)
            for b in range(MH):
                dve.wait_ge(ym_turned, b // 2 + 1)
                v.tensor_scalar(ymT[:, b, :], B[4 + b // 2 * 2 + 1][:, (b % 2) * S:(b % 2 + 1) * S], wcol(HEAD_W + b),
                                None, ALU.mult).then_inc(ymT_ready, 1)
            dve.wait_ge(taken["gm1"], 2)
            for c in range(2 * TT):
                t, n = c // 2, c % 2
                if c < 2 * TT - 1:
                    dve.wait_ge(branched, c + 1)
                else:
                    dve.wait_ge(slots_used, Q_OUT)
                cut = slice(n * N, (n + 1) * N)
                v.tensor_tensor(sga[:, t, cut], B[2 - 2 * (c % 2)][:, :], sga[:, t, cut], ALU.mult).then_inc(gated_br, 1)
                v.tensor_tensor(sgm[:, t, cut], B[2 - 2 * (c % 2) + 1][:, :], sgm[:, t, cut], ALU.mult).then_inc(gated_br, 1)
                dve.wait_ge(gated_br, 2 * c + 2)
                v.tensor_tensor(mg[:, t, cut], sga[:, t, cut], sgm[:, t, cut], ALU.add).then_inc(merged, 1)
            for t in range(TT):
                for n in range(2):
                    c = 2 * t + n
                    cut = slice(n * N, (n + 1) * N)
                    if c < 2 * TT - 1:
                        dve.wait_ge(mixed, c + 1)
                    else:
                        dve.wait_ge(slots_used, Q_MOE)
                    v.tensor_tensor(xs[:, t, cut], B[c][:, :], xs[:, t, cut], ALU.add).then_inc(resid, 1)
                norm(1, t)
                dve.wait_ge(s_wffn, 16)
                v.scalar_tensor_tensor(out=xn[:, t, :], in0=xs[:, t, :], scalar=st[:, 6 + t:7 + t], in1=wffn,
                                       op0=ALU.mult, op1=ALU.mult).then_inc(xn_ready, 1)
                dve.wait_ge(xT_turned, 4 + 2 * t + 1)
                v.tensor_copy(xnT[:, 0:4, t * P:(t + 1) * P], B[4 + 2 * t][:, :].rearrange("p (k s) -> p k s", k=4))\
                 .then_inc(xT_even, 1)
            for c in range(2 * TT):
                v.memset(B[c][:, :], 0.0).then_inc(opened, 1)
            dve.wait_ge(ymT_ready, MH)
            v.memset(gated, 0.0).then_inc(gated_zero, 1)
            dve.wait_ge(s_small2, 16 * 2)
            dve.wait_ge(logits_done, 1)
            v.tensor_copy(lgT, B[4][:, 0:S]).then_inc(lgT_ready, 1)
            dve.wait_ge(logits_done, 2)
            v.tensor_reduce(lg[:, :, 5, :], B[5][:, 0:TT * P].rearrange("p (t j e) -> p t e j", t=TT, j=4), AX, ALU.add)\
             .then_inc(logit_sum, 1)
            dve.wait_ge(logit_sum, 1)
            v.tensor_tensor(lg[:, :, 0, :], lg[:, :, 5, :], brt[:, :].unsqueeze(1).broadcast_to([P, TT, E]), ALU.add)\
             .then_inc(router_step, 1)
            dve.wait_ge(router_step, 1)
            for t in range(TT):
                v.max(out=mx8[:, t, 0:8], in_=lg[:, t, 0, :]).then_inc(router_step, 1)
            dve.wait_ge(router_step, 3)
            v.memset(mx8[:, :, TOPK:8], 3.0e38).then_inc(router_step, 1)
            v.tensor_scalar(mx8[:, :, 8:9], mx8[:, :, 0:1], -1.0, None, ALU.mult).then_inc(neg_top, 1)
            dve.wait_ge(router_step, 4)
            for t in range(TT):
                v.match_replace(out=lg[:, t, 3, :], in_to_replace=mx8[:, t, 0:8], in_values=lg[:, t, 0, :],
                                imm_value=-3.0e38).then_inc(router_step, 1)
            dve.wait_ge(router_step, 6)
            v.tensor_tensor(lg[:, :, 1, :], lg[:, :, 0, :], lg[:, :, 3, :], ALU.not_equal).then_inc(chosen, 1)
            dve.wait_ge(counted, 1)
            v.tensor_scalar(cnt[:, 0, :], B[4][0:1, 0:E], C + 0.5, 1.0, ALU.is_gt, ALU.add).then_inc(count_step, 1)
            v.tensor_scalar(cnt[:, 1, :], B[4][0:1, 0:E], 2 * C + 0.5, None, ALU.is_gt).then_inc(count_step, 1)
            v.tensor_scalar(cnt[:, 2, :], B[4][0:1, 0:E], 3 * C + 0.5, None, ALU.is_gt).then_inc(count_step, 1)
            dve.wait_ge(count_step, 3)
            v.tensor_tensor(cnt[:, 0, :], cnt[:, 0, :], cnt[:, 1, :], ALU.add).then_inc(count_step, 1)
            dve.wait_ge(count_step, 4)
            v.tensor_tensor(cnt[:, 0, :], cnt[:, 0, :], cnt[:, 2, :], ALU.add).then_inc(count_step, 1)
            dve.wait_ge(count_step, 5)
            v.tensor_tensor_scan(cnt[:, 3, :], cnt[:, 0, :], cnt[:, 0, :], 0.0, ALU.add, ALU.bypass).then_inc(count_step, 1)
            v.memset(first_item[:, 0:1], 0).then_inc(count_step, 1)
            dve.wait_ge(count_step, 7)
            v.tensor_copy(first_item[:, 1:E + 1], cnt[:, 3, :]).then_inc(firsts, 1)
            v.tensor_scalar(first_item[:, E + 1:E + 2], cnt[:, 3, E - 1:E], 1.0, None, ALU.add).then_inc(firsts, 1)
            dve.wait_ge(ranked, 1)
            for t in range(TT):
                v.scalar_tensor_tensor(out=pos[:, t, 0:E], in0=B[6][:, t * E:(t + 1) * E], scalar=1.0,
                                       in1=lg[:, t, 1, :], op0=ALU.add, op1=ALU.mult).then_inc(pos_step, 1)
            dve.wait_ge(pos_step, 2)
            v.tensor_scalar(pos[:, :, 0:E], pos[:, :, 0:E], -1.0, None, ALU.add).then_inc(pos_ready, 1)
            v.memset(pos[:, :, E:E + 1], -1.0).then_inc(pos_ready, 1)
            v.memset(gate[:, :, E:E + 1], 0.0).then_inc(pos_ready, 1)
            def place(e, i):
                after = dve.value_load(first_item[0:1, bass.ds(e + 1, 1)], min_val=1, max_val=ITEMS)
                r = nc.s_assert_within(after - 1 - i, 0, NR - 1, skip_runtime_bounds_check_because=
                                       "an expert has 1 to NR tiles, by the sum that made the table")
                return cst[:, bass.ds(r * C + K_IOTA, C)], [pos[:, t, bass.ds(e, 1)] for t in range(TT)]

            def one_hots(e, i):
                places, at = place(e, i)
                for t in range(TT):
                    v.tensor_scalar(oneh[:, t, :], places, at[t], None, ALU.is_equal).then_inc(onehot, 1)

            def take_xgT(ready):
                dve.wait_ge(xg_turned, ready)
                v.tensor_copy(xgT, B[6][:, :].rearrange("p (j g s) -> p j g s", j=4, g=2)).then_inc(xg_ready, 1)

            dve.wait_ge(pos_ready, 3)
            dve.wait_ge(firsts, 2)
            one_hots(0, 0)
            dve.wait_ge(chosen, 1)
            dve.wait_ge(rexp, 2)
            v.tensor_tensor(lg[:, :, 4, :], lg[:, :, 2, :], lg[:, :, 1, :], ALU.mult).then_inc(router, 1)
            dve.wait_ge(router, 1)
            v.tensor_reduce(mx8[:, :, 9:10].rearrange("p t a -> p (t a)"), lg[:, :, 4, :], AX, ALU.add).then_inc(router, 1)
            dve.wait_ge(router, 2)
            v.reciprocal(mx8[:, :, 10:11], mx8[:, :, 9:10]).then_inc(router, 1)
            dve.wait_ge(router, 3)
            v.tensor_tensor(gate[:, :, 0:E], lg[:, :, 4, :], mx8[:, :, 10:11].broadcast_to([P, TT, E]), ALU.mult)\
             .then_inc(gates_ready, 1)
            dve.wait_ge(gates_ready, 1)
            dve.wait_ge(gated_zero, 1)
            for g in range(2):
                v.tensor_copy(gated[:, :, g * C:g * C + E], gate[:, :, 0:E]).then_inc(gated_ready, 1)
            spread = mg[0:1, :, :].rearrange("p t n -> p (t n)")[:, 0:ITEMS * E].rearrange("p (i e) -> p i e", e=E)
            dve.wait_ge(mg_turned, 2 * TT)
            v.tensor_tensor(spread, cnt[:, 3, :].unsqueeze(1).broadcast_to([1, ITEMS, E]),
                            cst[0:1, K_IOTA:K_IOTA + ITEMS].unsqueeze(2).broadcast_to([1, ITEMS, E]), ALU.is_le)\
             .then_inc(count_step, 1)
            dve.wait_ge(count_step, 8)
            v.tensor_reduce(item_sum[:, 0:ITEMS], spread, AX, ALU.add).then_inc(count_step, 1)
            dve.wait_ge(count_step, 9)
            v.tensor_copy(item_expert[:, 0:ITEMS], item_sum[:, 0:ITEMS]).then_inc(tabled, 1)
            take_xgT(1)
            dve.wait_ge(gt_turned, 1)
            v.tensor_copy(gatedT, B[5][:, 0:S]).then_inc(gT_ready, 1)
            dve.wait_ge(tabled, 1)
            items = dve.value_load(first_item[0:1, E:E + 1], min_val=1, max_val=ITEMS - 1)
            with dve.Fori(0, items) as i:
                e = dve.value_load(item_expert[0:1, bass.ds(i, 1)], min_val=0, max_val=E)
                places, at = place(e, i)
                dve.wait_ge(gt_turned, i + 1)
                for t in range(TT):
                    v.tensor_scalar(gated[:, t, :].rearrange("p (g s) -> p g s", g=2),
                                    places.unsqueeze(1).broadcast_to([P, 2, C]), at[t],
                                    gate[:, t, bass.ds(e, 1)], ALU.is_equal, ALU.mult).then_inc(gated_ready, 1)
                dve.wait_ge(gath, i + 1)
                one_hots(dve.value_load(item_expert[0:1, bass.ds(i + 1, 1)], min_val=0, max_val=E), i + 1)
                dve.wait_ge(slots_used, i * PER_EXPERT + (Q_MOE + KB))
                v.tensor_scalar(glu, B[4][:, :], LIMIT, None, ALU.min).then_inc(glu_ready, 1)
                v.tensor_scalar(lin, B[5][:, :], LIMIT, -LIMIT, ALU.min, ALU.max).then_inc(lin_ready, 1)
                dve.wait_ge(glu_ready, i + 1)
                dve.wait_ge(lin_ready, i + 1)
                v.scalar_tensor_tensor(out=lin, in0=lin, scalar=1.0, in1=glu, op0=ALU.add, op1=ALU.mult)\
                 .then_inc(glin, 1)
                dve.wait_ge(glin, i + 1)
                dve.wait_ge(sig_ready, i + 1)
                v.tensor_tensor(actv, lin, sig, ALU.mult).then_inc(act_ready, 1)
                dve.wait_ge(turned_a, i + 1)
                v.tensor_copy(actT[:, 0:2, :], B[7][:, 0:2 * P].rearrange("p (j c) -> p j c", j=2)).then_inc(actT_a, 1)
                take_xgT(i + 2)
                dve.wait_ge(gt_turned, i + 2)
                v.tensor_copy(gatedT, B[5][:, 0:S]).then_inc(gT_ready, 1)
            dve.wait_ge(scat, items + 1)
            for t in range(TT):
                for n in range(2):
                    cut = slice(n * N, (n + 1) * N)
                    v.tensor_tensor(xs[:, t, cut], B[2 * t + n][:, :], xs[:, t, cut], ALU.add).then_inc(resid, 1)
            dve.wait_ge(s_small2, 16 * 3)
            for t in range(TT):
                norm(2, t)
                v.scalar_tensor_tensor(out=xn[:, t, :], in0=xs[:, t, :], scalar=st[:, 6 + t:7 + t], in1=wfin,
                                       op0=ALU.mult, op1=ALU.mult).then_inc(normed, 1)


_INS = ["x", "norm_mix_w", "w_in", "m_conv_w", "m_conv_b", "m_gate_bias", "m_head_norm_w", "w_branch", "w_out",
        "norm_ffn_w", "w_router", "b_router", "w_mlp1", "b_mlp1", "w_mlp2", "b_mlp2", "norm_final_w"]


def kernel(**inputs):
    import concourse.bacc as _bacc
    from concourse.bass_utils import run_bass_kernel_spmd as _run

    nc = _bacc.Bacc("TRN2", target_bir_lowering=False, num_devices=1)
    arrays, args = {}, []
    for name in _INS:
        a = np.ascontiguousarray(inputs[name])
        arrays[f"in_{name}_dram"] = a
        args.append(nc.dram_tensor(f"in_{name}_dram", a.shape, mybir.dt.from_np(a.dtype), kind="ExternalInput").ap())
    table = constants()
    arrays["table_dram"] = table
    args.append(nc.dram_tensor("table_dram", table.shape, F32, kind="ExternalInput").ap())
    args.append(nc.dram_tensor("out_dram", (1, S, D), F32, kind="ExternalOutput").ap())
    build(nc, *args)
    r = _run(nc, [arrays], core_ids=[0])
    return r.results[0]["out_dram"]
```
